# Optimizing a Trainium2 kernel written in Bass

```python
import jax, jax.numpy as jnp
from jax import lax
import numpy as np

D_MODEL = 1024
BATCH = 1
SEQ = 256
DEPTH = 1

GRID_W = 64
CTX_LEN = 256
HG_DIM = 128
HG_WIDTH = D_MODEL // 2
HG_HEADS = HG_WIDTH // HG_DIM
MLP_WIDTH = D_MODEL - HG_WIDTH
MLP_HEADS = 4
MLP_DIM = MLP_WIDTH // MLP_HEADS
MLP_CHUNK = 128
SCAN_CHUNK = 32
MIX_WIDTH = HG_WIDTH + MLP_WIDTH
PROJ_WIDTH = 5 * HG_WIDTH + 2 * MLP_WIDTH
D_FF = 2816
CONV_W = 3
EPS = 1e-6


def rmsnorm(x, gain):
    xf = x.astype(jnp.float32)
    y = xf * lax.rsqrt(jnp.mean(xf * xf, axis=-1, keepdims=True) + EPS)
    return (y * gain.astype(jnp.float32)).astype(x.dtype)

def layernorm(x, gain, bias):
    xf = x.astype(jnp.float32)
    mu = jnp.mean(xf, axis=-1, keepdims=True)
    var = jnp.mean(jnp.square(xf - mu), axis=-1, keepdims=True)
    y = (xf - mu) * lax.rsqrt(var + EPS) * gain.astype(jnp.float32) + bias.astype(jnp.float32)
    return y.astype(x.dtype)

def modulate(h, shift, scale):
    return h * (1.0 + scale) + shift

def split_heads(a, n_heads):
    b, t, w = a.shape
    return a.reshape(b, t, n_heads, w // n_heads).transpose(0, 2, 1, 3)

def merge_heads(a):
    b, h, t, d = a.shape
    return a.transpose(0, 2, 1, 3).reshape(b, t, h * d)

def flip_t(a):
    return jnp.flip(a, axis=2)

def lower_bounds(logits):
    cum = jnp.cumsum(jax.nn.softmax(logits.astype(jnp.float32), axis=0), axis=0)
    return cum - cum[0:1]

def forget_gate(f_logit, lb, first):
    f = f_logit.astype(jnp.float32)
    if first:
        return jax.nn.log_sigmoid(f), jax.nn.sigmoid(-f)
    gate = lb + (1.0 - lb) * jax.nn.sigmoid(f)
    return jnp.log(gate), 1.0 - gate

def hgrn2_gates(p, lb_f, lb_b, first):
    w = HG_WIDTH
    logf_f, k_f = forget_gate(p[..., :w], lb_f, first)
    logf_b, k_b = forget_gate(p[..., w:2 * w], lb_b, first)
    v = p[..., 2 * w:3 * w].astype(jnp.float32)
    return tuple(split_heads(a, HG_HEADS) for a in (logf_f, k_f, logf_b, k_b, v))

def advance_state(h, k, v, b):
    b_last = b[:, :, -1:, :]
    return (jnp.exp(b_last)[:, :, 0, :, None] * h
            + jnp.einsum('bhsk,bhsv->bhkv', k * jnp.exp(b_last - b), v))

def chunk_gla(q, k, v, log_f, h0):
    b_, h_, t, _ = q.shape
    n = t // SCAN_CHUNK

    def to_chunks(a):
        return jnp.moveaxis(a.reshape(b_, h_, n, SCAN_CHUNK, a.shape[-1]), 2, 0)

    mask = jnp.tril(jnp.ones((SCAN_CHUNK, SCAN_CHUNK), dtype=bool))[:, :, None]

    def step(h, blk):
        qc, kc, vc, gc = blk
        b = jnp.cumsum(gc, axis=2)
        o_inter = jnp.einsum('bhtk,bhkv->bhtv', qc * jnp.exp(b), h)
        diff = b[:, :, :, None, :] - b[:, :, None, :, :]
        decay = jnp.where(mask, jnp.exp(jnp.where(mask, diff, 0.0)), 0.0)
        scores = jnp.einsum('bhtk,bhsk,bhtsk->bhts', qc, kc, decay)
        o = o_inter + jnp.einsum('bhts,bhsv->bhtv', scores, vc)
        return advance_state(h, kc, vc, b), o

    h_end, o = lax.scan(step, h0, (to_chunks(q), to_chunks(k), to_chunks(v), to_chunks(log_f)))
    o = jnp.moveaxis(o, 0, 2).reshape(b_, h_, t, v.shape[-1])
    return o, h_end

def chunk_sgu(u, v, ln_g, ln_b, w_s, b_s):
    bsz, t, _ = u.shape
    n = t // MLP_CHUNK
    u = jax.nn.gelu(u, approximate=False).reshape(bsz, n, MLP_CHUNK, MLP_HEADS, MLP_DIM)
    v = jax.nn.gelu(v, approximate=False).reshape(bsz, n, MLP_CHUNK, MLP_HEADS, MLP_DIM)
    v = layernorm(v, ln_g.reshape(MLP_HEADS, MLP_DIM), ln_b.reshape(MLP_HEADS, MLP_DIM))
    z = jnp.einsum('hpq,bnqhc->bnphc', w_s.astype(v.dtype), v) + jnp.transpose(b_s)[None, None, :, :, None]
    return (u * z).reshape(bsz, t, MLP_WIDTH)

def token_mixers(p, lb_f, lb_b, first, h0_f, h0_b, hg_gain, sgu_g, sgu_b, w_s, b_s):
    w = HG_WIDTH
    logf_f, k_f, logf_b, k_b, v = hgrn2_gates(p, lb_f, lb_b, first)
    q = split_heads(jax.nn.silu(p[..., 3 * w:4 * w].astype(jnp.float32)), HG_HEADS) * (HG_DIM ** -0.5)
    o_f, h_f = chunk_gla(q, k_f, v, logf_f, h0_f)
    o_b, h_b = chunk_gla(flip_t(q), flip_t(k_b), flip_t(v), flip_t(logf_b), h0_b)
    o = rmsnorm(o_f + flip_t(o_b), hg_gain.reshape(HG_HEADS, 1, HG_DIM))
    o_hg = merge_heads(o).astype(p.dtype) * jax.nn.silu(p[..., 4 * w:5 * w])
    o_mlp = chunk_sgu(p[..., 5 * w:5 * w + MLP_WIDTH], p[..., 5 * w + MLP_WIDTH:], sgu_g, sgu_b, w_s, b_s)
    return jnp.concatenate([o_hg, o_mlp], axis=-1), h_f, h_b

def conv_ffn(h, w_up, taps, conv_b, w_down, rows):
    a, g = jnp.split(h @ w_up, 2, axis=-1)
    bsz, t, f = g.shape
    if rows is None:
        g2, tp = g.reshape(bsz, 1, t, f), taps[1:2]
    else:
        g2, tp = g.reshape(bsz, rows, GRID_W, f), taps
    gc = lax.conv_general_dilated(g2, tp[:, :, None, :].astype(g.dtype), (1, 1), 'SAME',
                                  dimension_numbers=('NHWC', 'HWIO', 'NHWC'), feature_group_count=f)
    gc = gc.reshape(bsz, t, f) + conv_b
    return (a * jax.nn.gelu(gc, approximate=False)) @ w_down

def first_inputs(seed: int = 0) -> dict:
    key = jax.random.key(seed)
    ks = jax.random.split(key, 22)
    nrm = jax.random.normal
    L, D, F = DEPTH, D_MODEL, D_FF
    return {
        "x": nrm(ks[0], (BATCH, SEQ, D), jnp.float32),
        "c": nrm(ks[1], (BATCH, D), jnp.float32),
        "ctx": nrm(ks[2], (BATCH, CTX_LEN, D), jnp.float32),
        "c_ctx": nrm(ks[3], (D,), jnp.float32),
        "w_ada": nrm(ks[4], (L, D, 6 * D), jnp.float32) * (0.5 * D ** -0.5),
        "b_ada": nrm(ks[5], (L, 6 * D), jnp.float32) * 0.02,
        "norm_mix": 1.0 + 0.1 * nrm(ks[6], (L, D), jnp.float32),
        "norm_ffn": 1.0 + 0.1 * nrm(ks[7], (L, D), jnp.float32),
        "w_in": nrm(ks[8], (L, D, PROJ_WIDTH), jnp.float32) * D ** -0.5,
        "lb_logits_fwd": nrm(ks[9], (L, HG_WIDTH), jnp.float32),
        "lb_logits_bwd": nrm(ks[10], (L, HG_WIDTH), jnp.float32),
        "hg_norm": 1.0 + 0.1 * nrm(ks[11], (L, HG_WIDTH), jnp.float32),
        "sgu_norm_g": 1.0 + 0.1 * nrm(ks[12], (L, MLP_WIDTH), jnp.float32),
        "sgu_norm_b": 0.02 * nrm(ks[13], (L, MLP_WIDTH), jnp.float32),
        "w_spatial": nrm(ks[14], (L, MLP_HEADS, MLP_CHUNK, MLP_CHUNK), jnp.float32) * MLP_CHUNK ** -0.5,
        "b_spatial": 1.0 + 0.1 * nrm(ks[15], (L, MLP_HEADS, MLP_CHUNK), jnp.float32),
        "w_out": nrm(ks[16], (L, MIX_WIDTH, D), jnp.float32) * MIX_WIDTH ** -0.5,
        "w_up": nrm(ks[17], (L, D, 2 * F), jnp.float32) * D ** -0.5,
        "conv_w": nrm(ks[18], (L, CONV_W, CONV_W, F), jnp.float32) / CONV_W,
        "conv_b": 0.02 * nrm(ks[19], (L, F), jnp.float32),
        "w_down": nrm(ks[20], (L, F, D), jnp.float32) * F ** -0.5,
        "norm_final": 1.0 + 0.1 * nrm(ks[21], (D,), jnp.float32),
    }

def first_block(x, c, ctx, c_ctx, w_ada, b_ada, norm_mix, norm_ffn, w_in, lb_logits_fwd, lb_logits_bwd,
              hg_norm, sgu_norm_g, sgu_norm_b, w_spatial, b_spatial, w_out, w_up, conv_w, conv_b, w_down,
              norm_final):
    w = HG_WIDTH
    rows = x.shape[1] // GRID_W
    bsz = x.shape[0]
    lb_f_all = lower_bounds(lb_logits_fwd)
    lb_b_all = lower_bounds(lb_logits_bwd)
    ada = jnp.einsum('bd,lde->lbe', jax.nn.silu(c), w_ada) + b_ada[:, None, :]
    ada_c = jnp.einsum('d,lde->le', jax.nn.silu(c_ctx), w_ada) + b_ada
    h0 = jnp.zeros((bsz, HG_HEADS, HG_DIM, HG_DIM), jnp.float32)
    xc = ctx
    for l in range(DEPTH):
        first, last = l == 0, l == DEPTH - 1
        sh1, sc1, g1, sh2, sc2, g2 = (m[:, None, :] for m in jnp.split(ada[l], 6, axis=-1))
        csh1, csc1, cg1, csh2, csc2, cg2 = jnp.split(ada_c[l], 6, axis=-1)
        lb_f, lb_b = lb_f_all[l], lb_b_all[l]
        mix_args = (hg_norm[l], sgu_norm_g[l], sgu_norm_b[l], w_spatial[l], b_spatial[l])

        hc = modulate(rmsnorm(xc, norm_mix[l]), csh1, csc1)
        if last:
            logf_f, k_f, logf_b, k_b, vc = hgrn2_gates(hc @ w_in[l][:, :3 * w], lb_f, lb_b, first)
            hf_c = advance_state(h0, k_f, vc, jnp.cumsum(logf_f, axis=2))
            hb_c = advance_state(h0, flip_t(k_b), flip_t(vc), jnp.cumsum(flip_t(logf_b), axis=2))
        else:
            oc, hf_c, hb_c = token_mixers(hc @ w_in[l], lb_f, lb_b, first, h0, h0, *mix_args)

        h = modulate(rmsnorm(x, norm_mix[l]), sh1, sc1)
        o, _, _ = token_mixers(h @ w_in[l], lb_f, lb_b, first, hf_c, hb_c, *mix_args)
        x = x + g1 * (o @ w_out[l])
        h2 = modulate(rmsnorm(x, norm_ffn[l]), sh2, sc2)
        x = x + g2 * conv_ffn(h2, w_up[l], conv_w[l], conv_b[l], w_down[l], rows)

        if not last:
            xc = xc + cg1 * (oc @ w_out[l])
            hc2 = modulate(rmsnorm(xc, norm_ffn[l]), csh2, csc2)
            xc = xc + cg2 * conv_ffn(hc2, w_up[l], conv_w[l], conv_b[l], w_down[l], None)
    return rmsnorm(x, norm_final)


PLE_DIM = 256
BRANCH_WIDTH = D_MODEL // 2
N_BRANCH = 3
FOX_HEAD_DIM = 64
FOX_HEADS = BRANCH_WIDTH // FOX_HEAD_DIM
FOX_WIDTH = FOX_HEADS * FOX_HEAD_DIM
FOX_BLOCK = 128
SC_WIDTH = BRANCH_WIDTH
SC_KERNEL = 3
DN_HEAD_DIM = 128
DN_HEADS = BRANCH_WIDTH // DN_HEAD_DIM
DN_WIDTH = DN_HEADS * DN_HEAD_DIM
DN_CONV = 4
DN_CHUNK = 64
D_FF_2 = 128 * ((8 * D_MODEL // 3 + 127) // 128)
FFN_CONV = 3

IN_SIZES = (3 * FOX_WIDTH, FOX_HEADS, 3 * SC_WIDTH, 3 * DN_WIDTH, DN_HEADS, DN_HEADS, DN_WIDTH, N_BRANCH * D_MODEL)
IN_WIDTH = sum(IN_SIZES)


def split_cols(t, sizes):
    offs = []
    acc = 0
    for s in sizes[:-1]:
        acc += s
        offs.append(acc)
    return jnp.split(t, offs, axis=-1)

def rmsnorm_2(x, gain):
    xf = x.astype(jnp.float32)
    y = xf * lax.rsqrt(jnp.mean(xf * xf, axis=-1, keepdims=True) + EPS)
    return (y * gain.astype(jnp.float32)).astype(x.dtype)

def l2norm(x):
    xf = x.astype(jnp.float32)
    return xf * lax.rsqrt(jnp.sum(xf * xf, axis=-1, keepdims=True) + EPS)

def causal_dwconv(x, w):
    k_width, chans = w.shape
    return lax.conv_general_dilated(x, w[:, None, :].astype(x.dtype), window_strides=(1,),
                                    padding=[(k_width - 1, 0)],
                                    dimension_numbers=('NWC', 'WIO', 'NWC'),
                                    feature_group_count=chans)

def forgetting_attention(q, k, v, f_logit, b_f, q_gain, k_gain):
    seq = q.shape[1]
    dh = q.shape[-1]
    q = rmsnorm_2(q, q_gain).transpose(0, 2, 1, 3)
    k = rmsnorm_2(k, k_gain).transpose(0, 2, 1, 3)
    v = v.transpose(0, 2, 1, 3)
    log_f = jax.nn.log_sigmoid(f_logit.astype(jnp.float32) + b_f.astype(jnp.float32))
    cum_f = jnp.cumsum(log_f, axis=1).transpose(0, 2, 1)
    scale = dh ** -0.5
    outs = []
    for start in range(0, seq, FOX_BLOCK):
        end = start + FOX_BLOCK
        s = jnp.einsum('bhqd,bhkd->bhqk', q[:, :, start:end], k[:, :, :end],
                       preferred_element_type=jnp.float32) * scale
        s = s + cum_f[:, :, start:end, None] - cum_f[:, :, None, :end]
        causal = jnp.arange(start, end)[:, None] >= jnp.arange(end)[None, :]
        s = jnp.where(causal, s, -jnp.inf)
        pr = jax.nn.softmax(s, axis=-1).astype(v.dtype)
        outs.append(jnp.einsum('bhqk,bhkd->bqhd', pr, v[:, :, :end]))
    return jnp.concatenate(outs, axis=1)

def gated_delta_rule(q, k, v, g, beta):
    bsz, seq, heads, dk = q.shape
    dv = v.shape[-1]
    c = DN_CHUNK
    n_chunks = seq // c

    def to_chunks(t):
        return t.astype(jnp.float32).reshape(bsz, n_chunks, c, heads, -1).transpose(1, 0, 3, 2, 4)

    qc = to_chunks(q) * dk ** -0.5
    kc = to_chunks(k)
    vc = to_chunks(v)
    gc = to_chunks(g[..., None])[..., 0]
    bc = to_chunks(beta[..., None])[..., 0]
    gcum = jnp.cumsum(gc, axis=-1)
    incl = jnp.tril(jnp.ones((c, c), dtype=bool))
    strict = jnp.tril(jnp.ones((c, c), dtype=bool), k=-1)
    decay = jnp.exp(jnp.where(incl, gcum[..., :, None] - gcum[..., None, :], -jnp.inf))
    kb = kc * bc[..., None]
    a_mat = jnp.where(strict, jnp.einsum('nbhid,nbhjd->nbhij', kb, kc) * decay, 0.0) \
        + jnp.eye(c, dtype=jnp.float32)
    rhs = jnp.concatenate([vc * bc[..., None], kb * jnp.exp(gcum)[..., None]], axis=-1)
    sol = lax.linalg.triangular_solve(a_mat, rhs, left_side=True, lower=True, unit_diagonal=True)
    u_val, k_cum = sol[..., :dv], sol[..., dv:]
    qk = jnp.where(incl, jnp.einsum('nbhid,nbhjd->nbhij', qc, kc) * decay, 0.0)
    q_dec = qc * jnp.exp(gcum)[..., None]
    k_dec = kc * jnp.exp(gcum[..., -1:] - gcum)[..., None]
    g_tot = jnp.exp(gcum[..., -1])

    def step(state, xs):
        u_i, kcum_i, qk_i, qdec_i, kdec_i, gtot_i = xs
        v_new = u_i - jnp.einsum('bhck,bhkv->bhcv', kcum_i, state)
        out = jnp.einsum('bhck,bhkv->bhcv', qdec_i, state) + jnp.einsum('bhij,bhjv->bhiv', qk_i, v_new)
        state = state * gtot_i[..., None, None] + jnp.einsum('bhck,bhcv->bhkv', kdec_i, v_new)
        return state, out

    state0 = jnp.zeros((bsz, heads, dk, dv), jnp.float32)
    _, out = lax.scan(step, state0, (u_val, k_cum, qk, q_dec, k_dec, g_tot))
    return out.transpose(1, 0, 3, 2, 4).reshape(bsz, seq, heads, dv)

def hybrid_layer(x, p_i, g_mix, w_in, b_fox_f, fox_q_gain, fox_k_gain, sc_conv_w, dn_conv_w,
                 dn_a_log, dn_dt_bias, dn_norm_gain, w_branch, w_o, g_ffn, w_up, ffn_conv_w,
                 w_down, g_ple, w_ple_gate, w_ple):
    bsz, seq, _ = x.shape
    h = rmsnorm_2(x, g_mix)
    proj = h @ w_in
    fox_qkv, fox_f, sc_bcv, dn_qkv, dn_b, dn_a, dn_z, br_gate = split_cols(proj, IN_SIZES)

    fq, fk, fv = [t.reshape(bsz, seq, FOX_HEADS, FOX_HEAD_DIM) for t in jnp.split(fox_qkv, 3, axis=-1)]
    y_fox = forgetting_attention(fq, fk, fv, fox_f, b_fox_f, fox_q_gain, fox_k_gain)
    y_fox = y_fox.reshape(bsz, seq, FOX_WIDTH)

    sb, sc, sv = jnp.split(sc_bcv, 3, axis=-1)
    y_sc = sb * causal_dwconv(sc * sv, sc_conv_w)

    dn_qkv = jax.nn.silu(causal_dwconv(dn_qkv, dn_conv_w))
    dq, dk_, dv_ = [t.reshape(bsz, seq, DN_HEADS, DN_HEAD_DIM) for t in jnp.split(dn_qkv, 3, axis=-1)]
    beta = jax.nn.sigmoid(dn_b.astype(jnp.float32))
    g = -jnp.exp(dn_a_log.astype(jnp.float32)) * jax.nn.softplus(dn_a.astype(jnp.float32) + dn_dt_bias.astype(jnp.float32))
    o_dn = gated_delta_rule(l2norm(dq), l2norm(dk_), dv_, g, beta).astype(x.dtype)
    z = dn_z.reshape(bsz, seq, DN_HEADS, DN_HEAD_DIM)
    y_dn = (rmsnorm_2(o_dn, dn_norm_gain) * jax.nn.silu(z)).reshape(bsz, seq, DN_WIDTH)

    ys = jnp.stack([y_fox, y_sc, y_dn], axis=2)
    gates = jax.nn.sigmoid(br_gate).reshape(bsz, seq, N_BRANCH, D_MODEL)
    merged = jnp.sum(jnp.einsum('bsnc,ncd->bsnd', ys, w_branch) * gates, axis=2)
    x = x + merged @ w_o

    u = causal_dwconv(rmsnorm_2(x, g_ffn) @ w_up, ffn_conv_w)
    u_gate, u_val = jnp.split(u, 2, axis=-1)
    x = x + (jax.nn.silu(u_gate) * u_val) @ w_down

    x = x + jax.nn.sigmoid(rmsnorm_2(x, g_ple) @ w_ple_gate) * (p_i.astype(x.dtype) @ w_ple)
    return x

def second_inputs(seed: int = 0) -> dict:
    key = jax.random.key(seed)
    ks = jax.random.split(key, 24)
    f32 = jnp.float32

    def nrm(k, shape, scale):
        return jax.random.normal(k, shape, f32) * scale

    def gain(k, shape):
        return 1.0 + 0.02 * jax.random.normal(k, shape, f32)

    x = nrm(ks[0], (BATCH, SEQ, D_MODEL), 1.0)
    p = nrm(ks[1], (DEPTH, BATCH, SEQ, PLE_DIM), 1.0)
    g_mix = gain(ks[2], (DEPTH, D_MODEL))
    w_in = nrm(ks[3], (DEPTH, D_MODEL, IN_WIDTH), D_MODEL ** -0.5)
    b_fox_f = jnp.linspace(1.0, 5.0, FOX_HEADS, dtype=f32)[None, :] + nrm(ks[4], (DEPTH, FOX_HEADS), 0.1)
    fox_q_gain = gain(ks[5], (DEPTH, FOX_HEAD_DIM))
    fox_k_gain = gain(ks[6], (DEPTH, FOX_HEAD_DIM))
    sc_conv_w = nrm(ks[7], (DEPTH, SC_KERNEL, SC_WIDTH), SC_KERNEL ** -0.5)
    dn_conv_w = nrm(ks[8], (DEPTH, DN_CONV, 3 * DN_WIDTH), DN_CONV ** -0.5)
    dn_a_log = jnp.log(jax.random.uniform(ks[9], (DEPTH, DN_HEADS), f32, 1.0, 16.0))
    dt = jnp.exp(jax.random.uniform(ks[10], (DEPTH, DN_HEADS), f32, float(np.log(1e-3)), float(np.log(1e-1))))
    dn_dt_bias = dt + jnp.log(-jnp.expm1(-dt))
    dn_norm_gain = gain(ks[11], (DEPTH, DN_HEAD_DIM))
    w_branch = nrm(ks[12], (DEPTH, N_BRANCH, BRANCH_WIDTH, D_MODEL), BRANCH_WIDTH ** -0.5)
    w_o = nrm(ks[13], (DEPTH, D_MODEL, D_MODEL), D_MODEL ** -0.5)
    g_ffn = gain(ks[14], (DEPTH, D_MODEL))
    w_up = nrm(ks[15], (DEPTH, D_MODEL, 2 * D_FF_2), D_MODEL ** -0.5)
    ffn_conv_w = nrm(ks[16], (DEPTH, FFN_CONV, 2 * D_FF_2), FFN_CONV ** -0.5)
    w_down = nrm(ks[17], (DEPTH, D_FF_2, D_MODEL), D_FF_2 ** -0.5)
    g_ple = gain(ks[18], (DEPTH, D_MODEL))
    w_ple_gate = nrm(ks[19], (DEPTH, D_MODEL, D_MODEL), D_MODEL ** -0.5)
    w_ple = nrm(ks[20], (DEPTH, PLE_DIM, D_MODEL), PLE_DIM ** -0.5)
    return {'x': x, 'p': p, 'g_mix': g_mix, 'w_in': w_in, 'b_fox_f': b_fox_f,
            'fox_q_gain': fox_q_gain, 'fox_k_gain': fox_k_gain, 'sc_conv_w': sc_conv_w,
            'dn_conv_w': dn_conv_w, 'dn_a_log': dn_a_log, 'dn_dt_bias': dn_dt_bias,
            'dn_norm_gain': dn_norm_gain, 'w_branch': w_branch, 'w_o': w_o, 'g_ffn': g_ffn,
            'w_up': w_up, 'ffn_conv_w': ffn_conv_w, 'w_down': w_down, 'g_ple': g_ple,
            'w_ple_gate': w_ple_gate, 'w_ple': w_ple}

def second_block(x, p, g_mix, w_in, b_fox_f, fox_q_gain, fox_k_gain, sc_conv_w, dn_conv_w,
              dn_a_log, dn_dt_bias, dn_norm_gain, w_branch, w_o, g_ffn, w_up, ffn_conv_w,
              w_down, g_ple, w_ple_gate, w_ple):
    for i in range(DEPTH):
        x = hybrid_layer(x, p[i], g_mix[i], w_in[i], b_fox_f[i], fox_q_gain[i], fox_k_gain[i],
                         sc_conv_w[i], dn_conv_w[i], dn_a_log[i], dn_dt_bias[i], dn_norm_gain[i],
                         w_branch[i], w_o[i], g_ffn[i], w_up[i], ffn_conv_w[i], w_down[i],
                         g_ple[i], w_ple_gate[i], w_ple[i])
    return x


def setup_inputs(seed=0):
    out = dict(first_inputs(seed))
    for name, value in second_inputs(seed + 1).items():
        if name != "x":
            out[name + "_2"] = value
    return out


def reference(
    x, c, ctx, c_ctx, w_ada, b_ada, norm_mix, norm_ffn, w_in, lb_logits_fwd, lb_logits_bwd,
    hg_norm, sgu_norm_g, sgu_norm_b, w_spatial, b_spatial, w_out, w_up, conv_w, conv_b, w_down,
    norm_final, p_2, g_mix_2, w_in_2, b_fox_f_2, fox_q_gain_2, fox_k_gain_2, sc_conv_w_2,
    dn_conv_w_2, dn_a_log_2, dn_dt_bias_2, dn_norm_gain_2, w_branch_2, w_o_2, g_ffn_2, w_up_2,
    ffn_conv_w_2, w_down_2, g_ple_2, w_ple_gate_2, w_ple_2,
):
    x = first_block(
        x, c, ctx, c_ctx, w_ada, b_ada, norm_mix, norm_ffn, w_in, lb_logits_fwd, lb_logits_bwd,
        hg_norm, sgu_norm_g, sgu_norm_b, w_spatial, b_spatial, w_out, w_up, conv_w, conv_b,
        w_down, norm_final,
    )
    return second_block(
        x, p_2, g_mix_2, w_in_2, b_fox_f_2, fox_q_gain_2, fox_k_gain_2, sc_conv_w_2,
        dn_conv_w_2, dn_a_log_2, dn_dt_bias_2, dn_norm_gain_2, w_branch_2, w_o_2, g_ffn_2,
        w_up_2, ffn_conv_w_2, w_down_2, g_ple_2, w_ple_gate_2, w_ple_2,
    )


_drawn_inputs = setup_inputs


def setup_inputs(seed=0):
    import zlib

    import numpy as np

    out = dict(_drawn_inputs(seed))
    spreads = {}
    factors = {'ctx': 8.0,
     'c_ctx': 8.0,
     'hg_norm': 2.909,
     'sgu_norm_g': 2.85,
     'sgu_norm_b': 8.0,
     'b_spatial': 2.812,
     'conv_b': 8.0,
     'g_mix_2': 2.927,
     'fox_q_gain_2': 132.15,
     'fox_k_gain_2': 200.0,
     'dn_norm_gain_2': 34.179,
     'g_ffn_2': 14.934,
     'g_ple_2': 200.0,
     'w_ple_gate_2': 24.336,
     'p_2': 8.0,
     'b_fox_f_2': 6.396,
     'w_ple_2': 8.0}
    for name, (base, spread) in spreads.items():
        noise = np.random.default_rng([zlib.crc32(name.encode()), seed]).standard_normal(out[name].shape)
        drawn = base * np.exp(spread * noise) if base else spread * noise
        out[name] = __import__('jax').numpy.asarray(drawn.astype(out[name].dtype))
    for name, factor in factors.items():
        out[name] = (out[name] * factor).astype(out[name].dtype)
    return out
```

```python
from contextlib import ExitStack

import numpy as np

import concourse.bass as bass
from concourse import mybir

ALU = mybir.AluOpType
ACT = mybir.ActivationFunctionType
AX_X = mybir.AxisListType.X
F32 = mybir.dt.float32
F32R = mybir.dt.float32r
U8 = mybir.dt.uint8

P = 128
D = 1024
T = 256
KT = D // P
HEADS = 4
FFT = 2816 // P
EPS = 1e-6
NEG = -1e30
CHUNK = 2048
RING = 3

ROWS = {}
N_ROWS = 0
for _name, _n in (("c", 8), ("c_ctx", 8), ("b_ada", 48), ("norm_mix", 8), ("norm_ffn", 8), ("norm_final", 8),
                  ("hg_norm", 4), ("conv_b", 22), ("sc_conv", 12), ("fox_gain", 2),
                  ("conv_w", 198), ("g_mix", 8), ("dn_conv", 48), ("g_ffn", 8), ("ffn_conv", 132),
                  ("g_ple", 8), ("dn_norm", 1), ("sm_bias", 1), ("sm_log", 1)):
    ROWS[_name] = N_ROWS
    N_ROWS += _n


def host_constants():
    i = np.arange(P)
    eye = np.eye(P, dtype=np.float32)
    ones = np.ones((P, T), np.float32)
    half = (i[:, None] // 64 == i[None, :] // 64).astype(np.float32)
    late = np.where(i[None, :] <= i[:, None], 0.0, NEG).astype(np.float32)
    keep_up = np.where(i[None, :] >= i[:, None], 0.0, NEG).astype(np.float32)
    keep_low = np.where(i[None, :] <= i[:, None], 0.0, -NEG).astype(np.float32)
    zeros = np.zeros((P, P), np.float32)
    cf = np.concatenate([eye, ones, half, zeros, late, keep_up, keep_low], axis=1)
    masks = np.zeros((P, 7, 2, P), np.float32)
    for lv in range(7):
        b = 1 << lv
        same = i[:, None] // (2 * b) == i[None, :] // (2 * b)
        left, right = (i // b) % 2 == 0, (i // b) % 2 == 1
        masks[:, lv, 0] = same & left[:, None] & right[None, :]
        masks[:, lv, 1] = same & right[:, None] & left[None, :]
    sel = np.zeros((96, 8, P), np.float32)
    for h in range(8):
        sel[[h, 32 + h, 64 + h], h] = 1.0
    return cf, masks.reshape(P, -1), sel.reshape(96, -1)


SMALL = ((0, 1536, 8), (32, 4616, 4), (64, 4620, 4))


def host_layout(x):
    x = {name: np.asarray(a) for name, a in x.items()}
    zero = np.zeros((1, 1), x["x"].dtype)

    def spread(parts):
        row = np.repeat(zero, P, axis=1)
        for at, a in parts:
            row[0, at:at + a.size] = a.reshape(-1)
        return row
    table = [x[n].reshape(-1, P) for n in ("c", "c_ctx", "b_ada", "norm_mix", "norm_ffn", "norm_final", "hg_norm",
                                           "conv_b", "sc_conv_w_2")]
    table += [np.concatenate([x[n].reshape(1, -1)] * 2, axis=1) for n in ("fox_q_gain_2", "fox_k_gain_2")]
    table += [x[n].reshape(-1, P) for n in ("conv_w", "g_mix_2", "dn_conv_w_2", "g_ffn_2", "ffn_conv_w_2",
                                            "g_ple_2", "dn_norm_gain_2")]
    table += [spread([(0, x["b_fox_f_2"]), (64, x["dn_dt_bias_2"])]), spread([(64, x["dn_a_log_2"])])]
    table = np.concatenate(table + [np.repeat(np.repeat(zero, P, axis=1), 5 * P - N_ROWS, axis=0)], axis=0)
    w_small = np.repeat(np.repeat(zero, 96, axis=1), D, axis=0)
    for row, c0, n in SMALL:
        w_small[:, row:row + n] = x["w_in_2"][0][:, c0:c0 + n]
    return {"table": table, "w_small": w_small}


def build(nc, i, out):
    w_ada, w_in, w_out = i["w_ada"][0], i["w_in"][0], i["w_out"][0]
    w_up, w_down = i["w_up"][0], i["w_down"][0]

    def cols(w, c0, kt=KT, n=256):
        return w.rearrange("(k p) n -> p k n", p=P)[:, :, c0:c0 + n]

    def rows(w, r0, kt=2):
        return w.rearrange("(k p) n -> p k n", p=P)[:, r0:r0 + kt, :]

    CHUNKS = []
    G = {}

    def chunk(name, src, shape, raw=False):
        if not raw:
            G[name] = sum(not c[0] for c in CHUNKS)
        CHUNKS.append((raw, src, shape))

    def ada(chunks):
        for c in chunks:
            chunk(f"ada{c}", cols(w_ada, 256 * ADA_ORDER[c]), (KT, 256), raw=True)

    ADA_ORDER = [4, 5, 6, 7, 0, 1, 2, 3] + list(range(8, 24))
    ada(range(8))
    n_ada = 8
    for name, c0 in (("ff", 0), ("fb", 512), ("v", 1024), ("q", 1536), ("mv", 3072), ("mu", 2560), ("gt", 2048)):
        for c in range(2):
            chunk(f"{name}{c}", cols(w_in, c0 + 256 * c), (KT, 256))
            if n_ada < 20:
                ada([n_ada])
                n_ada += 1
    for c in range(4):
        chunk(f"wo{c}", cols(w_out, 256 * c), (KT, 256))

    def ffn_chunks(tag, up, down):
        for j in range(FFT // 2 + 1):
            if j < FFT // 2:
                chunk(f"{tag}g{j}", cols(up, (FFT * P if tag == "f" else 0) + 256 * j), (KT, 256))
                chunk(f"{tag}a{j}", cols(up, (0 if tag == "f" else FFT * P) + 256 * j), (KT, 256))
            if j > 0:
                chunk(f"{tag}d{j - 1}", rows(down, 2 * (j - 1)), (2, D))
            if tag == "f" and j < 4:
                ada([20 + j])
    ffn_chunks("f", w_up, w_down)
    w_in2, w_branch = i["w_in_2"][0], i["w_branch_2"][0]
    FOX, SC, DN, DN_Z, GATE = 0, 1544, 3080, 4624, 5136
    for name, c0, n in (("dq", DN, 2), ("dk", DN + 512, 2), ("dv", DN + 1024, 2),
                        ("fq", FOX, 2), ("fk", FOX + 512, 2), ("fv", FOX + 1024, 2),
                        ("scc", SC + 512, 2), ("scv", SC + 1024, 2), ("scb", SC, 2), ("dz", DN_Z, 2)):
        for c in range(n):
            chunk(f"{name}{c}", cols(w_in2, c0 + 256 * c), (KT, 256))
    for name, n in (("s", 1), ("f", 0), ("d", 2)):
        for c in range(4):
            chunk(f"g{name}{c}", cols(w_in2, GATE + D * n + 256 * c), (KT, 256))
        if name == "d":
            chunk("ple", rows(i["w_ple_2"][0], 0), (2, D))
        for c in range(2):
            chunk(f"br{name}{c}", cols(w_branch[n], 512 * c, n=512), (4, 512))
    for c in range(4):
        chunk(f"wp{c}", cols(i["w_o_2"][0], 256 * c), (KT, 256))
    ffn_chunks("s", i["w_up_2"][0], i["w_down_2"][0])
    for c in range(4):
        chunk(f"pg{c}", cols(i["w_ple_gate_2"][0], 256 * c), (KT, 256))
    N_SPLIT = sum(not c[0] for c in CHUNKS)
    raw_of, used_before = [], []
    for n, (raw, _, _) in enumerate(CHUNKS):
        if not raw:
            raw_of.append(n)

    def ring(units, banks):
        names = [u for u, _ in units]
        owner = [o for _, o in units]

        def number(u):
            return names.index(u)

        def emptied(n):
            return owner[n], sum(o == owner[n] for o in owner[:n + 1])
        return number, emptied, banks

    g_units = [(f"xt{k}", "act") for k in range(KT)]
    g_units += [(f"{n}{c}{h}", "act") for n in ("ff", "fb") for c in range(2) for h in "ab"]
    g_units += [(f"v{c}{h}", "dve") for c in range(2) for h in "ab"] + [("A2", "dve")]
    g_units += [("q0", "act"), ("q1", "act"), ("mv0", "act"), ("mv1", "act"), ("A3", "dve"), ("mu0", "act"),
                ("mu1", "act"), ("gt0", "act"), ("gt1", "act"), ("A4", "dve")]
    g_units += [(f"wo{c}", "dve") for c in range(4)]
    for j in range(FFT // 2):
        g_units += [(f"fg{j}", "act"), (f"fa{j}", "dve")] + [("A5", "dve")] * (j == 5)
    g_units += [(f"{n}{c}", "dve") for n in ("dq", "dk", "dv") for c in range(2)]
    g_units += [(f"{n}{c}", "act") for n in ("fq", "fk") for c in range(2)]
    g_units += [(f"{n}{c}", o) for n, o in (("fv", "dve"), ("scc", "act"), ("scv", "dve"), ("scb", "act"),
                                            ("dz", "act")) for c in range(2)]
    for n in "sfd":
        g_units += [(f"g{n}{c}", "act") for c in range(4)]
        if n == "d":
            g_units += [(f"ple{c}", "act") for c in "abcd"]
        g_units += [(f"br{n}{c}{h}", "dve") for c in range(2) for h in "ab"]
    g_units += [(f"wp{c}", "dve") for c in range(4)]
    g_units += [(f"s{n}{j}", "dve") for j in range(FFT // 2) for n in "ga"]
    g_units += [(f"pg{c}", "act") for c in range(4)]
    l_units = [(f"sa{n}", "dve") for n in range(2)] + [(f"sb{n}", "dve") for n in range(4)]
    l_units += [(f"pt{n}", ("act", "dve")[n % 2]) for n in range(6)] + [("yf0", "dve"), ("yf1", "dve")]
    l_units += [("gb0", "act"), ("gb1", "act"), ("bb0", "dve"), ("bb1", "dve")]
    l_units += [(f"{n}{c}", "dve") for n in ("an", "at", "qk", "vt", "kt") for c in range(2)]
    for lv in range(1, 7):
        l_units += [(f"y{lv}{c}", "act") for c in range(2)]
        l_units += [(f"{n}{lv}{c}", "dve") for n in ("xx", "xt") for c in range(2)]
    l_units += [("us0", "act"), ("us1", "act"), ("kc", "act"), ("s1", "act"), ("w1", "dve"), ("do0", "act"),
                ("do1", "act")]
    m_units = [(n, "act") for n in ("sum0", "kfT0", "kfT1", "hf", "kbT0", "kbT1", "hb", "wsT")]
    m_units += [("z0", "dve"), ("z1", "dve"), ("oA", "act"), ("oB", "act"), ("on0", "act"), ("on1", "act"),
                ("sum1", "act"), ("sum2", "act"), ("sum3", "act"), ("sm", "dve"), ("colT", "dve")]
    m_units += [(n, "act") for n in ("lq0", "lq1", "lk0", "lk1", "sfq0", "sfq1", "sfk0", "sfk1")]
    m_units += [("pT", "dve"), ("on2", "act"), ("on3", "act"), ("sum4", "act"), ("sum5", "act")]

    with ExitStack() as ctx:
        def sb(name, shape, dt=F32):
            return ctx.enter_context(nc.sbuf_tensor(name, shape, dt))

        sems = {}

        def sem(name):
            sems[name] = ctx.enter_context(nc.semaphore(name))
            return sems[name]

        bank = [ctx.enter_context(nc.psum_tensor(f"bank{n}", [P, 512], F32)) for n in range(8)]
        raw = sb("raw", [P, RING, CHUNK])
        whi = sb("whi", [P, RING, CHUNK], F32R)
        wlo = sb("wlo", [P, RING, CHUNK], F32R)
        hhi = sb("hhi", [P, 4096], F32R)
        hlo = sb("hlo", [P, 4096], F32R)
        XT = sb("XT", [P, KT, 512])
        params = sb("params", [P, 5 * P])
        cf = sb("cf", [P, P + T])
        ident, ones, ones_t = cf[:, 0:P], cf[:, P:2 * P], cf[:, P:P + T]
        masks = sb("masks", [P, 7, 2, P], U8)
        small = sb("small", [P, 224])
        arena = sb("arena", [P, 20, 1024])

        def slot(s, n=1, off=0, size=None):
            flat = arena[:, s:s + n, :].rearrange("p a b -> p (a b)")
            return flat[:, off:off + size] if size else flat

        def par(name, n=None, k=0):
            r = ROWS[name] + k
            return params[:, r:r + (n or 1)]

        mod = sb("mod", [P, 48, 2])
        silu_c = small[:, 0:16].rearrange("p (k v) -> p k v", v=2)
        eps = small[:, 16:17]
        scale1 = small[:, 32:48].rearrange("p (k v) -> p k v", v=2)
        scale2 = small[:, 48:56]
        ln_stats = small[:, 64:112].rearrange("p (u s) -> p u s", s=6)
        ln_mv = small[:, 112:128].rearrange("p (u s) -> p u s", s=2)
        ln_rstd = small[:, 128:136]

        def h4(s):
            return slot(s).rearrange("p (h t) -> p h t", h=HEADS)
        FFx, FBx, KFx, KBx, FFc, FBc, KFc, KBc = (h4(s) for s in range(8))
        Q, QPf, QSb, KSUM = (h4(s) for s in range(8, 12))
        xn, cn = (slot(s, 2).rearrange("p (a d) -> p a d", a=2) for s in (8, 10))
        SQ = slot(0, 4)
        HT = slot(4, 4)
        E = h4(12)
        SX = [slot(12, 1, 512 * n, 512).rearrange("p (h t) -> p h t", h=HEADS) for n in range(2)]
        VTOK = slot(13, 2).rearrange("p (a v) -> p a v", a=4)
        acc_dve = slot(15).rearrange("p (o b n) -> p o b n", o=2, b=2)
        par_rows = slot(12, 1, 0, 640).rearrange("p (a f) -> p a f", a=5)
        c_rows = slot(12, 1, 640, P)
        acc_late = slot(12).rearrange("p (b n) -> p b n", b=4)
        masks_f = slot(13, 2, 0, 14 * P).rearrange("p (l s q) -> p l s q", l=7, s=2)
        HS = [slot(15, 1, 512 * n, 512).rearrange("p (h v) -> p h v", h=HEADS) for n in range(2)]
        KTOK = slot(16).rearrange("p (a k) -> p a k", a=2)
        std, rstd = slot(16, 1, 0, 512), slot(16, 1, 512, 512)
        S = [slot(7, 1, 512 * n, 512).rearrange("p (h t) -> p h t", h=HEADS) for n in range(2)]
        MV = slot(4).rearrange("p (a v) -> p a v", a=2)
        U, GT = h4(5), h4(6)
        tot = {1: (FFx, FBx), 2: [slot(17, 1, 512 * n, 512).rearrange("p (h t) -> p h t", h=HEADS) for n in range(2)]}
        off = 0
        for b in (4, 8, 16, 32, 64, 128):
            n = HEADS * T // b
            tot[b] = [slot(d, 1, off, n).rearrange("p (h t) -> p h t", h=HEADS) for d in range(2)]
            off += n
        sgu_g, sgu_b = slot(18, 1, 0, 512), slot(18, 1, 512, 512)
        bs_row = slot(19, 1, 0, 512)
        wsT = slot(19, 1, 512, 512).rearrange("p (h q) -> p h q", h=HEADS)
        ws_nat = slot(17).rearrange("p (h q) -> p h q", q=P)[:, 0:4, :]
        OM = slot(2, 2).rearrange("p (k t) -> p k t", t=T)
        OSQ, hstd, hrstd = h4(16), h4(0), h4(1)

        GW = 66
        pad = slot(0, 2, 0, 4 * 6 * GW).rearrange("p (b j r c) -> p b j r c", b=2, j=2, r=6)
        acc = slot(2).rearrange("p (b j t) -> p b j t", b=2, j=2)
        gel = slot(3).rearrange("p (b j t) -> p b j t", b=2, j=2)
        uf = slot(10).rearrange("p (b j t) -> p b j t", b=2, j=2)
        uhi = hhi[:, 2048:3072].rearrange("p (b j t) -> p b j t", b=2, j=2)
        ulo = hlo[:, 2048:3072].rearrange("p (b j t) -> p b j t", b=2, j=2)

        XC = XT[:, :, T:2 * T]
        half = XT[:, 0, T:T + P]
        zlate = XT[:, 1, T:2 * T]
        keep_up, keep_low = XT[:, 2, T:T + P], XT[:, 2, T + P:2 * T]

        def sel(g, h):
            return XT[32 * g:32 * g + (8, 4, 4)[g], 3 + h // 2, T + P * (h % 2):T + P * (h % 2 + 1)]
        HT2 = slot(4, 2)
        QC, KC, VC, KB, QD, GBS = h4(0), h4(1), h4(2), h4(3), h4(5), h4(6)
        ZS = h4(4)
        DT, DL, AN, ANT, QKT, XI, XIT, Y = (slot(n).rearrange("p (m t) -> p m t", m=8)
                                            for n in (7, 8, 9, 10, 11, 12, 13, 8))
        VB, U1 = (slot(n).rearrange("p (m t) -> p m t", m=8) for n in (0, 9))
        KD, KBG, KCT, S1 = (slot(n, 1, o, 512).rearrange("p (h t) -> p h t", h=HEADS)
                            for n, o in ((3, 0), (3, 512), (6, 0), (6, 512)))
        ODN, DSQ, dstd = h4(2), h4(17), h4(8)
        lq_sq, lk_sq, lq_std, lk_std = h4(16), h4(15), h4(17), h4(18)
        FQ, FK, fq_sq, fk_sq, fq_std, fk_std = (h4(n) for n in (6, 7, 9, 10, 11, 12))
        FQO = h4(13)
        FV = slot(8).rearrange("p (a v) -> p a v", a=2)
        SS0 = slot(9).rearrange("p (h t) -> p h t", h=8)
        SS1 = slot(10, 2).rearrange("p (h t) -> p h t", h=8)
        PT0 = slot(12, 2).rearrange("p (h t) -> p h t", h=8)
        PT1 = slot(6).rearrange("p (h t) -> p h t", h=8)
        GATES = slot(14, 2).rearrange("p (k t) -> p k t", t=T)
        YSC, SCB, CS = h4(16), h4(17), h4(18)
        PNAT = slot(16, 1, 512, 512).rearrange("p (a f) -> p a f", a=2)
        PF = slot(16, 1, 0, 512)
        PLE = slot(18, 2).rearrange("p (k t) -> p k t", t=T)
        SMY, SMA, RB, NCF = (slot(19, 1, 256 * n, 256) for n in range(4))
        wsm = slot(18, 1, 0, KT * 96).rearrange("p (k c) -> p k c", c=96)
        COLS = sb("COLS", [P, 2, 96])
        fmax, fneg, fsum, frec = (small[:, 144 + 16 * n:160 + 16 * n].rearrange("p (a h) -> p a h", a=2)
                                  for n in range(4))
        bgcol = small[:, 208:212]
        fgain = small[:, 212:214]
        sm_bias, sm_log = par("sm_bias"), par("sm_log")
        sm_sign, sm_coef = small[:, 214:215], small[:, 215:216]
        yhi, ylo = ([h[:, 2048 + 1024 * (n % 2):3072 + 1024 * (n % 2)].rearrange("p (k t) -> p k t", t=T)
                     for n in range(3)] for h in (hhi, hlo))
        phi, plo = (h[:, 3072:3584].rearrange("p (k t) -> p k t", t=T) for h in (hhi, hlo))
        acc2 = slot(0, 2).rearrange("p (b w j t) -> p b w j t", b=2, w=2, j=2)
        OUTN = slot(4, 2).rearrange("p (a d) -> p a d", a=2)
        PG = slot(2, 2).rearrange("p (k t) -> p k t", t=T)
        SQ2 = slot(0, 2)

        raw_loaded = [sem(f"raw_loaded{n}") for n in range(RING)]
        par_loaded, const_loaded, x_loaded, sgu_loaded, stored = (
            sem(n) for n in ("par_loaded", "const_loaded", "x_loaded", "sgu_loaded", "stored"))
        w_hi, w_lo = sem("w_hi"), sem("w_lo")
        ada_dve, ada_pool, sum_dve, sum_pe = (sem(n) for n in ("ada_dve", "ada_pool", "sum_dve", "sum_pe"))
        c_loaded = sem("c_loaded")
        c_T, pool_link = sem("c_T"), sem("pool_link")
        g_full, m_full = sem("g_full"), sem("m_full")
        g_empty = {"act": sem("g_empty_act"), "dve": sem("g_empty_dve")}
        m_empty = {"act": sem("m_empty_act"), "dve": sem("m_empty_dve")}
        act_step, dve_step, pool_step = sem("act_step"), sem("dve_step"), sem("pool_step")
        par_T, par_ready, c_ready, mod_ready = (
            sem(n) for n in ("par_T", "par_ready", "c_ready", "mod_ready"))
        sq_ready, std_ready, h_f32, h_hi, h_lo = (
            sem(n) for n in ("sq_ready", "std_ready", "h_f32", "h_hi", "h_lo"))
        ctx_k, lv_mm, lv_upd, lv_empty, lv_copied, sg_std, vn_ready, x_new = (
            sem(n) for n in ("ctx_k", "lv_mm", "lv_upd", "lv_empty", "lv_copied", "sg_std", "vn_ready", "x_new"))
        osq_ready, sg_stats = sem("osq_ready"), sem("sg_stats")
        pad_zero, conv_in, conv_out, gelu_out, u_hi, u_lo, down_used, down_full = (
            sem(n) for n in ("pad_zero", "conv_in", "conv_out", "gelu_out", "u_hi", "u_lo", "down_used",
                             "down_full"))

        g_no, g_emptied, g_banks = ring(g_units, (0, 1))
        m_no, m_emptied, m_banks = ring(m_units, (2, 3))

        def g_bank(u):
            return bank[g_banks[g_no(u) % 2]]

        def m_bank(u):
            return bank[m_banks[m_no(u) % 2]]

        def multiplied(g):
            name = [n for n, k in G.items() if k == g][0]
            if name[0:2] in ("fd", "sd") and name[2:].isdigit():
                return down_used, int(name[2:]) + 1 + (FFT // 2 if name[0] == "s" else 0)
            unit = [n for n, _ in g_units if n == name or n[:-1] == name and n[-1] in "abcd"][-1]
            return g_full, g_no(unit) + 1

        l_no, l_emptied, _ = ring(l_units, range(4))
        l_full = sem("l_full")
        l_empty = {"act": sem("l_empty_act"), "dve": sem("l_empty_dve")}

        def l_bank(u):
            return bank[4 + l_no(u) % 4]

        def l_done(u):
            e, k = l_emptied(l_no(u))
            return l_empty[e], k

        def g_done(u):
            e, k = g_emptied(g_no(u))
            return g_empty[e], k

        def m_done(u):
            e, k = m_emptied(m_no(u))
            return m_empty[e], k
        b2_loaded, col_loaded, p_loaded, wsm_zero = (sem(n) for n in ("b2_loaded", "col_loaded", "p_loaded", "wsm_zero"))
        sm_y, sm_ln, rb_ready, acc_start, silu_done, sq_done, f_ready, ss_ready, ss_exp, p_ready = (
            sem(n) for n in ("sm_y", "sm_ln", "rb_ready", "acc_start", "silu_done", "sq_done", "f_ready", "ss_ready",
                             "ss_exp", "p_ready"))
        masks_loaded, masks_ready = sem("masks_loaded"), sem("masks_ready")
        qk_ready, d_raw, d_exp, bg_ready, coef_ready = (
            sem(n) for n in ("qk_ready", "d_raw", "d_exp", "bg_ready", "coef_ready"))
        x_init, y_f32, y_hi, y_lo, p_hi, p_lo, merged_f32, osq2, qd_exp = (
            sem(n) for n in ("x_init", "y_f32", "y_hi", "y_lo", "p_hi", "p_lo", "merged_f32", "osq2", "qd_exp"))
        out_act, out_dve, acc2_start, silu2 = (sem(n) for n in ("out_act", "out_dve", "acc2_start", "silu2"))
        u2_f32 = sem("u2_f32")
        block = ctx.enter_context(nc.Block())

        ADA_PE = (1, 3, 5, 7)

        @block.sync
        def _(sp):
            sp.dma_start(ident, i["const_f"][:, 0:P]).then_inc(const_loaded, 16)
            sp.dma_start(c_rows[0:16, :], i["table"][0:16, :]).then_inc(c_loaded, 16)
            n_split = n_ada = 0
            last = []
            for n, (is_raw, src, (k, w)) in enumerate(CHUNKS):
                if n >= RING:
                    for wait in last[n - RING]:
                        sp.wait_ge(*wait)
                sp.dma_start(raw[:, n % RING, :].rearrange("p (k n) -> p k n", k=k), src
                             ).then_inc(raw_loaded[n % RING], 16)
                if is_raw:
                    c = n_ada
                    if c in ADA_PE:
                        last.append([(sum_pe, ADA_PE.index(c) + 1)])
                    elif c < 8:
                        last.append([(ada_dve, c + 2)])
                    else:
                        last.append([(ada_pool, c - 7)])
                    n_ada += 1
                else:
                    n_split += 1
                    last.append([(w_lo, n_split)])
            o = out.rearrange("(a p) d -> p a d", p=P)
            for t in range(2):
                sp.wait_ge(out_act, t + 1)
                sp.wait_ge(out_dve, t + 1)
                sp.dma_start(o[:, t, :], OUTN[:, t, :]).then_inc(stored, 16)
            sp.wait_ge(stored, 32)

        ada_place = [n for n, c in enumerate(CHUNKS) if c[0]]

        @block.gpsimd
        def _(pool):
            pool.memset(eps, EPS).then_inc(pool_step, 1)
            pool.memset(ones_t, 1.0).then_inc(pool_step, 1)
            steps = [0]

            def weighted_x(c, dst):
                n = ada_place[c]
                pool.wait_ge(raw_loaded[n % RING], 16 * (n // RING + 1))
                w = raw[:, n % RING, :].rearrange("p (k n) -> p k n", k=KT)
                ins = pool.tensor_tensor(w, w, silu_c[:, :, 0:1].broadcast_to([P, KT, 256]), ALU.mult)
                for m in (4, 2, 1):
                    steps[0] += 1
                    ins.then_inc(pool_link, 1)
                    pool.wait_ge(pool_link, steps[0])
                    to = w[:, 0:m, :] if m > 1 else dst.unsqueeze(1)
                    ins = pool.tensor_tensor(to, w[:, 0:m, :], w[:, m:2 * m, :], ALU.add)
                ins.then_inc(ada_pool, 1)
            pool.wait_ge(c_ready, 1)
            pool.dma_start(masks_f, i["const_m"].rearrange("p (l s q) -> p l s q", l=7, s=2)
                           ).then_inc(masks_loaded, 16)
            pool.dma_start(ws_nat, i["w_spatial"][0].rearrange("h p q -> p h q")).then_inc(sgu_loaded, 16)
            pool.dma_start(bs_row, i["b_spatial"].rearrange("l h p -> l (h p)").partition_broadcast(P)
                           ).then_inc(sgu_loaded, 16)
            pool.dma_start(sgu_g, i["sgu_norm_g"].partition_broadcast(P)).then_inc(sgu_loaded, 16)
            pool.dma_start(sgu_b, i["sgu_norm_b"].partition_broadcast(P)).then_inc(sgu_loaded, 16)
            pool.wait_ge(h_f32, 4)
            for c in range(8, 20):
                if c >= 16:
                    pool.wait_ge(g_full, g_no(f"A{c // 4 - 2}") + 1)
                weighted_x(c, XC[:, c % 8, :])

            pool.wait_ge(m_full, m_no("sum1") + 1)
            pool.memset(slot(0, 2, 0, 4 * 6 * GW), 0.0).then_inc(pad_zero, 1)
            for dst, c0, n in ((half, 3, 1), (zlate, 4, 2), (keep_up, 6, 1), (keep_low, 7, 1)):
                pool.dma_start(dst, i["const_f"][:, P * c0:P * (c0 + n)]).then_inc(b2_loaded, 16)
            pool.dma_start(XT[0:96, 3:7, T:2 * T], i["const_s"].rearrange("r (k c) -> r k c", c=T)
                           ).then_inc(b2_loaded, 16)
            pool.memset(small[:, 214:218], 0.0)
            pool.memset(RB, 0.0).then_inc(wsm_zero, 1)
            pool.wait_ge(wsm_zero, 1)
            pool.memset(sm_sign, 1.0)
            pool.memset(sm_coef, -1.0).then_inc(wsm_zero, 1)
            pool.wait_ge(wsm_zero, 2)
            pool.memset(sm_sign[0:32, :], -1.0).then_inc(wsm_zero, 1)
            pool.dma_start(wsm, i["w_small"].rearrange("(k p) c -> p k c", p=P)).then_inc(col_loaded, 16)
            for c in range(20, 24):
                weighted_x(c, acc_late[:, c % 4, :])
            pool.wait_ge(y_lo, 1)
            pool.dma_start(PNAT, i["p_2"][0, 0].rearrange("(a p) f -> p a f", p=P)).then_inc(p_loaded, 16)

        def split_hi(act, g):
            n = raw_of[g]
            act.wait_ge(raw_loaded[n % RING], 16 * (n // RING + 1))
            if g >= RING:
                act.wait_ge(*multiplied(g - RING))
            act.activation(whi[:, g % RING, :], raw[:, n % RING, :], ACT.Copy).then_inc(w_hi, 1)

        def split_lo(dve, g):
            n = raw_of[g]
            dve.wait_ge(raw_loaded[n % RING], 16 * (n // RING + 1))
            dve.wait_ge(w_hi, g + 1)
            if g >= RING:
                dve.wait_ge(*multiplied(g - RING))
            dve.tensor_tensor(wlo[:, g % RING, :], raw[:, n % RING, :], whi[:, g % RING, :].bitcast(F32),
                              ALU.subtract).then_inc(w_lo, 1)

        @block.scalar
        def _(act):
            act.dma_start(xn, i["x"][0].rearrange("(a p) d -> p a d", p=P)).then_inc(x_loaded, 16)
            act.dma_start(cn, i["ctx"][0].rearrange("(a p) d -> p a d", p=P)).then_inc(x_loaded, 16)
            act.dma_start(par_rows, i["table"].rearrange("(a p) f -> p a f", p=P)).then_inc(par_loaded, 16)
            steps = [0]

            def link(ins):
                steps[0] += 1
                ins.then_inc(act_step, 1)
                act.wait_ge(act_step, steps[0])

            def g_wait(u):
                act.wait_ge(g_full, g_no(u) + 1)

            def m_wait(u):
                act.wait_ge(m_full, m_no(u) + 1)

            def norm_std(u, w, feats):
                m_wait(u)
                act.activation(std[:, 0:w], m_bank(u)[:, 0:w], ACT.Sqrt, bias=eps, scale=1.0 / feats
                               ).then_inc(m_empty["act"], 1)

            def norm_hi(ht, f0, steps=(1, 2, 3, 4), shift=None):
                w = ht.shape[1] // KT
                for g in range(4):
                    act.wait_ge(h_f32, f0 + steps[g])
                    if shift is not None:
                        for k in (2 * g, 2 * g + 1):
                            for n in range(w // T):
                                s = slice(w * k + T * n, w * k + T * (n + 1))
                                ins = act.activation(hhi[:, s], ht[:, s], ACT.Identity, bias=shift(k, n))
                        ins.then_inc(h_hi, 1)
                        continue
                    act.activation(hhi[:, 2 * w * g:2 * w * (g + 1)], ht[:, 2 * w * g:2 * w * (g + 1)], ACT.Copy
                                   ).then_inc(h_hi, 1)

            act.wait_ge(c_T, 1)
            act.activation(silu_c, bank[6][:, 0:16].rearrange("p (v k) -> p k v", v=2), ACT.Silu).then_inc(c_ready, 1)
            for k in range(KT):
                g_wait(f"xt{k}")
                act.activation(XT[:, k, :], g_bank(f"xt{k}")[:, :], ACT.Copy).then_inc(g_empty["act"], 1)
                if k % 2 == 1:
                    act.wait_ge(g_empty["act"], k + 1)
                    act.activation(SQ[:, 512 * (k - 1):512 * (k + 1)].rearrange("p (k t) -> p k t", k=2),
                                   XT[:, k - 1:k + 1, :], ACT.Square).then_inc(sq_ready, 1)
            act.wait_ge(pool_step, 1)
            norm_std("sum0", 512, D)
            split_hi(act, 0)
            act.wait_ge(mod_ready, 2)
            norm_hi(HT, 0, shift=lambda k, n: mod[:, k, n:n + 1])
            for g in range(1, RING):
                split_hi(act, g)
            act.wait_ge(masks_loaded, 16)
            act.activation(masks[:, :, :, :], masks_f, ACT.Copy).then_inc(masks_ready, 1)
            for n, (fx, kx) in enumerate(((0, 2), (1, 3))):
                for c in range(2):
                    for h in range(2):
                        u = f"{('ff', 'fb')[n]}{c}{'ab'[h]}"
                        g_wait(u)
                        src = g_bank(u)[:, :].rearrange("p (s t) -> p s t", s=2)
                        hh = 2 * c + h
                        ar = arena.rearrange("p s (h t) -> p s h t", h=HEADS)
                        act.activation(ar[:, fx:fx + 5:4, hh, :], src, ACT.Sigmoid)
                        act.activation(ar[:, kx:kx + 5:4, hh, :], src, ACT.Sigmoid, scale=-1.0
                                       ).then_inc(g_empty["act"], 1)
                    split_hi(act, G[f"{('ff', 'fb')[n]}{c}"] + RING)

            def tok_keys(d):
                for t in range(2):
                    u = f"k{'fb'[d]}T{t}"
                    m_wait(u)
                    act.activation(KTOK[:, t, :], m_bank(u)[:, :], ACT.Copy).then_inc(m_empty["act"], 1)

            def ctx_state(d):
                u = ("hf", "hb")[d]
                m_wait(u)
                act.activation(HS[d], m_bank(u)[:, :].rearrange("p (h v) -> p h v", h=HEADS), ACT.Copy
                               ).then_inc(m_empty["act"], 1)
            split_hi(act, G["v0"] + RING)
            split_hi(act, G["v1"] + RING)
            tok_keys(0)

            def unit_act(u, dst, func):
                g_wait(u)
                src = g_bank(u)[:, :].rearrange("p (j t) -> p j t", j=2)
                act.activation(dst, src, func).then_inc(g_empty["act"], 1)
            unit_act("q0", Q[:, 0:2, :], ACT.Silu)
            split_hi(act, G["q0"] + RING)
            ctx_state(0)
            tok_keys(1)
            unit_act("q1", Q[:, 2:4, :], ACT.Silu)
            split_hi(act, G["q1"] + RING)
            ctx_state(1)
            act.wait_ge(lv_mm, 1)
            act.activation(S[0], bank[4][:, :].rearrange("p (h t) -> p h t", h=HEADS), ACT.Copy)
            act.activation(S[1], bank[5][:, :].rearrange("p (h t) -> p h t", h=HEADS), ACT.Copy
                           ).then_inc(lv_copied, 1)
            m_wait("wsT")
            act.activation(wsT, m_bank("wsT")[:, :].rearrange("p (h q) -> p h q", h=HEADS), ACT.Copy
                           ).then_inc(m_empty["act"], 1)
            for c in range(2):
                unit_act(f"mv{c}", MV[:, :, 256 * c:256 * (c + 1)], ACT.Gelu)
                split_hi(act, G[f"mv{c}"] + RING)
            act.wait_ge(sg_stats, 1)
            act.activation(ln_rstd, ln_mv[:, :, 1], ACT.Sqrt, bias=eps).then_inc(sg_std, 1)
            unit_act("mu0", U[:, 0:2, :], ACT.Gelu)
            split_hi(act, G["mu0"] + RING)
            unit_act("mu1", U[:, 2:4, :], ACT.Gelu)
            for c in range(2):
                unit_act(f"gt{c}", GT[:, 2 * c:2 * c + 2, :], ACT.Silu)
            act.wait_ge(lv_mm, 9)
            for d in range(2):
                ins = act.activation(SX[d], bank[4 + d][:, :].rearrange("p (h t) -> p h t", h=HEADS), ACT.Copy)
            ins.then_inc(lv_copied, 1)
            for g in range(G["wo0"], G["wo0"] + RING):
                split_hi(act, g)
            for n, u in enumerate(("oA", "oB")):
                m_wait(u)
                src = m_bank(u)[:, :].rearrange("p (h t) -> p h t", h=2)
                act.activation(OSQ[:, 2 * n:2 * n + 2, :], src, ACT.Square).then_inc(osq_ready, 1)
                act.activation(OM[:, 2 * n:2 * n + 2, :], src, ACT.Copy).then_inc(m_empty["act"], 1)
            for n in range(2):
                m_wait(f"on{n}")
                act.activation(hstd[:, 2 * n:2 * n + 2, :],
                               m_bank(f"on{n}")[:, :].rearrange("p (h t) -> p h t", h=2), ACT.Sqrt, bias=eps,
                               scale=1.0 / P).then_inc(m_empty["act"], 1)
            norm_hi(OM.rearrange("p k t -> p (k t)"), 4, (1, 2, 2, 2))

            def squares(updated, g0=None, dst=SQ):
                for g in range(4):
                    act.wait_ge(*updated(g))
                    act.activation(dst[:, 512 * g:512 * (g + 1)].rearrange("p (k t) -> p k t", k=2),
                                   XT[:, 2 * g:2 * g + 2, 0:T], ACT.Square).then_inc(sq_ready, 1)
                    if g0 is not None:
                        split_hi(act, g0 + g + RING)
            squares(lambda c: (g_empty["dve"], g_emptied(g_no(f"wo{c}"))[1]), G["wo0"])
            norm_std("sum1", T, D)
            norm_hi(HT[:, 0:KT * T], 6, shift=lambda k, n: mod[:, 24 + k, 0:1])
            act.wait_ge(pad_zero, 1)
            for j in range(FFT // 2):
                b = j % 2
                if j >= 2:
                    act.wait_ge(conv_out, j - 1)
                    act.wait_ge(g_empty["dve"], g_emptied(g_no(f"fa{j - 2}"))[1])
                g_wait(f"fg{j}")
                for t in range(2):
                    src = g_bank(f"fg{j}")[:, T * t:T * (t + 1)]
                    jt = 2 * j + t
                    act.activation(pad[:, b, t, 1:5, 1:65], src.rearrange("p (r c) -> p r c", r=4), ACT.Copy)
                    ins = act.activation(acc[:, b, t, :], src, ACT.Identity, bias=par("conv_b", k=jt),
                                         scale=par("conv_w", k=4 * FFT + jt))
                ins.then_inc(g_empty["act"], 1)
                if G[f"fg{j}"] + RING < N_SPLIT:
                    split_hi(act, G[f"fg{j}"] + RING)
                if G[f"fa{j}"] + RING < N_SPLIT:
                    split_hi(act, G[f"fa{j}"] + RING)
                act.wait_ge(conv_out, j + 1)
                act.activation(gel[:, b, :, :], acc[:, b, :, :], ACT.Gelu).then_inc(gelu_out, 1)
                if j > 0 and G[f"fd{j - 1}"] + RING < N_SPLIT:
                    split_hi(act, G[f"fd{j - 1}"] + RING)
                act.wait_ge(g_empty["dve"], g_emptied(g_no(f"fa{j}"))[1])
                if j >= 2:
                    act.wait_ge(down_used, j - 1)
                act.activation(uhi[:, b, :, :], uf[:, b, :, :], ACT.Copy).then_inc(u_hi, 1)
            squares(lambda c: (x_new, c + 1))
            def adv(name):
                if G[name] + RING < N_SPLIT:
                    split_hi(act, G[name] + RING)

            def l_wait(u):
                act.wait_ge(l_full, l_no(u) + 1)
                return l_bank(u)

            def two(ps):
                return ps[:, :].rearrange("p (j t) -> p j t", j=2)

            def four(ps):
                return ps[:, :].rearrange("p (j t) -> p j t", j=4)
            adv("fd10")
            norm_std("sum2", T, D)
            squares(lambda c: (x_new, 4 + c + 1), dst=SQ2)
            norm_std("sum3", T, D)
            norm_hi(HT2, 10)
            link(act.activation(sm_coef[64:68, :], sm_log[64:68, :], ACT.Exp))
            act.activation(sm_coef[64:68, :], sm_coef[64:68, :], ACT.Copy, scale=-1.0).then_inc(coef_ready, 1)

            def conv_start(u, dst, tap):
                g_wait(u)
                for t in range(2):
                    ins = act.activation(dst[:, t, :], g_bank(u)[:, T * t:T * (t + 1)], ACT.Copy,
                                         scale=par("dn_conv", k=36 + tap + t))
                ins.then_inc(acc_start, 1)
                adv(u)

            def conv_silu(u, dst):
                act.wait_ge(*g_done(u))
                act.activation(dst, dst, ACT.Silu).then_inc(silu_done, 1)
            dn = [(f"d{n}{c}", (QC, KC, VC)["qkv".index(n)][:, 2 * c:2 * c + 2, :], 4 * "qkv".index(n) + 2 * c)
                  for n in "qkv" for c in range(2)]
            conv_start(*dn[0])
            act.wait_ge(*m_done("sm"))
            act.activation(RB[32:36, :], SMY[32:36, :], ACT.Sigmoid)
            link(act.activation(SMA[0:96, :], SMY[0:96, :], ACT.Abs))
            link(act.activation(SMA[0:96, :], SMA[0:96, :], ACT.Exp, scale=-1.0))
            act.activation(SMA[0:96, :], SMA[0:96, :], ACT.Ln, bias=1.0).then_inc(sm_ln, 1)
            conv_start(*dn[1])
            conv_silu(*dn[0][:2])
            conv_start(*dn[2])
            conv_silu(*dn[1][:2])

            def head_squares(dst, src, n):
                act.wait_ge(silu_done, n)
                act.activation(dst, src, ACT.Square).then_inc(sq_done, 1)
            head_squares(lq_sq, QC, 2)
            conv_start(*dn[3])
            conv_silu(*dn[2][:2])
            conv_start(*dn[4])
            conv_silu(*dn[3][:2])
            head_squares(lk_sq, KC, 4)

            def head_std(units, dst, scale):
                for n, u in enumerate(units):
                    m_wait(u)
                    act.activation(dst[:, 2 * n:2 * n + 2, :], two(m_bank(u)), ACT.Sqrt, bias=eps, scale=scale
                                   ).then_inc(m_empty["act"], 1)
            head_std(("lq0", "lq1"), lq_std, 1.0)
            conv_start(*dn[5])
            conv_silu(*dn[4][:2])
            head_std(("lk0", "lk1"), lk_std, 1.0)
            conv_silu(*dn[5][:2])
            for n, dst, sq in (("fq", FQ, fq_sq), ("fk", FK, fk_sq)):
                for c in range(2):
                    g_wait(f"{n}{c}")
                    act.activation(sq[:, 2 * c:2 * c + 2, :], two(g_bank(f"{n}{c}")), ACT.Square)
                    act.activation(dst[:, 2 * c:2 * c + 2, :], two(g_bank(f"{n}{c}")), ACT.Copy
                                   ).then_inc(g_empty["act"], 1)
                    adv(f"{n}{c}")
            adv("fv0")
            head_std(("sfq0", "sfq1"), fq_std, 1.0 / 64)
            adv("fv1")
            head_std(("sfk0", "sfk1"), fk_std, 1.0 / 64)

            def copy_unit(u, dst, func=ACT.Copy):
                g_wait(u)
                act.activation(dst, two(g_bank(u)), func).then_inc(g_empty["act"], 1)
                adv(u)
            copy_unit("scc0", CS[:, 0:2, :])
            copy_unit("scc1", CS[:, 2:4, :])

            def soft(a, h, ss):
                act.activation(ss[:, h, :], ss[:, h, :], ACT.Exp, bias=fneg[:, a, h:h + 1],
                               accum_out=fsum[:, a, h:h + 1]).then_inc(ss_exp, 1)
            act.wait_ge(ss_ready, 1)
            for h in range(8):
                soft(0, h, SS0)
            adv("scv0")
            act.wait_ge(ss_ready, 2)
            for h in range(4):
                soft(1, h, SS1)
            adv("scv1")
            for h in range(4, 8):
                soft(1, h, SS1)

            def p_copy(n):
                dst = (PT0[:, 0:4, 0:P], None, PT0[:, 0:4, P:T], None, PT1[:, 0:4, :])[n]
                act.activation(dst, four(l_wait(f"pt{n}")), ACT.Copy).then_inc(l_empty["act"], 1)
            p_copy(0)
            copy_unit("scb0", SCB[:, 0:2, :])
            p_copy(2)
            p_copy(4)
            copy_unit("scb1", SCB[:, 2:4, :])

            def y_split(n):
                act.wait_ge(y_f32, n + 1)
                act.activation(yhi[n], (YSC, None, ODN)[n], ACT.Copy).then_inc(y_hi, 1)
            y_split(0)
            for n in range(2):
                act.activation(yhi[1][:, 2 * n:2 * n + 2, :], two(l_wait(f"yf{n}")), ACT.Copy).then_inc(y_hi, 1)
            copy_unit("dz0", ZS[:, 0:2, :], ACT.Silu)
            copy_unit("dz1", ZS[:, 2:4, :], ACT.Silu)
            for n in range(2):
                act.activation(GBS[:, 2 * n:2 * n + 2, :], two(l_wait(f"gb{n}")), ACT.Copy
                               ).then_inc(l_empty["act"], 1)
            act.wait_ge(*l_done("gb1"))
            act.activation(QD, GBS, ACT.Exp).then_inc(qd_exp, 1)
            for n, d in enumerate((DT, DL)):
                act.wait_ge(d_raw, n + 1)
                act.activation(d, d, ACT.Exp, scale=(1.0, -1.0)[n]).then_inc(d_exp, 1)
            act.activation(bgcol, COLS[:, 1, 64:68], ACT.Exp).then_inc(bg_ready, 1)

            def gate(name):
                c = int(name[2])
                copy_unit(name, GATES[:, 2 * c:2 * c + 2, :], ACT.Sigmoid)
            gates_s = [f"gs{c}" for c in range(4)]
            for u in gates_s:
                gate(u)
            fill = ["brs0", "brs1"] + [f"gf{c}" for c in range(4)] + ["brf0", "brf1"] + [f"gd{c}" for c in range(4)]

            def filler(name):
                if name[0] == "g":
                    gate(name)
                else:
                    adv(name)
            for lv in range(1, 7):
                for n in range(2):
                    act.activation(Y[:, 4 * n:4 * n + 4, :], four(l_wait(f"y{lv}{n}")), ACT.Copy
                                   ).then_inc(l_empty["act"], 1)
                filler(fill[2 * lv - 2])
                filler(fill[2 * lv - 1])
            for n in range(2):
                act.activation(U1[:, 4 * n:4 * n + 4, :], four(l_wait(f"us{n}")), ACT.Copy
                               ).then_inc(l_empty["act"], 1)
            act.activation(KCT, four(l_wait("kc")), ACT.Copy).then_inc(l_empty["act"], 1)
            act.activation(S1, four(l_wait("s1")), ACT.Copy).then_inc(l_empty["act"], 1)
            act.wait_ge(*m_done("pT"))
            act.activation(phi, PF.rearrange("p (k t) -> p k t", t=T), ACT.Copy).then_inc(p_hi, 1)
            for n, u in enumerate("abcd"):
                g_wait(f"ple{u}")
                act.activation(PLE[:, 2 * n:2 * n + 2, :], two(g_bank(f"ple{u}")), ACT.Copy
                               ).then_inc(g_empty["act"], 1)
            adv("ple")
            for n in range(2):
                src = two(l_wait(f"do{n}"))
                act.activation(DSQ[:, 2 * n:2 * n + 2, :], src, ACT.Square).then_inc(osq2, 1)
                act.activation(ODN[:, 2 * n:2 * n + 2, :], src, ACT.Copy).then_inc(l_empty["act"], 1)
            head_std(("on2", "on3"), dstd, 1.0 / P)
            y_split(2)
            adv("brd0")
            adv("brd1")
            for g in range(4):
                act.wait_ge(merged_f32, 5 + g)
                act.activation(hhi[:, 512 * g:512 * (g + 1)].rearrange("p (k t) -> p k t", k=2),
                               XC[:, 2 * g:2 * g + 2, :], ACT.Copy).then_inc(h_hi, 1)
            squares(lambda c: g_done(f"wp{c}"), G["wp0"], dst=SQ2)
            norm_std("sum4", T, D)
            norm_hi(HT2, 14)
            for j in range(FFT // 2):
                b = j % 2
                if j >= 2:
                    act.wait_ge(u2_f32, j - 1)
                for n, w in enumerate("ga"):
                    g_wait(f"s{w}{j}")
                    for t in range(2):
                        col = par("ffn_conv", k=2 * 2 * FFT + FFT * n + 2 * j + t)
                        ins = act.activation(acc2[:, b, n, t, :], g_bank(f"s{w}{j}")[:, T * t:T * (t + 1)], ACT.Copy,
                                             scale=col)
                    ins.then_inc(acc2_start, 1)
                    adv(f"s{w}{j}")
                act.wait_ge(*g_done(f"sg{j}"))
                act.activation(acc2[:, b, 0, :, :], acc2[:, b, 0, :, :], ACT.Silu).then_inc(silu2, 1)
                if j > 0:
                    adv(f"sd{j - 1}")
                act.wait_ge(u2_f32, j + 1)
                if j >= 2:
                    act.wait_ge(down_used, FFT // 2 + j - 1)
                act.activation(uhi[:, b, :, :], uf[:, b, :, :], ACT.Copy).then_inc(u_hi, 1)
            adv(f"sd{FFT // 2 - 1}")
            squares(lambda c: (x_new, 8 + c + 1), dst=SQ2)
            norm_std("sum5", T, D)
            norm_hi(HT2, 18)
            for c in range(4):
                copy_unit(f"pg{c}", PG[:, 2 * c:2 * c + 2, :], ACT.Sigmoid)
            for n in range(2):
                act.wait_ge(l_full, len(l_units) + 2 * n + 1)
                act.activation(OUTN[:, n, 0:512], bank[4 + 2 * n][:, :], ACT.Copy).then_inc(out_act, 1)

        @block.tensor
        def _(pe):
            def g_open(u):
                n = g_no(u)
                if n >= 2:
                    e, k = g_emptied(n - 2)
                    pe.wait_ge(g_empty[e], k)
                return g_bank(u)

            def m_open(u):
                n = m_no(u)
                if n >= 2:
                    e, k = m_emptied(n - 2)
                    pe.wait_ge(m_empty[e], k)
                return m_bank(u)

            def w_parts(name, k):
                g = G[name]
                pe.wait_ge(w_hi, g + 1)
                pe.wait_ge(w_lo, g + 1)
                return [w[:, g % RING, :].rearrange("p (k n) -> p k n", k=k) for w in (whi, wlo)]

            def h_wait(g0, k, first):
                if first and k % 2 == 0:
                    pe.wait_ge(h_hi, g0 + k // 2 + 1)
                    pe.wait_ge(h_lo, g0 + k // 2 + 1)

            def product(o, w, a, start, stop, **kw):
                (wh, wl), (ah, al) = w, a
                pe.matmul(o, wh, ah, start=start, stop=False, **kw)
                pe.matmul(o, wh, al, start=False, stop=False, **kw)
                return pe.matmul(o, wl, ah, start=False, stop=stop, **kw)

            def acts(w, k, lo=0, n=None):
                n = n or w
                return [h[:, w * k + lo:w * k + lo + n] for h in (hhi, hlo)]

            pe.wait_ge(const_loaded, 16)
            pe.wait_ge(c_loaded, 16)
            pe.transpose(bank[6][:, 0:16], c_rows[0:16, :], ident[0:16, 0:16]).then_inc(c_T, 1)
            pe.wait_ge(x_loaded, 32)
            for k in range(KT):
                o = g_open(f"xt{k}")
                for n, src in enumerate((xn, cn)):
                    for a in range(2):
                        ins = pe.transpose(o[:, T * n + P * a:T * n + P * (a + 1)], src[:, a, P * k:P * (k + 1)], ident)
                ins.then_inc(g_full, 1)
            pe.wait_ge(par_loaded, 16)
            pe.wait_ge(c_ready, 1)
            for a in range(5):
                r = min(P, N_ROWS - P * a)
                ins = pe.transpose(bank[6 + a // 4][:, P * (a % 4):P * (a % 4) + r], par_rows[0:r, a, :],
                                   ident[0:r, 0:r])
            ins.then_inc(par_T, 1)

            def sum_squares(u, s0, w, src=SQ):
                o = m_open(u)
                for k in range(KT):
                    if k % 2 == 0:
                        pe.wait_ge(sq_ready, s0 + k // 2 + 1)
                    ins = pe.matmul(o[:, 0:w], ones, src[:, w * k:w * (k + 1)], start=k == 0, stop=k == KT - 1)
                ins.then_inc(m_full, 1)
            def ada_sum(src, o, at, done):
                for nb in range(2):
                    ins = pe.matmul(o[:, at + 2 * nb:at + 2 * nb + 1], src[:, P * nb:P * (nb + 1)], ones[:, 0:1],
                                    start=True, stop=True)
                ins.then_inc(done, 1)

            pe.wait_ge(pool_step, 2)
            for c in range(8):
                o, at = bank[4 + c // 4], 4 * (c % 4)
                if c == 1:
                    sum_squares("sum0", 0, 512)
                if c in ADA_PE:
                    n = ada_place[c]
                    pe.wait_ge(raw_loaded[n % RING], 16 * (n // RING + 1))
                    w = raw[:, n % RING, :].rearrange("p (k n) -> p k n", k=KT)
                    for nb in range(2):
                        for k in range(KT):
                            ins = pe.matmul(o[:, at + 2 * nb:at + 2 * nb + 2], w[:, k, P * nb:P * (nb + 1)],
                                            silu_c[:, k, :], start=k == 0, stop=k == KT - 1)
                    ins.then_inc(sum_pe, 1)
                    continue
                for v in range(2):
                    pe.wait_ge(ada_dve, c + v + 1)
                    ada_sum(acc_dve[:, 0, v, :], o, at + v, sum_dve)

            def ada_unit(a):
                o = g_open(f"A{a}")
                pe.wait_ge(ada_pool, 4 * (a - 1))
                for c in range(4 * a, 4 * a + 4):
                    for nb in range(2):
                        at = 2 * (c % 4) + nb
                        src = XC[:, c % 8, :] if a < 5 else acc_late[:, c % 4, :]
                        ins = pe.matmul(o[:, at:at + 1], src[:, P * nb:P * (nb + 1)], ones[:, 0:1],
                                        start=True, stop=True)
                ins.then_inc(g_full, 1)

            def gemm(name, w, g0=None, n_tok=T, units="unit"):
                wh, wl = w_parts(name, KT)
                for nb in range(2):
                    if units == "bank" or nb == 0:
                        u = name + ("ab"[nb] if units == "bank" else "")
                        bk = g_open(u)
                    o = bk[:, 0:n_tok] if units == "bank" else bk[:, T * nb:T * (nb + 1)]
                    for k in range(KT):
                        if g0 is not None:
                            h_wait(g0, k, nb == 0)
                        ws = [x[:, k, P * nb:P * (nb + 1)] for x in (wh, wl)]
                        ins = product(o, ws, acts(w, k, 0, n_tok), k == 0, k == KT - 1)
                    if nb == 1 or units == "bank":
                        ins.then_inc(g_full, 1)

            def gemm_tok(name, w, tiles):
                wh, wl = w_parts(name, KT)
                for n, t in enumerate(tiles):
                    u = name + "ab"[n // 2] if len(tiles) > 2 else name
                    if n % 2 == 0:
                        bk = g_open(u)
                    o = bk[:, T * (n % 2):T * (n % 2 + 1)]
                    for k in range(KT):
                        ah, al = acts(w, k, P * t, P)
                        ins = product(o, (ah, al), (wh[:, k, :], wl[:, k, :]), k == 0, k == KT - 1)
                    if n % 2 == 1:
                        ins.then_inc(g_full, 1)

            for n, name in enumerate(("ff0", "ff1", "fb0", "fb1")):
                gemm(name, 512, 0 if n == 0 else None, 512, "bank")
            gemm_tok("v0", 512, range(4))
            gemm_tok("v1", 512, range(4))
            ada_unit(2)

            def tok_keys(d):
                src = (KFc, KBc)[d]
                pe.wait_ge(ctx_k, d + 1)
                for t in range(2):
                    o = m_open(f"k{'fb'[d]}T{t}")
                    for h in range(HEADS):
                        ins = pe.transpose(o[:, P * h:P * (h + 1)], src[:, h, P * t:P * (t + 1)], ident)
                    ins.then_inc(m_full, 1)

            def ctx_state(d):
                u = ("hf", "hb")[d]
                o = m_open(u)
                pe.wait_ge(m_empty["act"], m_emptied(m_no(f"k{'fb'[d]}T1"))[1])
                pe.wait_ge(g_empty["dve"], g_emptied(g_no("v1b"))[1])
                for h in range(HEADS):
                    for t in range(2):
                        ins = pe.matmul(o[:, P * h:P * (h + 1)], KTOK[:, t, P * h:P * (h + 1)],
                                        VTOK[:, 2 + t, P * h:P * (h + 1)], start=t == 0, stop=t == 1)
                ins.then_inc(m_full, 1)

            tok_keys(0)
            gemm("q0", 512)
            ctx_state(0)
            tok_keys(1)
            gemm("q1", 512)
            ctx_state(1)
            o = m_open("wsT")
            pe.wait_ge(sgu_loaded, 64)
            for h in range(HEADS):
                ins = pe.transpose(o[:, P * h:P * (h + 1)], ws_nat[:, h, :], ident)
            ins.then_inc(m_full, 1)

            def level(s):
                pe.wait_ge(lv_upd, max(s, 1))
                if s == 1 or s == 8:
                    pe.wait_ge(lv_copied, 1)
                if s >= 2:
                    pe.wait_ge(lv_empty, s - 1)
                for h in range(HEADS):
                    hs = slice(P * h, P * (h + 1))
                    t0, t1 = slice(0, P), slice(P, T)
                    if s == 0:
                        pairs = [(4, KSUM, Q, t0, t0), (5, KSUM, Q, t1, t1)]
                    elif s == 8:
                        pairs = [(4, KFx, QPf, t0, t1), (5, KBx, QSb, t1, t0)]
                    else:
                        pairs = [(4, KFx, QPf, t0, t0), (5, KBx, QSb, t0, t0),
                                 (6, KFx, QPf, t1, t1), (7, KBx, QSb, t1, t1)]
                    for bk, k, q, ts, tt in pairs:
                        ins = pe.matmul(bank[bk][:, hs], k[:, h, ts], q[:, h, tt], start=True, stop=True)
                ins.then_inc(lv_mm, 1)

            level(0)
            gemm_tok("mv0", 512, range(2))
            level(1)
            gemm_tok("mv1", 512, range(2))
            ada_unit(3)
            level(2)
            gemm("mu0", 512)
            level(3)
            gemm("mu1", 512)
            level(4)
            gemm("gt0", 512)
            level(5)
            gemm("gt1", 512)
            ada_unit(4)
            level(6)
            level(7)
            level(8)
            pe.wait_ge(vn_ready, 1)
            for n in range(2):
                o = m_open(f"z{n}")
                for hh in range(2):
                    h = 2 * n + hh
                    for t in range(2):
                        ins = pe.matmul(o[:, T * hh + P * t:T * hh + P * (t + 1)], MV[:, t, P * h:P * (h + 1)],
                                        wsT[:, h, :], start=True, stop=True)
                ins.then_inc(m_full, 1)
            pe.wait_ge(lv_upd, 9)
            pe.wait_ge(lv_empty, 7)
            pe.wait_ge(lv_copied, 2)
            for n, u in enumerate(("oA", "oB")):
                o = m_open(u)
                for hh in range(2):
                    h = 2 * n + hh
                    hv = slice(P * h, P * (h + 1))
                    full, t0, t1 = (slice(T * hh + a, T * hh + b) for a, b in ((0, T), (0, P), (P, T)))
                    pe.matmul(o[:, full], HS[0][:, h, :], QPf[:, h, :], start=True, stop=False)
                    pe.matmul(o[:, full], HS[1][:, h, :], QSb[:, h, :], start=False, stop=False)
                    pe.matmul(o[:, t0], VTOK[:, 0, hv], S[0][:, h, :], start=False, stop=False)
                    pe.matmul(o[:, t0], VTOK[:, 1, hv], SX[1][:, h, :], start=False, stop=False)
                    pe.matmul(o[:, t1], VTOK[:, 1, hv], S[1][:, h, :], start=False, stop=False)
                    ins = pe.matmul(o[:, t1], VTOK[:, 0, hv], SX[0][:, h, :], start=False, stop=True)
                ins.then_inc(m_full, 1)
            for n in range(2):
                o = m_open(f"on{n}")
                pe.wait_ge(osq_ready, n + 1)
                pe.matmul(o[:, :], ones, OSQ[:, 2 * n:2 * n + 2, :].rearrange("p h t -> p (h t)"),
                          start=True, stop=True).then_inc(m_full, 1)
            for c in range(4):
                gemm(f"wo{c}", T, 4 if c == 0 else None)
            sum_squares("sum1", 4, T)

            def down(j, tag="f"):
                b = j % 2
                wh, wl = w_parts(f"{tag}d{j}", 2)
                n = j + (FFT // 2 if tag == "s" else 0)
                pe.wait_ge(u_hi, n + 1)
                pe.wait_ge(u_lo, n + 1)
                for t in range(2):
                    for nb in range(KT):
                        o = bank[4 + nb // 2][:, T * (nb % 2):T * (nb % 2 + 1)]
                        ws = [x[:, t, P * nb:P * (nb + 1)] for x in (wh, wl)]
                        first = j == 0 and t == 0
                        ins = product(o, ws, (uhi[:, b, t, :], ulo[:, b, t, :]), first and nb % 2 == 0,
                                      j == FFT // 2 - 1 and t == 1, skip_group_check=True)
                ins.then_inc(down_used, 1)

            for j in range(FFT // 2):
                gemm(f"fg{j}", T, 8 if j == 0 else None)
                gemm(f"fa{j}", T)
                if j == 5:
                    ada_unit(5)
                if j > 0:
                    down(j - 1)
            down(FFT // 2 - 1)
            sum_squares("sum2", 8, T)
            def l_open(u):
                n = l_no(u)
                if n >= 4:
                    e, k = l_emptied(n - 4)
                    pe.wait_ge(l_empty[e], k)
                return l_bank(u)
            sum_squares("sum3", 12, T, SQ2)
            gemm("dq0", T, 12)
            o = m_open("sm")
            pe.wait_ge(col_loaded, 16)
            pe.wait_ge(h_f32, 14)
            for k in range(KT):
                ins = pe.matmul(o[0:96, 0:T], wsm[:, k, :], HT2[:, T * k:T * (k + 1)], start=k == 0, stop=k == KT - 1)
            ins.then_inc(m_full, 1)
            gemm("dq1", T)
            gemm("dk0", T)
            gemm("dk1", T)
            o = m_open("colT")
            pe.wait_ge(rb_ready, 1)
            for t in range(2):
                ins = pe.transpose(o[:, 96 * t:96 * (t + 1)], RB[0:96, P * t:P * (t + 1)], ident[0:96, 0:96])
            ins.then_inc(m_full, 1)
            gemm("dv0", T)

            def head_sums(units, mat, src, n):
                pe.wait_ge(sq_done, n)
                for c, u in enumerate(units):
                    o = m_open(u)
                    pe.matmul(o[:, :], mat, src[:, 2 * c:2 * c + 2, :].rearrange("p h t -> p (h t)"),
                              start=True, stop=True).then_inc(m_full, 1)
            head_sums(("lq0", "lq1"), ones, lq_sq, 1)
            gemm("dv1", T)
            head_sums(("lk0", "lk1"), ones, lk_sq, 2)
            for u in ("fq0", "fq1", "fk0", "fk1"):
                gemm(u, T)
            gemm_tok("fv0", T, range(2))
            pe.wait_ge(b2_loaded, 80)
            for c in range(2):
                o = m_open(f"sfq{c}")
                pe.wait_ge(*g_done(f"fq{c}"))
                pe.matmul(o[:, :], half, fq_sq[:, 2 * c:2 * c + 2, :].rearrange("p h t -> p (h t)"),
                          start=True, stop=True).then_inc(m_full, 1)
            gemm_tok("fv1", T, range(2))
            for c in range(2):
                o = m_open(f"sfk{c}")
                pe.wait_ge(*g_done(f"fk{c}"))
                pe.matmul(o[:, :], half, fk_sq[:, 2 * c:2 * c + 2, :].rearrange("p h t -> p (h t)"),
                          start=True, stop=True).then_inc(m_full, 1)
            gemm("scc0", T)

            def fox_scores(u, a, heads):
                o = l_open(u)
                n = P * (a + 1)
                for m, h in enumerate(heads):
                    q, k = (FQ, FQO)[h % 2][:, h // 2, P * a:P * (a + 1)], FK[:, h // 2, 0:n]
                    pe.matmul(o[:, n * m:n * (m + 1)], q, k, start=True, stop=False)
                    ins = pe.matmul(o[:, n * m:n * (m + 1)], sel(0, h), NCF[0:8, 0:n], start=False, stop=True)
                ins.then_inc(l_full, 1)
            pe.wait_ge(f_ready, 2)
            fox_scores("sa0", 0, range(4))
            fox_scores("sa1", 0, range(4, 8))
            fox_scores("sb0", 1, range(0, 2))
            fox_scores("sb1", 1, range(2, 4))
            gemm("scc1", T)
            fox_scores("sb2", 1, range(4, 6))
            fox_scores("sb3", 1, range(6, 8))
            gemm("scv0", T)
            gemm("scv1", T)

            def fox_turn(n):
                src = (SS0[:, :, :], SS1[:, :, 0:P], SS1[:, :, P:T])[n // 2]
                o = l_open(f"pt{n}")
                for h in range(4):
                    ins = pe.transpose(o[:, P * h:P * (h + 1)], src[:, 4 * (n % 2) + h, :], ident)
                ins.then_inc(l_full, 1)
            pe.wait_ge(p_ready, 1)
            fox_turn(0)
            fox_turn(1)
            gemm("scb0", T)
            pe.wait_ge(p_ready, 2)
            for n in range(2, 6):
                fox_turn(n)
            gemm("scb1", T)
            for e in (4, 5):
                pe.wait_ge(*l_done(f"pt{e}"))
            for n in range(2):
                o = l_open(f"yf{n}")
                for pair in range(2):
                    for odd in range(2):
                        h = 4 * n + 2 * pair + odd
                        r = slice(64 * odd, 64 * odd + 64)
                        pe.matmul(o[r, T * pair:T * (pair + 1)], FV[:, 0, 64 * h:64 * h + 64], PT0[:, h, :],
                                  start=True, stop=False)
                        ins = pe.matmul(o[r, T * pair + P:T * (pair + 1)], FV[:, 1, 64 * h:64 * h + 64],
                                        PT1[:, h, :], start=False, stop=True)
                ins.then_inc(l_full, 1)
            gemm("dz0", T)
            gemm("dz1", T)
            for g, name in ((2, "gb"), (1, "bb")):
                for n in range(2):
                    o = l_open(f"{name}{n}")
                    for h in range(2):
                        ins = pe.matmul(o[:, T * h:T * (h + 1)], sel(g, 2 * n + h), RB[32 * g:32 * g + 4, :],
                                        start=True, stop=True)
                    ins.then_inc(l_full, 1)
            gemm("gs0", T)

            def per_chunk(name, lhsT, rhs):
                for c in range(2):
                    o = l_open(f"{name}{c}")
                    for h in range(HEADS):
                        ins = pe.matmul(o[:, P * h:P * (h + 1)], lhsT(c, h), rhs(c, h), start=True, stop=True)
                    ins.then_inc(l_full, 1)

            def tok(a):
                return lambda c, h: a[:, h, P * c:P * (c + 1)]

            def mat(a):
                return lambda c, h: a[:, 4 * c + h, :]
            pe.wait_ge(*l_done("bb1"))
            per_chunk("an", tok(KB), tok(KC))
            per_chunk("at", tok(KC), tok(KB))
            gemm("gs1", T)
            per_chunk("qk", tok(KC), tok(QC))

            def turn(name, src):
                for c in range(2):
                    o = l_open(f"{name}{c}")
                    for h in range(HEADS):
                        ins = pe.transpose(o[:, P * h:P * (h + 1)], src[:, h, P * c:P * (c + 1)], ident)
                    ins.then_inc(l_full, 1)
            turn("vt", VC)
            gemm("gs2", T)
            turn("kt", KC)
            gemm("gs3", T)

            def branch(name, n):
                wh, wl = w_parts(name, 4)
                pe.wait_ge(y_hi, (1, 3, 4)[n])
                pe.wait_ge(*((y_lo, 1), l_done("yf1"), (y_lo, 2))[n])
                for nb in range(4):
                    if nb % 2 == 0:
                        o = g_open(name + "ab"[nb // 2])
                    for k in range(4):
                        ws = [x[:, k, P * nb:P * (nb + 1)] for x in (wh, wl)]
                        ins = product(o[:, T * (nb % 2):T * (nb % 2 + 1)], ws, (yhi[n][:, k, :], ylo[n][:, k, :]),
                                      k == 0, k == 3)
                    if nb % 2 == 1:
                        ins.then_inc(g_full, 1)

            fill = ["brs0", "brs1"] + [f"gf{c}" for c in range(4)] + ["brf0", "brf1"] + [f"gd{c}" for c in range(4)]

            def filler(name):
                if name[0] == "g":
                    gemm(name, T)
                else:
                    branch(name, "sf".index(name[2]))
            pe.wait_ge(x_init, 1)
            for lv in range(1, 7):
                if lv > 1:
                    pe.wait_ge(*l_done(f"xt{lv - 1}1"))
                per_chunk(f"y{lv}", mat(ANT), mat(XI))
                filler(fill[2 * lv - 2])
                pe.wait_ge(*l_done(f"y{lv}1"))
                per_chunk(f"xx{lv}", mat(XIT), mat(Y))
                per_chunk(f"xt{lv}", mat(Y), mat(XIT))
                filler(fill[2 * lv - 1])
            pe.wait_ge(*l_done("xt61"))
            per_chunk("us", mat(XIT), mat(VB))
            o = l_open("kc")
            for h in range(HEADS):
                ins = pe.matmul(o[:, P * h:P * (h + 1)], KBG[:, h, :], XIT[:, 4 + h, :], start=True, stop=True)
            ins.then_inc(l_full, 1)
            o = m_open("pT")
            pe.wait_ge(p_loaded, 16)
            for k in range(2):
                for t in range(2):
                    ins = pe.transpose(o[:, T * k + P * t:T * k + P * (t + 1)], PNAT[:, t, P * k:P * (k + 1)], ident)
            ins.then_inc(m_full, 1)
            o = l_open("s1")
            pe.wait_ge(*l_done("us1"))
            for h in range(HEADS):
                ins = pe.matmul(o[:, P * h:P * (h + 1)], KD[:, h, :], U1[:, h, :], start=True, stop=True)
            ins.then_inc(l_full, 1)
            wh, wl = w_parts("ple", 2)
            pe.wait_ge(p_hi, 1)
            pe.wait_ge(p_lo, 1)
            for nb in range(KT):
                if nb % 2 == 0:
                    o = g_open("ple" + "abcd"[nb // 2])
                for k in range(2):
                    ws = [x[:, k, P * nb:P * (nb + 1)] for x in (wh, wl)]
                    ins = product(o[:, T * (nb % 2):T * (nb % 2 + 1)], ws, (phi[:, k, :], plo[:, k, :]), k == 0,
                                  k == 1)
                if nb % 2 == 1:
                    ins.then_inc(g_full, 1)
                if nb == 1:
                    ow = l_open("w1")
                    pe.wait_ge(*l_done("s1"))
                    for h in range(HEADS):
                        ins = pe.matmul(ow[:, P * h:P * (h + 1)], KCT[:, h, :], S1[:, h, :], start=True, stop=True)
                    ins.then_inc(l_full, 1)
            pe.wait_ge(*l_done("w1"))
            for n in range(2):
                o = l_open(f"do{n}")
                for hh in range(2):
                    h = 2 * n + hh
                    t0, t1 = slice(T * hh, T * hh + P), slice(T * hh + P, T * hh + T)
                    pe.matmul(o[:, t0], U1[:, h, :], QKT[:, h, :], start=True, stop=True)
                    pe.matmul(o[:, t1], S1[:, h, :], QD[:, h, P:T], start=True, stop=False)
                    ins = pe.matmul(o[:, t1], U1[:, 4 + h, :], QKT[:, 4 + h, :], start=False, stop=True)
                ins.then_inc(l_full, 1)
            for n in range(2):
                o = m_open(f"on{2 + n}")
                pe.wait_ge(osq2, n + 1)
                pe.matmul(o[:, :], ones, DSQ[:, 2 * n:2 * n + 2, :].rearrange("p h t -> p (h t)"),
                          start=True, stop=True).then_inc(m_full, 1)
            branch("brd0", 2)
            branch("brd1", 2)
            for c in range(4):
                gemm(f"wp{c}", T, 16 if c == 0 else None)
            sum_squares("sum4", 16, T, SQ2)
            for j in range(FFT // 2):
                gemm(f"sg{j}", T, 20 if j == 0 else None)
                gemm(f"sa{j}", T)
                if j > 0:
                    down(j - 1, "s")
            down(FFT // 2 - 1, "s")
            sum_squares("sum5", 20, T, SQ2)
            for c in range(4):
                gemm(f"pg{c}", T, 24 if c == 0 else None)
            for t in range(2):
                for c in range(2):
                    pe.wait_ge(x_new, 12 + 2 * (c + 1))
                    for k in range(4):
                        ins = pe.transpose(bank[4 + 2 * t + c][:, P * k:P * (k + 1)],
                                           XT[:, 4 * c + k, P * t:P * (t + 1)], ident)
                    ins.then_inc(l_full, 1)

        @block.vector
        def _(dve):
            steps = [0]

            def mark(ins):
                steps[0] += 1
                ins.then_inc(dve_step, 1)
                return steps[0]

            def link(ins):
                dve.wait_ge(dve_step, mark(ins))

            def g_wait(u):
                dve.wait_ge(g_full, g_no(u) + 1)
                return g_bank(u)


            def modulation(a, ps, done, v=1):
                b = par("b_ada", 8, 8 * a).unsqueeze(2).broadcast_to([P, 8, v])
                dve.tensor_tensor(mod[:, 8 * a:8 * a + 8, 0:v], ps[:, 0:8 * v].rearrange("p (n v) -> p n v", v=v), b,
                                  ALU.add).then_inc(done, 1)

            def normalise(ht, g0, w, xs, scale, shift, m_u):
                dve.wait_ge(m_empty["act"], m_emptied(m_no(m_u))[1])
                link(dve.reciprocal(rstd[:, 0:w], std[:, 0:w]))
                for g in range(4):
                    scaled(ht, w, xs, scale, g)
                    if g > 0:
                        low_parts(ht, w, shift, g0, g - 1)
                low_parts(ht, w, shift, g0, 3)

            def scaled(ht, w, xs, scale, g):
                for k in (2 * g, 2 * g + 1):
                    for n in range(w // T):
                        ins = dve.scalar_tensor_tensor(out=ht[:, w * k + T * n:w * k + T * (n + 1)],
                                                       in0=xs[:, k, T * n:T * (n + 1)], scalar=scale(k, n),
                                                       in1=rstd[:, T * n:T * (n + 1)], op0=ALU.mult, op1=ALU.mult)
                ins.then_inc(h_f32, 1)

            def low_parts(ht, w, shift, g0, g):
                dve.wait_ge(h_hi, g0 + g + 1)
                if shift is None:
                    s = slice(2 * w * g, 2 * w * (g + 1))
                    ins = dve.tensor_tensor(hlo[:, s], ht[:, s], hhi[:, s].bitcast(F32), ALU.subtract)
                else:
                    for k in (2 * g, 2 * g + 1):
                        for n in range(w // T):
                            s = slice(w * k + T * n, w * k + T * (n + 1))
                            ins = dve.scalar_tensor_tensor(out=hlo[:, s], in0=ht[:, s], scalar=shift(k, n),
                                                           in1=hhi[:, s].bitcast(F32), op0=ALU.add, op1=ALU.subtract)
                ins.then_inc(h_lo, 1)

            def weighted(c):
                n = ada_place[c]
                dve.wait_ge(raw_loaded[n % RING], 16 * (n // RING + 1))
                w = raw[:, n % RING, :].rearrange("p (k n) -> p k n", k=KT)
                marks = {}
                for k in range(KT):
                    for v in range(2):
                        a, dst = silu_c[:, k, v:v + 1], acc_dve[:, k % 2, v, :]
                        if k < 2:
                            if c >= 2 and k == 0:
                                dve.wait_ge(sum_dve, c - 1 + v)
                            ins = dve.tensor_scalar(dst, w[:, k, :], a, None, ALU.mult)
                        else:
                            dve.wait_ge(dve_step, marks[k - 2, v])
                            ins = dve.scalar_tensor_tensor(out=dst, in0=w[:, k, :], scalar=a, in1=dst,
                                                           op0=ALU.mult, op1=ALU.add)
                        marks[k, v] = mark(ins)
                for v in range(2):
                    dve.wait_ge(dve_step, marks[KT - 1, v])
                    dve.tensor_tensor(acc_dve[:, 0, v, :], acc_dve[:, 0, v, :], acc_dve[:, 1, v, :], ALU.add
                                      ).then_inc(ada_dve, 1)

            dve.wait_ge(c_ready, 1)
            for c in range(8):
                if c not in ADA_PE:
                    weighted(c)
                if c == 4:
                    dve.wait_ge(par_T, 1)
                    dve.tensor_copy(params[:, 0:512], bank[6][:, :]).then_inc(par_ready, 1)
                    dve.tensor_copy(params[:, 512:N_ROWS], bank[7][:, 0:N_ROWS - 512]).then_inc(par_ready, 1)
                    dve.wait_ge(m_empty["act"], m_emptied(m_no("sum0"))[1])
                    dve.reciprocal(rstd, std)
                    dve.wait_ge(par_ready, 2)
                    dve.wait_ge(sum_pe, 2)
                    dve.wait_ge(sum_dve, 4)
                    modulation(1, bank[4], mod_ready, 2)
                    dve.wait_ge(mod_ready, 1)
                    link(dve.scalar_tensor_tensor(out=scale1, in0=mod[:, 8:16, :], scalar=1.0,
                                                  in1=par("norm_mix", 8).unsqueeze(2).broadcast_to([P, 8, 2]),
                                                  op0=ALU.add, op1=ALU.mult))
                if c >= 4:
                    scaled(HT, 512, XT, lambda k, n: scale1[:, k, n:n + 1], c - 4)
            dve.wait_ge(sum_pe, 4)
            dve.wait_ge(sum_dve, 8)
            modulation(0, bank[5], mod_ready, 2)
            dve.wait_ge(mod_ready, 2)
            for g in range(4):
                low_parts(HT, 512, lambda k, n: mod[:, k, n:n + 1], 0, g)
                if g == 0:
                    split_lo(dve, 0)
            for g in range(1, RING):
                split_lo(dve, g)
            for name in ("ff0", "ff1", "fb0", "fb1"):
                split_lo(dve, G[name] + RING)

            def ctx_decay(d):
                f, k = ((FFc, KFc), (FBc, KBc))[d]
                dve.wait_ge(g_empty["act"], g_emptied(g_no(("ff1b", "fb1b")[d]))[1])
                link(dve.memset(E[:, :, T - 1:T] if d == 0 else E[:, :, 0:1], 1.0))
                for h in range(HEADS):
                    if d == 0:
                        ins = dve.tensor_tensor_scan(E[:, h, 0:T - 1][:, ::-1], f[:, h, 1:T][:, ::-1],
                                                     ones_t[:, 0:T - 1], 1.0, ALU.mult, ALU.mult)
                    else:
                        ins = dve.tensor_tensor_scan(E[:, h, 1:T], f[:, h, 0:T - 1], ones_t[:, 0:T - 1], 1.0,
                                                     ALU.mult, ALU.mult)
                link(ins)
                dve.tensor_tensor(k[:, :, :], k[:, :, :], E[:, :, :], ALU.mult).then_inc(ctx_k, 1)
                dve.wait_ge(ctx_k, d + 1)

            def values(c):
                for n in range(2):
                    u = f"v{c}{'ab'[n]}"
                    dve.tensor_copy(VTOK[:, 2 * n:2 * n + 2, T * c:T * (c + 1)],
                                    g_wait(u)[:, :].rearrange("p (a v) -> p a v", a=2)).then_inc(g_empty["dve"], 1)
            ctx_decay(0)
            dve.wait_ge(masks_ready, 1)
            values(0)
            split_lo(dve, G["v0"] + RING)
            ctx_decay(1)
            values(1)
            modulation(2, g_wait("A2"), g_empty["dve"])
            split_lo(dve, G["v1"] + RING)
            dve.tensor_tensor(KSUM, KFx, KBx, ALU.add)
            dve.wait_ge(g_empty["act"], g_emptied(g_no("q0"))[1])
            link(dve.tensor_scalar(Q[:, 0:2, :], Q[:, 0:2, :], P ** -0.5, None, ALU.mult))
            dve.tensor_tensor(QPf[:, 0:2, :], Q[:, 0:2, :], FFx[:, 0:2, :], ALU.mult)
            dve.tensor_tensor(QSb[:, 0:2, :], Q[:, 0:2, :], FBx[:, 0:2, :], ALU.mult)
            split_lo(dve, G["q0"] + RING)
            dve.wait_ge(g_empty["act"], g_emptied(g_no("q1"))[1])
            link(dve.tensor_scalar(Q[:, 2:4, :], Q[:, 2:4, :], P ** -0.5, None, ALU.mult))
            dve.tensor_tensor(QPf[:, 2:4, :], Q[:, 2:4, :], FFx[:, 2:4, :], ALU.mult)
            dve.tensor_tensor(QSb[:, 2:4, :], Q[:, 2:4, :], FBx[:, 2:4, :], ALU.mult).then_inc(lv_upd, 1)
            split_lo(dve, G["q1"] + RING)

            def level(s):
                b = 1 << (s - 1)
                tf, tb = (t.rearrange("p h (n two) -> p (h n) two", two=2) for t in tot[b])

                def half(a, side):
                    return a.rearrange("p h (n two b) -> p (h n) two b", two=2, b=b)[:, :, side, :]

                def wide(t, side):
                    return t[:, :, side:side + 1].broadcast_to([P, HEADS * T // (2 * b), b])
                dve.wait_ge(lv_mm, s + 1)
                dve.wait_ge(lv_upd, s)
                dve.tensor_tensor(half(QPf, 1), half(QPf, 1), wide(tf, 0), ALU.mult)
                ins = dve.tensor_tensor(half(QSb, 0), half(QSb, 0), wide(tb, 1), ALU.mult)
                if s < 8:
                    dve.tensor_tensor(half(KFx, 0), half(KFx, 0), wide(tf, 1), ALU.mult)
                    dve.tensor_tensor(half(KBx, 1), half(KBx, 1), wide(tb, 0), ALU.mult)
                    for t, nxt in ((tf, tot[2 * b][0]), (tb, tot[2 * b][1])):
                        ins = dve.tensor_tensor(nxt.rearrange("p h n -> p (h n)").unsqueeze(2), t[:, :, 0:1],
                                                t[:, :, 1:2], ALU.mult)
                ins.then_inc(lv_upd, 1)
                if s == 8:
                    return
                if s == 1:
                    dve.wait_ge(lv_copied, 1)
                for d in range(2):
                    if d > 0:
                        dve.wait_ge(dve_step, kept[-1])
                    for t in range(2):
                        src = bank[4 + 2 * t + d][:, :].rearrange("p (h t) -> p h t", h=HEADS)
                        m = masks[:, s - 1, d, :].unsqueeze(1).broadcast_to([P, HEADS, P])
                        ins = dve.copy_predicated(S[t], m, src)
                        if d == 0 and t == 1:
                            kept.append(mark(ins))
                ins.then_inc(lv_empty, 1)
                dve.wait_ge(lv_empty, s)

            kept = []
            level(1)
            split_lo(dve, G["mv0"] + RING)
            level(2)
            dve.wait_ge(g_empty["act"], g_emptied(g_no("mv1"))[1])
            for t in range(2):
                for h in range(HEADS):
                    ins = dve.bn_stats(ln_stats[:, 4 * t + h, :], MV[:, t, P * h:P * (h + 1)])
            link(ins)
            for n in range(8):
                ins = dve.bn_aggr(ln_mv[:, n, :], ln_stats[:, n, :])
            ins.then_inc(sg_stats, 1)
            split_lo(dve, G["mv1"] + RING)
            level(3)
            modulation(3, g_wait("A3"), g_empty["dve"])
            split_lo(dve, G["mu0"] + RING)
            dve.wait_ge(sg_std, 1)
            link(dve.reciprocal(ln_rstd, ln_rstd))
            for t in range(2):
                for h in range(HEADS):
                    n = 4 * t + h
                    ins = dve.tensor_scalar(MV[:, t, P * h:P * (h + 1)], MV[:, t, P * h:P * (h + 1)],
                                            ln_mv[:, n, 0:1], ln_rstd[:, n:n + 1], ALU.subtract, ALU.mult)
            link(ins)
            level(4)
            dve.wait_ge(sgu_loaded, 64)
            link(dve.tensor_tensor(MV, MV, sgu_g.unsqueeze(1).broadcast_to([P, 2, 512]), ALU.mult))
            level(5)
            dve.tensor_tensor(MV, MV, sgu_b.unsqueeze(1).broadcast_to([P, 2, 512]), ALU.add).then_inc(vn_ready, 1)
            level(6)
            modulation(4, g_wait("A4"), g_empty["dve"])
            level(7)
            level(8)
            for n in range(2):
                dve.wait_ge(m_full, m_no(f"z{n}") + 1)
                z = m_bank(f"z{n}")[:, :].rearrange("p (h t) -> p h t", h=2)
                o = OM[:, 4 + 2 * n:6 + 2 * n, :]
                for h in range(2):
                    bs = bs_row[:, P * (2 * n + h):P * (2 * n + h + 1)].unsqueeze(1).broadcast_to([P, 2, P])
                    ins = dve.tensor_tensor(o[:, h, :].rearrange("p (a t) -> p a t", a=2),
                                            z[:, h, :].rearrange("p (a t) -> p a t", a=2), bs, ALU.add)
                ins.then_inc(m_empty["dve"], 1)
                dve.wait_ge(m_empty["dve"], n + 1)
                dve.wait_ge(g_empty["act"], g_emptied(g_no("mu1"))[1])
                link(dve.tensor_tensor(o, o, U[:, 2 * n:2 * n + 2, :], ALU.mult))
            for g in range(G["wo0"], G["wo0"] + RING):
                split_lo(dve, g)
            dve.wait_ge(g_empty["dve"], g_emptied(g_no("A4"))[1])
            link(dve.scalar_tensor_tensor(out=scale2, in0=mod[:, 32:40, 0], scalar=1.0, in1=par("norm_ffn", 8),
                                          op0=ALU.add, op1=ALU.mult))
            dve.wait_ge(g_empty["act"], g_emptied(g_no("gt1"))[1])
            for n in range(2):
                s = slice(2 * n, 2 * n + 2)
                dve.wait_ge(m_empty["act"], m_emptied(m_no(f"on{n}"))[1])
                link(dve.reciprocal(hrstd[:, s, :], hstd[:, s, :]))
                link(dve.tensor_tensor(OM[:, s, :], OM[:, s, :], hrstd[:, s, :], ALU.mult))
                for h in (2 * n, 2 * n + 1):
                    ins = dve.scalar_tensor_tensor(out=OM[:, h, :], in0=OM[:, h, :], scalar=par("hg_norm", k=h),
                                                   in1=GT[:, h, :], op0=ALU.mult, op1=ALU.mult)
                ins.then_inc(h_f32, 1)
            def lows(g0, src, w):
                for g in range(4):
                    dve.wait_ge(h_hi, g0 + g + 1)
                    s = slice(2 * w * g, 2 * w * (g + 1))
                    dve.tensor_tensor(hlo[:, s], src[:, s], hhi[:, s].bitcast(F32), ALU.subtract).then_inc(h_lo, 1)
            lows(4, OM.rearrange("p k t -> p (k t)"), T)

            def residual(nb, ps, gate):
                return dve.scalar_tensor_tensor(out=XT[:, nb, 0:T], in0=ps, scalar=mod[:, gate + nb, 0:1],
                                                in1=XT[:, nb, 0:T], op0=ALU.mult, op1=ALU.add)
            for c in range(4):
                ps = g_wait(f"wo{c}")
                for h in range(2):
                    ins = residual(2 * c + h, ps[:, T * h:T * (h + 1)], 16)
                ins.then_inc(g_empty["dve"], 1)
                split_lo(dve, G[f"wo{c}"] + RING)
            normalise(HT[:, 0:KT * T], 8, T, XT[:, :, 0:T], lambda k, n: scale2[:, k:k + 1],
                      lambda k, n: mod[:, 24 + k, 0:1], "sum1")
            for j in range(FFT // 2):
                b = j % 2
                dve.wait_ge(g_empty["act"], g_emptied(g_no(f"fg{j}"))[1])
                last = [None, None]
                for tap in range(9):
                    if tap == 4:
                        continue
                    for t in range(2):
                        if last[t]:
                            dve.wait_ge(dve_step, last[t])
                        dy, dx = tap // 3, tap % 3
                        a = acc[:, b, t, :].rearrange("p (r c) -> p r c", r=4)
                        ins = dve.scalar_tensor_tensor(out=a, in0=pad[:, b, t, dy:dy + 4, dx:dx + 64],
                                                       scalar=par("conv_w", k=FFT * tap + 2 * j + t), in1=a,
                                                       op0=ALU.mult, op1=ALU.add)
                        if tap < 8:
                            last[t] = mark(ins)
                    if tap == 3 and G[f"fg{j}"] + RING < N_SPLIT:
                        split_lo(dve, G[f"fg{j}"] + RING)
                ins.then_inc(conv_out, 1)
                if G[f"fa{j}"] + RING < N_SPLIT:
                    split_lo(dve, G[f"fa{j}"] + RING)
                dve.wait_ge(gelu_out, j + 1)
                if j >= 2:
                    dve.wait_ge(u_hi, j - 1)
                ps = g_wait(f"fa{j}")
                dve.tensor_tensor(uf[:, b, :, :], ps[:, :].rearrange("p (j t) -> p j t", j=2), gel[:, b, :, :],
                                  ALU.mult).then_inc(g_empty["dve"], 1)
                if j > 0 and G[f"fd{j - 1}"] + RING < N_SPLIT:
                    split_lo(dve, G[f"fd{j - 1}"] + RING)
                dve.wait_ge(u_hi, j + 1)
                if j >= 2:
                    dve.wait_ge(down_used, j - 1)
                dve.tensor_tensor(ulo[:, b, :, :], uf[:, b, :, :], uhi[:, b, :, :].bitcast(F32), ALU.subtract
                                  ).then_inc(u_lo, 1)
                if j == 5:
                    modulation(5, g_wait("A5"), g_empty["dve"])
            dve.wait_ge(down_used, FFT // 2)
            for c in range(4):
                for h in range(2):
                    ins = residual(2 * c + h, bank[4 + c][:, T * h:T * (h + 1)], 40)
                ins.then_inc(x_new, 1)
            def adv(name):
                if G[name] + RING < N_SPLIT:
                    split_lo(dve, G[name] + RING)

            def l_wait(u):
                dve.wait_ge(l_full, l_no(u) + 1)
                return l_bank(u)

            def two(ps):
                return ps[:, :].rearrange("p (j t) -> p j t", j=2)

            def four(ps):
                return ps[:, :].rearrange("p (j t) -> p j t", j=4)
            adv("fd10")
            dve.wait_ge(*m_done("sum2"))
            dve.wait_ge(x_new, 4)
            link(dve.reciprocal(rstd[:, 0:T], std[:, 0:T]))
            done = []
            for g in range(4):
                k = slice(2 * g, 2 * g + 2)
                done.append(mark(dve.tensor_tensor(XT[:, k, 0:T], XT[:, k, 0:T],
                                                   rstd[:, 0:T].unsqueeze(1).broadcast_to([P, 2, T]), ALU.mult)))
            for g in range(4):
                dve.wait_ge(dve_step, done[g])
                for k in (2 * g, 2 * g + 1):
                    ins = dve.tensor_scalar(XT[:, k, 0:T], XT[:, k, 0:T], par("norm_final", k=k), None, ALU.mult)
                ins.then_inc(x_new, 1)
            dve.wait_ge(x_new, 8)
            normalise(HT2, 12, T, XT[:, :, 0:T], lambda k, n: par("g_mix", k=k), None, "sum3")

            def conv_dn(u, dst, tap):
                dve.wait_ge(acc_start, dn_no[u] + 1)
                ps = g_wait(u)
                last = [None, None]
                for d in (1, 2, 3):
                    for t in range(2):
                        if last[t]:
                            dve.wait_ge(dve_step, last[t])
                        ins = dve.scalar_tensor_tensor(
                            out=dst[:, t, d:T], in0=ps[:, T * t:T * (t + 1) - d],
                            scalar=par("dn_conv", k=12 * (3 - d) + tap + t), in1=dst[:, t, d:T], op0=ALU.mult,
                            op1=ALU.add)
                        if d < 3:
                            last[t] = mark(ins)
                ins.then_inc(g_empty["dve"], 1)
                adv(u)
            dn = [(f"d{n}{c}", (QC, KC, VC)["qkv".index(n)][:, 2 * c:2 * c + 2, :], 4 * "qkv".index(n) + 2 * c)
                  for n in "qkv" for c in range(2)]
            dn_no = {d[0]: n for n, d in enumerate(dn)}
            conv_dn(*dn[0])
            dve.wait_ge(m_full, m_no("sm") + 1)
            dve.wait_ge(wsm_zero, 3)
            dve.tensor_scalar(SMY[0:96, :], m_bank("sm")[0:96, 0:T], sm_bias[0:96, :], sm_sign[0:96, :], ALU.add,
                              ALU.mult).then_inc(m_empty["dve"], 1)
            conv_dn(*dn[1])
            dve.wait_ge(sm_ln, 1)
            dve.wait_ge(coef_ready, 1)
            link(dve.scalar_tensor_tensor(out=SMA[0:96, :], in0=SMY[0:96, :], scalar=0.0, in1=SMA[0:96, :],
                                          op0=ALU.max, op1=ALU.add))
            link(dve.tensor_scalar(SMA[0:96, :], SMA[0:96, :], sm_coef[0:96, :], None, ALU.mult))
            link(dve.tensor_tensor_scan(RB[0:8, :], ones_t[0:8, :], SMA[0:8, :], 0.0, ALU.mult, ALU.add))
            dve.tensor_scalar(NCF[0:8, :], RB[0:8, :], -1.0, None, ALU.mult)
            for c in range(2):
                s_ = slice(P * c, P * (c + 1))
                ins = dve.tensor_tensor_scan(RB[64:68, s_], ones_t[64:68, s_], SMA[64:68, s_], 0.0, ALU.mult, ALU.add)
            ins.then_inc(rb_ready, 1)
            conv_dn(*dn[2])
            conv_dn(*dn[3])
            dve.wait_ge(m_full, m_no("colT") + 1)
            dve.tensor_copy(COLS[:, :, :], m_bank("colT")[:, 0:192].rearrange("p (a r) -> p a r", a=2)
                            ).then_inc(m_empty["dve"], 1)
            conv_dn(*dn[4])

            def unit_norm(dst, std_, u, gain, sem_, odd=None):
                dve.wait_ge(*m_done(u))
                link(dve.reciprocal(std_, std_))
                if odd is not None:
                    link(dve.scalar_tensor_tensor(out=odd, in0=dst, scalar=fgain[:, 1:2], in1=std_, op0=ALU.mult,
                                                  op1=ALU.mult))
                dve.scalar_tensor_tensor(out=dst, in0=dst, scalar=gain, in1=std_, op0=ALU.mult, op1=ALU.mult
                                         ).then_inc(sem_, 1)
            dve.wait_ge(silu_done, 2)
            unit_norm(QC, lq_std, "lq1", P ** -0.5, qk_ready)
            conv_dn(*dn[5])
            dve.wait_ge(silu_done, 4)
            unit_norm(KC, lk_std, "lk1", 1.0, qk_ready)
            for u in ("fq0", "fq1", "fk0", "fk1"):
                adv(u)

            def fox_values(c):
                u = f"fv{c}"
                dve.tensor_copy(FV[:, :, T * c:T * (c + 1)], two(g_wait(u))).then_inc(g_empty["dve"], 1)
                adv(u)
            fox_values(0)
            dve.wait_ge(b2_loaded, 80)
            for n in range(2):
                ins = dve.tensor_scalar(fgain[:, n:n + 1], half[:, 127 * n:127 * n + 1], par("fox_gain", k=0),
                                        64 ** -0.5, ALU.mult, ALU.mult)
            link(ins)
            dve.wait_ge(*g_done("fq1"))
            unit_norm(FQ, fq_std, "sfq1", fgain[:, 0:1], f_ready, FQO)
            fox_values(1)
            dve.wait_ge(*g_done("fk1"))
            unit_norm(FK, fk_std, "sfk1", par("fox_gain", k=1), f_ready)
            adv("scc0")

            def fox_max(u, a, heads):
                ps = l_wait(u)
                n = P * (a + 1)
                for m, h in enumerate(heads):
                    ins = dve.tensor_tensor_reduce((SS0, SS1)[a][:, h, :], ps[:, n * m:n * (m + 1)],
                                                   zlate[:, T - n:T], 1.0, -3e38, ALU.add, ALU.max,
                                                   fmax[:, a, h:h + 1])
                ins.then_inc(l_empty["dve"], 1)

            def fox_bias(a):
                cum = COLS[:, a, 0:8]
                link(dve.tensor_tensor(fmax[:, a, :], fmax[:, a, :], cum, ALU.add))
                dve.tensor_tensor(fneg[:, a, :], cum, fmax[:, a, :], ALU.subtract).then_inc(ss_ready, 1)
            dve.wait_ge(b2_loaded, 80)
            fox_max("sa0", 0, range(4))
            fox_max("sa1", 0, range(4, 8))
            dve.wait_ge(*l_done("sa1"))
            fox_bias(0)
            fox_max("sb0", 1, range(0, 2))
            fox_max("sb1", 1, range(2, 4))
            adv("scc1")
            fox_max("sb2", 1, range(4, 6))
            fox_max("sb3", 1, range(6, 8))
            dve.wait_ge(*l_done("sb3"))
            fox_bias(1)

            def fox_prob(a, ss):
                dve.wait_ge(ss_exp, 8 * (a + 1))
                link(dve.reciprocal(frec[:, a, :], fsum[:, a, :]))
                dve.tensor_tensor(ss, ss, frec[:, a, :].unsqueeze(2).broadcast_to([P, 8, P * (a + 1)]), ALU.mult
                                  ).then_inc(p_ready, 1)
            fox_prob(0, SS0)

            def sc_product(c):
                s_ = slice(2 * c, 2 * c + 2)
                dve.wait_ge(*g_done(f"scc{c}"))
                dve.tensor_tensor(CS[:, s_, :], two(g_wait(f"scv{c}")), CS[:, s_, :], ALU.mult
                                  ).then_inc(g_empty["dve"], 1)
                adv(f"scv{c}")
            sc_product(0)
            sc_product(1)
            fox_prob(1, SS1)

            def p_copy(n):
                dst = (None, PT0[:, 4:8, 0:P], None, PT0[:, 4:8, P:T], None, PT1[:, 4:8, :])[n]
                dve.tensor_copy(dst, four(l_wait(f"pt{n}"))).then_inc(l_empty["dve"], 1)
            p_copy(1)
            adv("scb0")
            dve.wait_ge(*g_done("scv1"))
            last = [None] * HEADS
            for d in range(3):
                for t in range(HEADS):
                    w = par("sc_conv", k=4 * (2 - d) + t)
                    if d == 0:
                        last[t] = mark(dve.tensor_scalar(YSC[:, t, :], CS[:, t, :], w, None, ALU.mult))
                    else:
                        dve.wait_ge(dve_step, last[t])
                        last[t] = mark(dve.scalar_tensor_tensor(out=YSC[:, t, d:T], in0=CS[:, t, 0:T - d], scalar=w,
                                                                in1=YSC[:, t, d:T], op0=ALU.mult, op1=ALU.add))
            p_copy(3)
            p_copy(5)
            adv("scb1")
            dve.wait_ge(*g_done("scb1"))
            dve.wait_ge(dve_step, last[3])
            dve.tensor_tensor(YSC, YSC, SCB, ALU.mult).then_inc(y_f32, 1)

            def y_split(n):
                dve.wait_ge(y_hi, (1, 3, 4)[n])
                dve.tensor_tensor(ylo[n], (YSC, None, ODN)[n], yhi[n].bitcast(F32), ALU.subtract).then_inc(y_lo, 1)
            y_split(0)
            for n in range(2):
                s_ = slice(2 * n, 2 * n + 2)
                ps = two(l_wait(f"yf{n}"))
                dve.wait_ge(y_hi, 2 + n)
                dve.tensor_tensor(ylo[1][:, s_, :], ps, yhi[1][:, s_, :].bitcast(F32), ALU.subtract
                                  ).then_inc(l_empty["dve"], 1)
            adv("dz0")
            adv("dz1")
            dve.wait_ge(*l_done("gb1"))
            for n, (d, keep) in enumerate(((DT, keep_up), (DL, keep_low))):
                for c in range(2):
                    for h in range(HEADS):
                        ins = dve.scalar_tensor_tensor(out=d[:, 4 * c + h, :], in0=GBS[:, h, P * c:P * (c + 1)],
                                                       scalar=COLS[:, c, 64 + h:65 + h], in1=keep,
                                                       op0=ALU.subtract, op1=ALU.add)
                ins.then_inc(d_raw, 1)
            for n in range(2):
                s_ = slice(2 * n, 2 * n + 2)
                dve.tensor_tensor(KB[:, s_, :], KC[:, s_, :], two(l_wait(f"bb{n}")), ALU.mult
                                  ).then_inc(l_empty["dve"], 1)
            dve.wait_ge(qd_exp, 1)
            dve.tensor_tensor(QD, QC, QD, ALU.mult)
            eye8 = ident.unsqueeze(1).broadcast_to([P, 8, P])
            dve.tensor_copy(XI, eye8)
            link(dve.tensor_copy(XIT, eye8))
            adv("gs0")
            dve.wait_ge(d_exp, 2)
            for name, dst, d in (("an", AN, DL), ("at", ANT, DT)):
                for c in range(2):
                    s_ = slice(4 * c, 4 * c + 4)
                    dve.scalar_tensor_tensor(out=dst[:, s_, :], in0=four(l_wait(f"{name}{c}")), scalar=-1.0,
                                             in1=d[:, s_, :], op0=ALU.mult, op1=ALU.mult).then_inc(l_empty["dve"], 1)
            adv("gs1")
            dve.wait_ge(*l_done("at1"))
            low, up = (masks[:, 0, n, :].unsqueeze(1).broadcast_to([P, 8, P]) for n in (1, 0))
            dve.copy_predicated(XI, low, AN)
            dve.copy_predicated(XIT, up, ANT).then_inc(x_init, 1)
            for c in range(2):
                s_ = slice(4 * c, 4 * c + 4)
                dve.tensor_tensor(QKT[:, s_, :], four(l_wait(f"qk{c}")), DT[:, s_, :], ALU.mult
                                  ).then_inc(l_empty["dve"], 1)
            for c in range(2):
                dve.tensor_tensor(VB[:, 4 * c:4 * c + 4, :], four(l_wait(f"vt{c}")),
                                  COLS[:, c, 32:36].unsqueeze(2).broadcast_to([P, HEADS, P]), ALU.mult
                                  ).then_inc(l_empty["dve"], 1)
            adv("gs2")
            dve.wait_ge(bg_ready, 1)
            link(dve.tensor_tensor(bgcol, bgcol, COLS[:, 1, 32:36], ALU.mult))
            dve.tensor_tensor(KD, four(l_wait("kt0")), DT[:, 0:4, P - 1:P].broadcast_to([P, HEADS, P]), ALU.mult
                              ).then_inc(l_empty["dve"], 1)
            dve.tensor_tensor(KBG, four(l_wait("kt1")), bgcol.unsqueeze(2).broadcast_to([P, HEADS, P]), ALU.mult
                              ).then_inc(l_empty["dve"], 1)
            adv("gs3")
            gated = slot(17).rearrange("p (b j t) -> p b j t", b=2, j=2)
            n_gated = [0]

            def gated_sum(name, n):
                for u in "ab":
                    k = 4 * int(name[3]) + 2 * "ab".index(u)
                    ps = two(g_wait(name + u))
                    if n == 0:
                        dve.tensor_tensor(XC[:, k:k + 2, :], ps, GATES[:, k:k + 2, :], ALU.mult
                                          ).then_inc(g_empty["dve"], 1)
                        continue
                    b = n_gated[0] % 2
                    n_gated[0] += 1
                    dve.tensor_tensor(gated[:, b], ps, GATES[:, k:k + 2, :], ALU.mult).then_inc(g_empty["dve"], 1)
                    dve.wait_ge(*g_done(name + u))
                    dve.tensor_tensor(XC[:, k:k + 2, :], XC[:, k:k + 2, :], gated[:, b], ALU.add
                                      ).then_inc(merged_f32, 1)
                adv(name)
            fill = ["brs0", "brs1"] + [f"gf{c}" for c in range(4)] + ["brf0", "brf1"] + [f"gd{c}" for c in range(4)]

            def filler(name):
                if name[0] == "g":
                    adv(name)
                    return
                n = "sfd".index(name[2])
                dve.wait_ge(*g_done(f"g{name[2]}3"))
                gated_sum(name, n)
            for lv in range(1, 7):
                filler(fill[2 * lv - 2])
                for name, dst, side in (("xx", XI, 1), ("xt", XIT, 0)):
                    for c in range(2):
                        m = masks[:, lv, side, :].unsqueeze(1).broadcast_to([P, HEADS, P])
                        dve.copy_predicated(dst[:, 4 * c:4 * c + 4, :], m, four(l_wait(f"{name}{lv}{c}"))
                                            ).then_inc(l_empty["dve"], 1)
                filler(fill[2 * lv - 1])
            dve.wait_ge(m_full, m_no("pT") + 1)
            dve.tensor_copy(PF, m_bank("pT")[:, :]).then_inc(m_empty["dve"], 1)
            dve.wait_ge(p_hi, 1)
            dve.tensor_tensor(plo, PF.rearrange("p (k t) -> p k t", t=T), phi.bitcast(F32), ALU.subtract
                              ).then_inc(p_lo, 1)
            dve.wait_ge(*l_done("us1"))
            dve.tensor_tensor(U1[:, 4:8, :], U1[:, 4:8, :], four(l_wait("w1")), ALU.subtract
                              ).then_inc(l_empty["dve"], 1)
            adv("ple")
            dve.wait_ge(*m_done("on3"))
            link(dve.reciprocal(dstd, dstd))
            link(dve.tensor_tensor(ODN, ODN, dstd, ALU.mult))
            dve.scalar_tensor_tensor(out=ODN, in0=ODN, scalar=par("dn_norm"), in1=ZS, op0=ALU.mult, op1=ALU.mult
                                     ).then_inc(y_f32, 2)
            y_split(2)
            for name in ("brd0", "brd1"):
                gated_sum(name, 2)
            for g in range(4):
                dve.wait_ge(h_hi, 16 + g + 1)
                dve.wait_ge(merged_f32, 5 + g)
                s_ = slice(512 * g, 512 * (g + 1))
                dve.tensor_tensor(hlo[:, s_].rearrange("p (k t) -> p k t", k=2), XC[:, 2 * g:2 * g + 2, :],
                                  hhi[:, s_].rearrange("p (k t) -> p k t", k=2).bitcast(F32), ALU.subtract
                                  ).then_inc(h_lo, 1)

            def add_x(nb, ps):
                return dve.tensor_tensor(XT[:, nb:nb + 2, 0:T], two(ps), XT[:, nb:nb + 2, 0:T], ALU.add)
            for c in range(4):
                add_x(2 * c, g_wait(f"wp{c}")).then_inc(g_empty["dve"], 1)
                adv(f"wp{c}")
            dve.wait_ge(*g_done("wp3"))
            normalise(HT2, 20, T, XT[:, :, 0:T], lambda k, n: par("g_ffn", k=k), None, "sum4")
            for j in range(FFT // 2):
                b = j % 2
                for n, w in enumerate("ga"):
                    ps = g_wait(f"s{w}{j}")
                    dve.wait_ge(acc2_start, 2 * j + n + 1)
                    last = [None, None]
                    for d in (1, 2):
                        for t in range(2):
                            if last[t]:
                                dve.wait_ge(dve_step, last[t])
                            ins = dve.scalar_tensor_tensor(
                                out=acc2[:, b, n, t, d:T], in0=ps[:, T * t:T * (t + 1) - d],
                                scalar=par("ffn_conv", k=2 * FFT * (2 - d) + FFT * n + 2 * j + t),
                                in1=acc2[:, b, n, t, d:T], op0=ALU.mult, op1=ALU.add)
                            if d == 1:
                                last[t] = mark(ins)
                    ins.then_inc(g_empty["dve"], 1)
                    adv(f"s{w}{j}")
                dve.wait_ge(silu2, j + 1)
                dve.wait_ge(*g_done(f"sa{j}"))
                if j >= 2:
                    dve.wait_ge(u_hi, FFT // 2 + j - 1)
                dve.tensor_tensor(uf[:, b, :, :], acc2[:, b, 0, :, :], acc2[:, b, 1, :, :], ALU.mult
                                  ).then_inc(u2_f32, 1)
                if j > 0:
                    adv(f"sd{j - 1}")
                dve.wait_ge(u_hi, FFT // 2 + j + 1)
                if j >= 2:
                    dve.wait_ge(down_used, FFT // 2 + j - 1)
                dve.tensor_tensor(ulo[:, b, :, :], uf[:, b, :, :], uhi[:, b, :, :].bitcast(F32), ALU.subtract
                                  ).then_inc(u_lo, 1)
            adv(f"sd{FFT // 2 - 1}")
            for c in range(4):
                add_x(2 * c, bank[4 + c]).then_inc(x_new, 1)
            dve.wait_ge(x_new, 12)
            normalise(HT2, 24, T, XT[:, :, 0:T], lambda k, n: par("g_ple", k=k), None, "sum5")
            for c in range(4):
                s_ = slice(2 * c, 2 * c + 2)
                adv(f"pg{c}")
                dve.wait_ge(*g_done(f"pg{c}"))
                link(dve.tensor_tensor(PG[:, s_, :], PG[:, s_, :], PLE[:, s_, :], ALU.mult))
                dve.tensor_tensor(XT[:, s_, 0:T], XT[:, s_, 0:T], PG[:, s_, :], ALU.add).then_inc(x_new, 1)
            for n in range(2):
                dve.wait_ge(l_full, len(l_units) + 2 * n + 2)
                dve.tensor_copy(OUTN[:, n, 512:1024], bank[5 + 2 * n][:, :]).then_inc(out_dve, 1)


_INS = ["x", "ctx", "w_ada", "w_in", "sgu_norm_g", "sgu_norm_b", "w_spatial", "b_spatial", "w_out", "w_up",
        "w_down", "p_2", "w_in_2", "w_branch_2", "w_o_2", "w_up_2", "w_down_2", "w_ple_gate_2", "w_ple_2"]


def kernel(**inputs):
    import numpy as _np
    import concourse.bacc as _bacc
    from concourse import mybir as _mybir
    from concourse.bass_utils import run_bass_kernel_spmd as _run

    nc = _bacc.Bacc("TRN2", target_bir_lowering=False, num_devices=1)
    arrays, args = {}, {}
    laid = dict(zip(("const_f", "const_m", "const_s"), host_constants()), **host_layout(inputs))
    for name in _INS + list(laid):
        a = _np.ascontiguousarray(laid[name] if name in laid else inputs[name])
        arrays[f"in_{name}_dram"] = a
        args[name] = nc.dram_tensor(f"in_{name}_dram", a.shape, _mybir.dt.from_np(a.dtype),
                                    kind="ExternalInput").ap()
    out = nc.dram_tensor("out_0_dram", (1, T, D), _mybir.dt.float32, kind="ExternalOutput").ap()
    build(nc, args, out.rearrange("b t d -> (b t) d"))
    r = _run(nc, [arrays], core_ids=[0])
    return r.results[0]["out_0_dram"]
```

```python
from contextlib import ExitStack

import numpy as np

import concourse.bass as bass
from concourse import mybir

ALU = mybir.AluOpType
ACT = mybir.ActivationFunctionType
AX_X = mybir.AxisListType.X
F32 = mybir.dt.float32
F32R = mybir.dt.float32r
U8 = mybir.dt.uint8

P = 128
D = 1024
T = 256
KT = D // P
HEADS = 4
FFT = 2816 // P
EPS = 1e-6
NEG = -1e30
CHUNK = 2048
RING = 3

ROWS = {}
N_ROWS = 0
for _name, _n in (("c", 8), ("c_ctx", 8), ("b_ada", 48), ("norm_mix", 8), ("norm_ffn", 8), ("norm_final", 8),
                  ("hg_norm", 4), ("conv_b", 22), ("sc_conv", 12), ("fox_gain", 2),
                  ("conv_w", 198), ("g_mix", 8), ("dn_conv", 48), ("g_ffn", 8), ("ffn_conv", 132),
                  ("g_ple", 8), ("dn_norm", 1), ("sm_bias", 1), ("sm_log", 1)):
    ROWS[_name] = N_ROWS
    N_ROWS += _n


def host_constants():
    i = np.arange(P)
    eye = np.eye(P, dtype=np.float32)
    ones = np.ones((P, T), np.float32)
    half = (i[:, None] // 64 == i[None, :] // 64).astype(np.float32)
    late = np.where(i[None, :] <= i[:, None], 0.0, NEG).astype(np.float32)
    keep_up = np.where(i[None, :] >= i[:, None], 0.0, NEG).astype(np.float32)
    keep_low = np.where(i[None, :] <= i[:, None], 0.0, -NEG).astype(np.float32)
    zeros = np.zeros((P, P), np.float32)
    cf = np.concatenate([eye, ones, half, zeros, late, keep_up, keep_low], axis=1)
    masks = np.zeros((P, 7, 2, P), np.float32)
    for lv in range(7):
        b = 1 << lv
        same = i[:, None] // (2 * b) == i[None, :] // (2 * b)
        left, right = (i // b) % 2 == 0, (i // b) % 2 == 1
        masks[:, lv, 0] = same & left[:, None] & right[None, :]
        masks[:, lv, 1] = same & right[:, None] & left[None, :]
    sel = np.zeros((96, 8, P), np.float32)
    for h in range(8):
        sel[[h, 32 + h, 64 + h], h] = 1.0
    return cf, masks.reshape(P, -1), sel.reshape(96, -1)


SMALL = ((0, 1536, 8), (32, 4616, 4), (64, 4620, 4))


def host_layout(x):
    zero = np.zeros((1, 1), x["x"].dtype)

    def spread(parts):
        row = np.repeat(zero, P, axis=1)
        for at, a in parts:
            row[0, at:at + a.size] = a.reshape(-1)
        return row
    table = [x[n].reshape(-1, P) for n in ("c", "c_ctx", "b_ada", "norm_mix", "norm_ffn", "norm_final", "hg_norm",
                                           "conv_b", "sc_conv_w_2")]
    table += [np.concatenate([x[n].reshape(1, -1)] * 2, axis=1) for n in ("fox_q_gain_2", "fox_k_gain_2")]
    table += [x[n].reshape(-1, P) for n in ("conv_w", "g_mix_2", "dn_conv_w_2", "g_ffn_2", "ffn_conv_w_2",
                                            "g_ple_2", "dn_norm_gain_2")]
    table += [spread([(0, x["b_fox_f_2"]), (64, x["dn_dt_bias_2"])]), spread([(64, x["dn_a_log_2"])])]
    table = np.concatenate(table + [np.repeat(np.repeat(zero, P, axis=1), 5 * P - N_ROWS, axis=0)], axis=0)
    w_small = np.repeat(np.repeat(zero, 96, axis=1), D, axis=0)
    for row, c0, n in SMALL:
        w_small[:, row:row + n] = x["w_in_2"][0][:, c0:c0 + n]
    return {"table": table, "w_small": w_small}


def build(nc, i, out):
    w_ada, w_in, w_out = i["w_ada"][0], i["w_in"][0], i["w_out"][0]
    w_up, w_down = i["w_up"][0], i["w_down"][0]

    def cols(w, c0, kt=KT, n=256):
        return w.rearrange("(k p) n -> p k n", p=P)[:, :, c0:c0 + n]

    def rows(w, r0, kt=2):
        return w.rearrange("(k p) n -> p k n", p=P)[:, r0:r0 + kt, :]

    CHUNKS = []
    G = {}

    def chunk(name, src, shape, raw=False):
        if not raw:
            G[name] = sum(not c[0] for c in CHUNKS)
        CHUNKS.append((raw, src, shape))

    def ada(chunks):
        for c in chunks:
            chunk(f"ada{c}", cols(w_ada, 256 * ADA_ORDER[c]), (KT, 256), raw=True)

    ADA_ORDER = [4, 5, 6, 7, 0, 1, 2, 3] + list(range(8, 24))
    ada(range(8))
    n_ada = 8
    for name, c0 in (("ff", 0), ("fb", 512), ("q", 1536), ("v", 1024), ("mv", 3072), ("mu", 2560), ("gt", 2048)):
        for c in range(2):
            chunk(f"{name}{c}", cols(w_in, c0 + 256 * c), (KT, 256))
            if n_ada < 20:
                ada([n_ada])
                n_ada += 1
    for c in range(4):
        chunk(f"wo{c}", cols(w_out, 256 * c), (KT, 256))

    def ffn_chunks(tag, up, down):
        for j in range(FFT // 2 + 2):
            if j < FFT // 2:
                chunk(f"{tag}g{j}", cols(up, (FFT * P if tag == "f" else 0) + 256 * j), (KT, 256))
                chunk(f"{tag}a{j}", cols(up, (0 if tag == "f" else FFT * P) + 256 * j), (KT, 256))
            if j > 1:
                chunk(f"{tag}d{j - 2}", rows(down, 2 * (j - 2)), (2, D))
            if tag == "f" and 2 <= j < 6:
                ada([18 + j])
    ffn_chunks("f", w_up, w_down)
    w_in2, w_branch = i["w_in_2"][0], i["w_branch_2"][0]
    FOX, SC, DN, DN_Z, GATE = 0, 1544, 3080, 4624, 5136
    for name, c0, n in (("dq", DN, 2), ("dk", DN + 512, 2), ("dv", DN + 1024, 2),
                        ("fq", FOX, 2), ("fk", FOX + 512, 2), ("fv", FOX + 1024, 2),
                        ("scc", SC + 512, 2), ("scv", SC + 1024, 2), ("scb", SC, 2), ("dz", DN_Z, 2)):
        for c in range(n):
            chunk(f"{name}{c}", cols(w_in2, c0 + 256 * c), (KT, 256))
    for name, n in (("s", 1), ("f", 0), ("d", 2)):
        for c in range(4):
            chunk(f"g{name}{c}", cols(w_in2, GATE + D * n + 256 * c), (KT, 256))
        for c in range(2):
            chunk(f"br{name}{c}", cols(w_branch[n], 512 * c, n=512), (4, 512))
    for c in range(4):
        chunk(f"wp{c}", cols(i["w_o_2"][0], 256 * c), (KT, 256))
    ffn_chunks("s", i["w_up_2"][0], i["w_down_2"][0])
    chunk("ple", rows(i["w_ple_2"][0], 0), (2, D))
    for c in range(4):
        chunk(f"pg{c}", cols(i["w_ple_gate_2"][0], 256 * c), (KT, 256))
    N_SPLIT = sum(not c[0] for c in CHUNKS)
    raw_of = []
    for n, (raw, _, _) in enumerate(CHUNKS):
        if not raw:
            raw_of.append(n)

    def ring(units, banks):
        names = [u for u, _ in units]
        owner = [o for _, o in units]

        def number(u):
            return names.index(u)

        def emptied(n):
            return owner[n], sum(o == owner[n] for o in owner[:n + 1])
        return number, emptied, banks

    g_units = [(f"xr{k}", "act") for k in range(4)] + [(f"xt{k}", "act") for k in range(KT)]
    g_units += [(f"{n}{c}{h}", "act") for n in ("ff", "fb") for c in range(2) for h in "ab"]
    g_units += [("q0", "act"), ("q1", "act"), ("A2", "dve")] + [(f"v{c}{h}", "dve") for c in range(2) for h in "ab"]
    g_units += [("mv0", "act"), ("mv1", "act"), ("mu0", "act"), ("A3", "dve"),
                ("mu1", "act"), ("gt0", "act"), ("gt1", "act"), ("A4", "dve")]
    g_units += [(f"wo{c}", "dve") for c in range(4)]
    for j in range(FFT // 2):
        g_units += [(f"fg{j}", "act"), (f"fa{j}", "dve")] + [("A5", "dve")] * (j == 7)
    g_units += [(f"{n}{c}", "dve") for n in ("dq", "dk", "dv") for c in range(2)]
    g_units += [(f"{n}{c}", "act") for n in ("fq", "fk") for c in range(2)]
    g_units += [(f"{n}{c}", o) for n, o in (("fv", "dve"), ("scc", "act"), ("scv", "dve"), ("scb", "act"),
                                            ("dz", "act")) for c in range(2)]
    for n in "sfd":
        g_units += [(f"g{n}{c}", "act") for c in range(4)]
        g_units += [(f"br{n}{c}{h}", "dve") for c in range(2) for h in "ab"]
    g_units += [(f"wp{c}", "dve") for c in range(4)]
    g_units += [(f"s{n}{j}", "dve") for j in range(FFT // 2) for n in "ga"]
    g_units += [(f"ple{c}", "act") for c in "abcd"] + [(f"pg{c}", "act") for c in range(4)]
    l_units = [(f"sa{n}", "dve") for n in range(2)] + [(f"sb{n}", "dve") for n in range(4)]
    l_units += [(f"pt{n}", ("act", "dve")[n % 2]) for n in range(6)] + [("yf0", "dve"), ("yf1", "dve")]
    l_units += [("gb0", "act"), ("gb1", "act"), ("bb0", "dve"), ("bb1", "dve")]
    l_units += [(f"{n}{c}", "dve") for n in ("an", "at", "qk", "vt", "kt") for c in range(2)]
    for lv in range(1, 7):
        l_units += [(f"y{lv}{c}", "act") for c in range(2)]
        l_units += [(f"{n}{lv}{c}", "dve") for n in ("xx", "xt") for c in range(2)]
    l_units += [("us0", "act"), ("us1", "act"), ("kc", "act"), ("s1", "act"), ("w1", "dve"), ("do0", "act"),
                ("do1", "act")]
    m_units = [(n, "act") for n in ("kfT0", "kfT1", "kbT0", "kbT1", "wsT", "hf", "hb")]
    m_units += [("z0", "dve"), ("z1", "dve"), ("oA", "act"), ("oB", "act"), ("on0", "act"), ("on1", "act"),
                ("sum1", "act"), ("sum2", "dve"), ("sum3", "dve"), ("sm", "dve"), ("colT", "dve")]
    m_units += [(n, "act") for n in ("lq0", "lq1", "lk0", "lk1", "sfq0", "sfq1", "sfk0", "sfk1")]
    m_units += [("pT", "dve"), ("on2", "act"), ("on3", "act"), ("sum4", "act"), ("sum5", "act")]

    with ExitStack() as ctx:
        def sb(name, shape, dt=F32):
            return ctx.enter_context(nc.sbuf_tensor(name, shape, dt))

        sems = {}

        def sem(name):
            sems[name] = ctx.enter_context(nc.semaphore(name))
            return sems[name]

        bank = [ctx.enter_context(nc.psum_tensor(f"bank{n}", [P, 512], F32)) for n in range(8)]
        raw = sb("raw", [P, RING, CHUNK])
        whi = sb("whi", [P, RING, CHUNK], F32R)
        wlo = sb("wlo", [P, RING, CHUNK], F32R)
        hhi = sb("hhi", [P, 4096], F32R)
        hlo = sb("hlo", [P, 4096], F32R)
        XT = sb("XT", [P, KT, 512])
        params = sb("params", [P, 5 * P])
        cf = sb("cf", [P, P + T])
        ident, ones, ones_t = cf[:, 0:P], cf[:, P:2 * P], cf[:, P:P + T]
        masks = sb("masks", [P, 7, 2, P], U8)
        small = sb("small", [P, 224])
        arena = sb("arena", [P, 20, 1024])

        def slot(s, n=1, off=0, size=None):
            flat = arena[:, s:s + n, :].rearrange("p a b -> p (a b)")
            return flat[:, off:off + size] if size else flat

        def par(name, n=None, k=0):
            r = ROWS[name] + k
            return params[:, r:r + (n or 1)]

        mod = sb("mod", [P, 48, 2])
        silu_c = small[:, 0:16].rearrange("p (k v) -> p k v", v=2)
        eps = small[:, 16:17]
        scale1 = small[:, 32:48].rearrange("p (k v) -> p k v", v=2)
        scale2 = small[:, 48:56]
        ln_stats = small[:, 64:112].rearrange("p (u s) -> p u s", s=6)
        ln_mv = small[:, 112:128].rearrange("p (u s) -> p u s", s=2)
        ln_rstd = small[:, 128:136]

        def h4(s):
            return slot(s).rearrange("p (h t) -> p h t", h=HEADS)
        FFx, FBx, KFx, KBx, FFc, FBc, KFc, KBc = (h4(s) for s in range(8))
        Q, QPf, QSb, KSUM = (h4(s) for s in range(8, 12))
        xn, cn = (slot(s, 2).rearrange("p (a d) -> p a d", a=2) for s in (8, 10))
        SQ = slot(0, 4)
        HT = slot(4, 4)
        E = h4(12)
        SX = [slot(12, 1, 512 * n, 512).rearrange("p (h t) -> p h t", h=HEADS) for n in range(2)]
        VTOK = slot(13, 2).rearrange("p (a v) -> p a v", a=4)
        acc_dve = slot(15).rearrange("p (b n) -> p b n", b=4)
        acc_odd = slot(19, 1, 512, 512).rearrange("p (v n) -> p v n", v=2)
        row_buf = slot(17, 1, 512, 512).rearrange("p (b n) -> p b n", b=2)
        xh, ch = (slot(s, 2).rearrange("p (a d) -> p a d", a=2) for s in (2, 10))
        ss = small[:, 57:61]
        par_rows = slot(12, 1, 0, 640).rearrange("p (a f) -> p a f", a=5)
        c_rows = slot(12, 1, 640, P)
        acc_late = slot(12).rearrange("p (b n) -> p b n", b=4)
        masks_f = slot(13, 2, 0, 14 * P).rearrange("p (l s q) -> p l s q", l=7, s=2)
        HS = [slot(15, 1, 512 * n, 512).rearrange("p (h v) -> p h v", h=HEADS) for n in range(2)]
        KTOK = [slot(n).rearrange("p (a k) -> p a k", a=2) for n in (16, 12)]
        std, rstd = slot(16, 1, 0, 512), slot(16, 1, 512, 512)
        S = [slot(7, 1, 512 * n, 512).rearrange("p (h t) -> p h t", h=HEADS) for n in range(2)]
        MV = slot(4).rearrange("p (a v) -> p a v", a=2)
        U, GT = h4(5), h4(6)
        tot = {1: (FFx, FBx), 2: [slot(17, 1, 512 * n, 512).rearrange("p (h t) -> p h t", h=HEADS) for n in range(2)]}
        off = 0
        for b in (4, 8, 16, 32, 64, 128):
            n = HEADS * T // b
            tot[b] = [slot(d, 1, off, n).rearrange("p (h t) -> p h t", h=HEADS) for d in range(2)]
            off += n
        sgu_g, sgu_b = slot(18, 1, 0, 512), slot(18, 1, 512, 512)
        bs_row = slot(19, 1, 0, 512)
        wsT = slot(19, 1, 512, 512).rearrange("p (h q) -> p h q", h=HEADS)
        ws_nat = slot(17).rearrange("p (h q) -> p h q", q=P)[:, 0:4, :]
        OM = slot(2, 2).rearrange("p (k t) -> p k t", t=T)
        OSQ, hstd, hrstd = h4(16), h4(0), h4(1)

        GW = 66
        pad = slot(0, 2, 0, 4 * 6 * GW).rearrange("p (b j r c) -> p b j r c", b=2, j=2, r=6)
        acc = slot(2).rearrange("p (b j t) -> p b j t", b=2, j=2)
        gel = slot(3).rearrange("p (b j t) -> p b j t", b=2, j=2)
        uf = slot(10).rearrange("p (b j t) -> p b j t", b=2, j=2)
        uhi = hhi[:, 2048:3584].rearrange("p (b j t) -> p b j t", b=3, j=2)
        ulo = hlo[:, 2048:3584].rearrange("p (b j t) -> p b j t", b=3, j=2)

        XC = XT[:, :, T:2 * T]
        half = XT[:, 0, T:T + P]
        zlate = XT[:, 1, T:2 * T]
        keep_up, keep_low = XT[:, 2, T:T + P], XT[:, 2, T + P:2 * T]

        def sel(g, h):
            return XT[32 * g:32 * g + (8, 4, 4)[g], 3 + h // 2, T + P * (h % 2):T + P * (h % 2 + 1)]
        HT2 = slot(4, 2)
        QC, KC, VC, KB, QD, GBS = h4(0), h4(1), h4(2), h4(3), h4(5), h4(6)
        ZS = h4(4)
        DT, DL, AN, ANT, QKT, XI, XIT, Y = (slot(n).rearrange("p (m t) -> p m t", m=8)
                                            for n in (7, 8, 9, 10, 11, 12, 13, 8))
        VB, U1 = (slot(n).rearrange("p (m t) -> p m t", m=8) for n in (0, 9))
        KD, KBG, KCT, S1 = (slot(n, 1, o, 512).rearrange("p (h t) -> p h t", h=HEADS)
                            for n, o in ((3, 0), (3, 512), (6, 0), (6, 512)))
        ODN, DSQ, dstd = h4(2), h4(12), h4(8)
        lq_sq, lk_sq, lq_std, lk_std = h4(16), h4(15), h4(17), h4(18)
        FQ, FK, fq_sq, fk_sq, fq_std, fk_std = (h4(n) for n in (6, 7, 9, 10, 11, 12))
        FQO = h4(13)
        FV = slot(8).rearrange("p (a v) -> p a v", a=2)
        SS0 = slot(9).rearrange("p (h t) -> p h t", h=8)
        SS1 = slot(10, 2).rearrange("p (h t) -> p h t", h=8)
        PT0 = slot(12, 2).rearrange("p (h t) -> p h t", h=8)
        PT1 = slot(6).rearrange("p (h t) -> p h t", h=8)
        GATES = slot(14, 2).rearrange("p (k t) -> p k t", t=T)
        YSC, SCB, CS = h4(16), h4(17), h4(18)
        PNAT = slot(16, 1, 512, 512).rearrange("p (a f) -> p a f", a=2)
        PF = slot(16, 1, 0, 512)
        PLE = slot(18, 2).rearrange("p (k t) -> p k t", t=T)
        SMY, SMA, RB, NCF = (slot(19, 1, 256 * n, 256) for n in range(4))
        wsm = slot(18, 1, 0, KT * 96).rearrange("p (k c) -> p k c", c=96)
        COLS = sb("COLS", [P, 2, 96])
        fmax, fneg, fsum, frec = (small[:, 144 + 16 * n:160 + 16 * n].rearrange("p (a h) -> p a h", a=2)
                                  for n in range(4))
        bgcol = small[:, 208:212]
        fgain = small[:, 212:214]
        sm_bias, sm_log = par("sm_bias"), par("sm_log")
        sm_sign, sm_coef = small[:, 214:215], small[:, 215:216]
        yhi, ylo = ([h[:, 2048 + 1024 * (n % 2):3072 + 1024 * (n % 2)].rearrange("p (k t) -> p k t", t=T)
                     for n in range(3)] for h in (hhi, hlo))
        phi, plo = (h[:, 3584:4096].rearrange("p (k t) -> p k t", t=T) for h in (hhi, hlo))
        acc2 = slot(0, 2).rearrange("p (b w j t) -> p b w j t", b=2, w=2, j=2)
        OUTN = slot(4, 2).rearrange("p (a d) -> p a d", a=2)
        PG = slot(2, 2).rearrange("p (k t) -> p k t", t=T)
        SQ2 = slot(0, 2)
        nf2 = small[:, 72:80]
        gain2 = small[:, 64:72]
        weigh = slot(6).rearrange("p (k n) -> p k n", n=P)
        std2, rstd2 = slot(16, 1, 256, 256), slot(16, 1, 768, 256)

        raw_loaded = [sem(f"raw_loaded{n}") for n in range(RING)]
        par_loaded, const_loaded, x_loaded, sgu_loaded, stored = (
            sem(n) for n in ("par_loaded", "const_loaded", "x_loaded", "sgu_loaded", "stored"))
        w_hi, w_lo = sem("w_hi"), sem("w_lo")
        ada_dve, ada_pool, sum_dve, rows_full, rows_copied, rows_turned = (
            sem(n) for n in ("ada_dve", "ada_pool", "sum_dve", "rows_full", "rows_copied", "rows_turned"))
        ctx_loaded, ss_std, ss_rstd, xh_ready = (sem(n) for n in ("ctx_loaded", "ss_std", "ss_rstd", "xh_ready"))
        c_loaded = sem("c_loaded")
        act_sq = sem("act_sq")
        c_T, pool_link = sem("c_T"), sem("pool_link")
        g_full, m_full = sem("g_full"), sem("m_full")
        g_empty = {"act": sem("g_empty_act"), "dve": sem("g_empty_dve")}
        m_empty = {"act": sem("m_empty_act"), "dve": sem("m_empty_dve")}
        act_step, dve_step, pool_step = sem("act_step"), sem("dve_step"), sem("pool_step")
        par_T, par_ready, c_ready, mod_ready = (
            sem(n) for n in ("par_T", "par_ready", "c_ready", "mod_ready"))
        sq_ready, h_f32, h_hi, h_lo = (
            sem(n) for n in ("sq_ready", "h_f32", "h_hi", "h_lo"))
        ctx_k, lv_mm, lv_upd, lv_empty, lv_copied, sg_std, vn_ready, x_new = (
            sem(n) for n in ("ctx_k", "lv_mm", "lv_upd", "lv_empty", "lv_copied", "sg_std", "vn_ready", "x_new"))
        osq_ready, sg_stats, sgu_out = sem("osq_ready"), sem("sg_stats"), sem("sgu_out")
        pad_zero, conv_out, gelu_out, u_hi, u_lo, down_used = (
            sem(n) for n in ("pad_zero", "conv_out", "gelu_out", "u_hi", "u_lo", "down_used"))

        g_no, g_emptied, g_banks = ring(g_units, (0, 1))
        m_no, m_emptied, m_banks = ring(m_units, (2, 3))

        def g_bank(u):
            return bank[g_banks[g_no(u) % 2]]

        def m_bank(u):
            return bank[m_banks[m_no(u) % 2]]

        def multiplied(g):
            name = [n for n, k in G.items() if k == g][0]
            if name[0:2] in ("fd", "sd") and name[2:].isdigit():
                return down_used, int(name[2:]) + 1 + (FFT // 2 if name[0] == "s" else 0)
            unit = [n for n, _ in g_units if n == name or n[:-1] == name and n[-1] in "abcd"][-1]
            return g_full, g_no(unit) + 1

        l_no, l_emptied, _ = ring(l_units, range(4))
        l_full = sem("l_full")
        l_empty = {"act": sem("l_empty_act"), "dve": sem("l_empty_dve")}

        def l_bank(u):
            return bank[4 + l_no(u) % 4]

        def l_done(u):
            e, k = l_emptied(l_no(u))
            return l_empty[e], k

        def g_done(u):
            e, k = g_emptied(g_no(u))
            return g_empty[e], k

        def m_done(u):
            e, k = m_emptied(m_no(u))
            return m_empty[e], k
        b2_loaded, col_loaded, p_loaded, wsm_zero = (sem(n) for n in ("b2_loaded", "col_loaded", "p_loaded", "wsm_zero"))
        sm_ln, rb_ready, acc_start, silu_done, sq_done, f_ready, ss_ready, ss_exp, p_ready = (
            sem(n) for n in ("sm_ln", "rb_ready", "acc_start", "silu_done", "sq_done", "f_ready", "ss_ready",
                             "ss_exp", "p_ready"))
        var_ready, rstd_ready, weigh_ready = sem("var_ready"), sem("rstd_ready"), sem("weigh_ready")
        masks_loaded, masks_ready = sem("masks_loaded"), sem("masks_ready")
        qk_ready, d_raw, d_exp, bg_ready, coef_ready = (
            sem(n) for n in ("qk_ready", "d_raw", "d_exp", "bg_ready", "coef_ready"))
        x_init, y_f32, y_hi, y_lo, p_hi, p_lo, merged_f32, osq2, qd_exp = (
            sem(n) for n in ("x_init", "y_f32", "y_hi", "y_lo", "p_hi", "p_lo", "merged_f32", "osq2", "qd_exp"))
        out_act, out_dve, acc2_start, silu2 = (sem(n) for n in ("out_act", "out_dve", "acc2_start", "silu2"))
        u2_f32 = sem("u2_f32")
        block = ctx.enter_context(nc.Block())

        ADA_PE, ADA_DVE = (1, 3, 4, 6, 7), (0, 2, 5)

        @block.sync
        def _(sp):
            def mixing_loads():
                sp.dma_start(masks_f, i["const_m"].rearrange("p (l s q) -> p l s q", l=7, s=2)
                               ).then_inc(masks_loaded, 16)
                sp.dma_start(ws_nat, i["w_spatial"][0].rearrange("h p q -> p h q")).then_inc(sgu_loaded, 16)
                sp.dma_start(bs_row, i["b_spatial"].rearrange("l h p -> l (h p)").partition_broadcast(P)
                               ).then_inc(sgu_loaded, 16)
                sp.dma_start(sgu_g, i["sgu_norm_g"].partition_broadcast(P)).then_inc(sgu_loaded, 16)
                sp.dma_start(sgu_b, i["sgu_norm_b"].partition_broadcast(P)).then_inc(sgu_loaded, 16)

            sp.dma_start(ident, i["const_f"][:, 0:P]).then_inc(const_loaded, 16)
            sp.dma_start(c_rows[0:16, :], i["table"][0:16, :]).then_inc(c_loaded, 16)
            n_split = n_ada = 0
            last = []
            for n, (is_raw, src, (k, w)) in enumerate(CHUNKS):
                if n >= RING:
                    for wait in last[n - RING]:
                        sp.wait_ge(*wait)
                sp.dma_start(raw[:, n % RING, :].rearrange("p (k n) -> p k n", k=k), src
                             ).then_inc(raw_loaded[n % RING], 16)
                if n_split == 1 and not is_raw:
                    mixing_loads()
                if is_raw:
                    c = n_ada
                    if c in ADA_PE:
                        last.append([(rows_full, ADA_PE.index(c) + 1)])
                    elif c < 8:
                        last.append([(ada_dve, 2 * ADA_DVE.index(c) + 2)])
                    else:
                        last.append([(ada_pool, c - 7)])
                    n_ada += 1
                else:
                    n_split += 1
                    last.append([(w_lo, n_split)])
            o = out.rearrange("(a p) d -> p a d", p=P)
            for t in range(2):
                sp.wait_ge(out_act, t + 1)
                sp.wait_ge(out_dve, t + 1)
                sp.dma_start(o[:, t, :], OUTN[:, t, :]).then_inc(stored, 16)
            sp.wait_ge(stored, 32)

        ada_place = [n for n, c in enumerate(CHUNKS) if c[0]]

        @block.gpsimd
        def _(pool):
            pool.memset(eps, EPS).then_inc(pool_step, 1)
            pool.memset(ones_t, 1.0).then_inc(pool_step, 1)
            steps = [0]

            def link(ins):
                steps[0] += 1
                ins.then_inc(pool_link, 1)
                pool.wait_ge(pool_link, steps[0])

            def weighted(c, dst):
                n = ada_place[c]
                pool.wait_ge(raw_loaded[n % RING], 16 * (n // RING + 1))
                w = raw[:, n % RING, :].rearrange("p (k n) -> p k n", k=KT)
                link(pool.tensor_tensor(w, w, silu_c[:, :, 0:1].broadcast_to([P, KT, 256]), ALU.mult))
                link(pool.tensor_tensor(w[:, 0:4, :], w[:, 0:4, :], w[:, 4:8, :], ALU.add))
                link(pool.tensor_tensor(w[:, 0:2, :], w[:, 0:2, :], w[:, 2:4, :], ALU.add))
                pool.tensor_tensor(dst, w[:, 0, :], w[:, 1, :], ALU.add).then_inc(ada_pool, 1)
            for c in range(8, 20):
                if c >= 16:
                    pool.wait_ge(g_full, g_no(f"A{c // 4 - 2}") + 1)
                weighted(c, XC[:, c % 8, :])

            pool.wait_ge(m_full, m_no("sum1") + 1)
            pool.memset(slot(0, 2, 0, 4 * 6 * GW), 0.0).then_inc(pad_zero, 1)
            for dst, c0, n in ((half, 3, 1), (zlate, 4, 2), (keep_up, 6, 1), (keep_low, 7, 1)):
                pool.dma_start(dst, i["const_f"][:, P * c0:P * (c0 + n)]).then_inc(b2_loaded, 16)
            pool.dma_start(XT[0:96, 3:7, T:2 * T], i["const_s"].rearrange("r (k c) -> r k c", c=T)
                           ).then_inc(b2_loaded, 16)
            pool.memset(small[:, 214:218], 0.0)
            pool.memset(RB, 0.0).then_inc(wsm_zero, 1)
            pool.wait_ge(wsm_zero, 1)
            pool.memset(sm_sign, 1.0)
            pool.memset(sm_coef, -1.0).then_inc(wsm_zero, 1)
            pool.wait_ge(wsm_zero, 2)
            pool.memset(sm_sign[0:32, :], -1.0).then_inc(wsm_zero, 1)
            pool.dma_start(wsm, i["w_small"].rearrange("(k p) c -> p k c", p=P)).then_inc(col_loaded, 16)
            for c in range(20, 24):
                weighted(c, acc_late[:, c % 4, :])
            pool.wait_ge(y_lo, 1)
            pool.dma_start(PNAT, i["p_2"][0, 0].rearrange("(a p) f -> p a f", p=P)).then_inc(p_loaded, 16)

        def split_hi(act, g):
            n = raw_of[g]
            act.wait_ge(raw_loaded[n % RING], 16 * (n // RING + 1))
            if g >= RING:
                act.wait_ge(*multiplied(g - RING))
            act.activation(whi[:, g % RING, :], raw[:, n % RING, :], ACT.Copy).then_inc(w_hi, 1)

        def split_lo(dve, g):
            n = raw_of[g]
            dve.wait_ge(raw_loaded[n % RING], 16 * (n // RING + 1))
            dve.wait_ge(w_hi, g + 1)
            if g >= RING:
                dve.wait_ge(*multiplied(g - RING))
            dve.tensor_tensor(wlo[:, g % RING, :], raw[:, n % RING, :], whi[:, g % RING, :].bitcast(F32),
                              ALU.subtract).then_inc(w_lo, 1)

        @block.scalar
        def _(act):
            act.dma_start(xn, i["x"][0].rearrange("(a p) d -> p a d", p=P)).then_inc(x_loaded, 16)
            act.dma_start(cn, i["ctx"][0].rearrange("(a p) d -> p a d", p=P)).then_inc(ctx_loaded, 16)
            act.dma_start(par_rows, i["table"].rearrange("(a p) f -> p a f", p=P)).then_inc(par_loaded, 16)
            steps = [0]

            def link(ins):
                steps[0] += 1
                ins.then_inc(act_step, 1)
                act.wait_ge(act_step, steps[0])

            def g_wait(u):
                act.wait_ge(g_full, g_no(u) + 1)

            def m_wait(u):
                act.wait_ge(m_full, m_no(u) + 1)

            def norm_std(u, w, feats):
                m_wait(u)
                act.activation(std[:, 0:w], m_bank(u)[:, 0:w], ACT.Sqrt, bias=eps, scale=1.0 / feats
                               ).then_inc(m_empty["act"], 1)

            def norm_hi(ht, f0, steps=(1, 2, 3, 4), shift=None):
                w = ht.shape[1] // KT
                for g in range(4):
                    act.wait_ge(h_f32, f0 + steps[g])
                    if shift is not None:
                        for k in (2 * g, 2 * g + 1):
                            for n in range(w // T):
                                s = slice(w * k + T * n, w * k + T * (n + 1))
                                ins = act.activation(hhi[:, s], ht[:, s], ACT.Identity, bias=shift(k, n))
                        ins.then_inc(h_hi, 1)
                        continue
                    act.activation(hhi[:, 2 * w * g:2 * w * (g + 1)], ht[:, 2 * w * g:2 * w * (g + 1)], ACT.Copy
                                   ).then_inc(h_hi, 1)

            act.wait_ge(c_T, 1)
            act.activation(silu_c, bank[6][:, 0:16].rearrange("p (v k) -> p k v", v=2), ACT.Silu).then_inc(c_ready, 1)
            def row_copy(n):
                act.wait_ge(rows_full, n + 1)
                if n >= 2:
                    act.wait_ge(rows_turned, n - 1)
                act.activation(row_buf[0:2, n % 2, :], bank[2 + n % 2][0:2, 0:256], ACT.Copy
                               ).then_inc(rows_copied, 1)
            act.wait_ge(x_loaded, 16)
            for n, src in enumerate((xn, cn)):
                if n == 1:
                    act.wait_ge(ctx_loaded, 16)
                for a in range(2):
                    act.activation(slot((0, 1, 4, 5)[2 * n + a]), src[:, a, :], ACT.Square, accum_out=ss[:, 2 * n + a:2 * n + a + 1]
                                   ).then_inc(act_sq, 1)
            for k in range(4):
                g_wait(f"xr{k}")
                act.activation(XT[:, 2 * k:2 * k + 2, 0:T], g_bank(f"xr{k}")[:, :].rearrange("p (k t) -> p k t", k=2),
                               ACT.Copy).then_inc(g_empty["act"], 1)
            act.wait_ge(pool_step, 1)
            act.wait_ge(act_sq, 4)
            act.activation(ss, ss, ACT.Sqrt, bias=eps, scale=1.0 / D).then_inc(ss_std, 1)
            row_copy(0)
            act.wait_ge(ss_rstd, 1)
            for n, (src, dst) in enumerate(((xn, xh), (cn, ch))):
                for a in range(2):
                    act.activation(dst[:, a, :], src[:, a, :], ACT.Copy, scale=ss[:, 2 * n + a:2 * n + a + 1]
                                   ).then_inc(xh_ready, 1)
            for k in range(KT):
                if k == 4:
                    row_copy(1)
                g_wait(f"xt{k}")
                act.activation(HT[:, 512 * k:512 * (k + 1)], g_bank(f"xt{k}")[:, :], ACT.Copy
                               ).then_inc(g_empty["act"], 1)
            for n in range(2, len(ADA_PE)):
                row_copy(n)
            split_hi(act, 0)
            act.wait_ge(mod_ready, 2)
            norm_hi(HT, 0, shift=lambda k, n: mod[:, k, n:n + 1])
            for g in range(1, RING):
                split_hi(act, g)
            act.wait_ge(masks_loaded, 16)
            act.activation(masks[:, :, :, :], masks_f, ACT.Copy).then_inc(masks_ready, 1)
            for n, (fx, kx) in enumerate(((0, 2), (1, 3))):
                for c in range(2):
                    for h in range(2):
                        u = f"{('ff', 'fb')[n]}{c}{'ab'[h]}"
                        g_wait(u)
                        src = g_bank(u)[:, :].rearrange("p (s t) -> p s t", s=2)
                        hh = 2 * c + h
                        ar = arena.rearrange("p s (h t) -> p s h t", h=HEADS)
                        act.activation(ar[:, fx:fx + 5:4, hh, :], src, ACT.Sigmoid)
                        act.activation(ar[:, kx:kx + 5:4, hh, :], src, ACT.Sigmoid, scale=-1.0
                                       ).then_inc(g_empty["act"], 1)
                    split_hi(act, G[f"{('ff', 'fb')[n]}{c}"] + RING)

            def tok_keys(d):
                for t in range(2):
                    u = f"k{'fb'[d]}T{t}"
                    m_wait(u)
                    act.activation(KTOK[d][:, t, :], m_bank(u)[:, :], ACT.Copy).then_inc(m_empty["act"], 1)

            def ctx_state(d):
                u = ("hf", "hb")[d]
                m_wait(u)
                act.activation(HS[d], m_bank(u)[:, :].rearrange("p (h v) -> p h v", h=HEADS), ACT.Copy
                               ).then_inc(m_empty["act"], 1)
            def unit_act(u, dst, func):
                g_wait(u)
                src = g_bank(u)[:, :].rearrange("p (j t) -> p j t", j=2)
                act.activation(dst, src, func).then_inc(g_empty["act"], 1)
            for c in range(2):
                unit_act(f"q{c}", Q[:, 2 * c:2 * c + 2, :], ACT.Silu)
                split_hi(act, G[f"q{c}"] + RING)
                tok_keys(c)
            act.wait_ge(lv_mm, 1)
            act.activation(S[0], bank[4][:, :].rearrange("p (h t) -> p h t", h=HEADS), ACT.Copy)
            act.activation(S[1], bank[5][:, :].rearrange("p (h t) -> p h t", h=HEADS), ACT.Copy
                           ).then_inc(lv_copied, 1)
            m_wait("wsT")
            act.activation(wsT, m_bank("wsT")[:, :].rearrange("p (h q) -> p h q", h=HEADS), ACT.Copy
                           ).then_inc(m_empty["act"], 1)
            split_hi(act, G["v0"] + RING)
            split_hi(act, G["v1"] + RING)
            ctx_state(0)
            ctx_state(1)
            for c in range(2):
                unit_act(f"mv{c}", MV[:, :, 256 * c:256 * (c + 1)], ACT.Gelu)
                split_hi(act, G[f"mv{c}"] + RING)
            unit_act("mu0", U[:, 0:2, :], ACT.Gelu)
            split_hi(act, G["mu0"] + RING)
            act.wait_ge(sg_stats, 1)
            act.activation(ln_rstd, ln_mv[:, :, 1], ACT.Sqrt, bias=eps).then_inc(sg_std, 1)
            unit_act("mu1", U[:, 2:4, :], ACT.Gelu)
            split_hi(act, G["mu1"] + RING)
            act.wait_ge(lv_mm, 9)
            for d in range(2):
                ins = act.activation(SX[d], bank[4 + d][:, :].rearrange("p (h t) -> p h t", h=HEADS), ACT.Copy)
            ins.then_inc(lv_copied, 1)
            unit_act("gt0", GT[:, 0:2, :], ACT.Silu)
            split_hi(act, G["gt0"] + RING)
            for n, u in enumerate(("oA", "oB")):
                m_wait(u)
                src = m_bank(u)[:, :].rearrange("p (h t) -> p h t", h=2)
                act.activation(OSQ[:, 2 * n:2 * n + 2, :], src, ACT.Square).then_inc(osq_ready, 1)
                act.activation(OM[:, 2 * n:2 * n + 2, :], src, ACT.Copy).then_inc(m_empty["act"], 1)
            unit_act("gt1", GT[:, 2:4, :], ACT.Silu)
            split_hi(act, G["gt1"] + RING)
            for n in range(2):
                m_wait(f"on{n}")
                act.activation(hstd[:, 2 * n:2 * n + 2, :],
                               m_bank(f"on{n}")[:, :].rearrange("p (h t) -> p h t", h=2), ACT.Sqrt, bias=eps,
                               scale=1.0 / P).then_inc(m_empty["act"], 1)
            for g, wait in ((2, (sgu_out, 1)), (3, (sgu_out, 2)), (0, (h_f32, 5)), (1, (h_f32, 6))):
                act.wait_ge(*wait)
                s = slice(2 * T * g, 2 * T * (g + 1))
                act.activation(hhi[:, s], OM.rearrange("p k t -> p (k t)")[:, s], ACT.Copy).then_inc(h_hi, 1)

            def squares(updated, g0=None, dst=SQ):
                for g in range(4):
                    act.wait_ge(*updated(g))
                    act.activation(dst[:, 512 * g:512 * (g + 1)].rearrange("p (k t) -> p k t", k=2),
                                   XT[:, 2 * g:2 * g + 2, 0:T], ACT.Square).then_inc(sq_ready, 1)
                    if g0 is not None and g < 3:
                        split_hi(act, g0 + g + RING)
            squares(lambda c: (g_empty["dve"], g_emptied(g_no(f"wo{c}"))[1]), G["wo0"])
            norm_std("sum1", T, D)
            norm_hi(HT[:, 0:KT * T], 6, shift=lambda k, n: mod[:, 24 + k, 0:1])
            split_hi(act, G["wo3"] + RING)
            act.wait_ge(pad_zero, 1)
            for j in range(FFT // 2):
                b = j % 2
                if j >= 2:
                    act.wait_ge(conv_out, j - 1)
                    act.wait_ge(g_empty["dve"], g_emptied(g_no(f"fa{j - 2}"))[1])
                g_wait(f"fg{j}")
                for t in range(2):
                    src = g_bank(f"fg{j}")[:, T * t:T * (t + 1)]
                    jt = 2 * j + t
                    act.activation(pad[:, b, t, 1:5, 1:65], src.rearrange("p (r c) -> p r c", r=4), ACT.Copy)
                    ins = act.activation(acc[:, b, t, :], src, ACT.Identity, bias=par("conv_b", k=jt),
                                         scale=par("conv_w", k=4 * FFT + jt))
                ins.then_inc(g_empty["act"], 1)
                if G[f"fg{j}"] + RING < N_SPLIT:
                    split_hi(act, G[f"fg{j}"] + RING)
                if G[f"fa{j}"] + RING < N_SPLIT:
                    split_hi(act, G[f"fa{j}"] + RING)
                act.wait_ge(conv_out, j + 1)
                act.activation(gel[:, b, :, :], acc[:, b, :, :], ACT.Gelu).then_inc(gelu_out, 1)
                if j > 1:
                    split_hi(act, G[f"fd{j - 2}"] + RING)
                act.wait_ge(*g_done(f"fa{j}"))
                if j >= 3:
                    act.wait_ge(down_used, j - 2)
                act.activation(uhi[:, j % 3, :, :], uf[:, b, :, :], ACT.Copy).then_inc(u_hi, 1)
            split_hi(act, G["fd9"] + RING)
            squares(lambda c: (x_new, c + 1))
            def adv(name):
                if G[name] + RING < N_SPLIT:
                    split_hi(act, G[name] + RING)

            def l_wait(u):
                act.wait_ge(l_full, l_no(u) + 1)
                return l_bank(u)

            def two(ps):
                return ps[:, :].rearrange("p (j t) -> p j t", j=2)

            def four(ps):
                return ps[:, :].rearrange("p (j t) -> p j t", j=4)
            act.wait_ge(var_ready, 1)
            act.activation(rstd2, std2, ACT.Sqrt).then_inc(rstd_ready, 1)
            act.activation(std[:, 0:T], rstd[:, 0:T], ACT.Sqrt).then_inc(rstd_ready, 1)
            norm_hi(HT2, 10)
            adv("fd10")
            link(act.activation(sm_coef[64:68, :], sm_log[64:68, :], ACT.Exp))
            act.activation(sm_coef[64:68, :], sm_coef[64:68, :], ACT.Copy, scale=-1.0).then_inc(coef_ready, 1)

            def conv_start(u, dst, tap):
                g_wait(u)
                for t in range(2):
                    ins = act.activation(dst[:, t, :], g_bank(u)[:, T * t:T * (t + 1)], ACT.Copy,
                                         scale=par("dn_conv", k=36 + tap + t))
                ins.then_inc(acc_start, 1)
                adv(u)

            def conv_silu(u, dst):
                act.wait_ge(*g_done(u))
                act.activation(dst, dst, ACT.Silu).then_inc(silu_done, 1)
            dn = [(f"d{n}{c}", (QC, KC, VC)["qkv".index(n)][:, 2 * c:2 * c + 2, :], 4 * "qkv".index(n) + 2 * c)
                  for n in "qkv" for c in range(2)]
            conv_start(*dn[0])
            act.wait_ge(*m_done("sm"))
            act.activation(RB[32:36, :], SMY[32:36, :], ACT.Sigmoid)
            link(act.activation(SMA[0:96, :], SMY[0:96, :], ACT.Abs))
            link(act.activation(SMA[0:96, :], SMA[0:96, :], ACT.Exp, scale=-1.0))
            act.activation(SMA[0:96, :], SMA[0:96, :], ACT.Ln, bias=1.0).then_inc(sm_ln, 1)
            conv_start(*dn[1])
            conv_silu(*dn[0][:2])
            conv_start(*dn[2])
            conv_silu(*dn[1][:2])

            def head_squares(dst, src, n):
                act.wait_ge(silu_done, n)
                act.activation(dst, src, ACT.Square).then_inc(sq_done, 1)
            head_squares(lq_sq, QC, 2)
            conv_start(*dn[3])
            conv_silu(*dn[2][:2])
            conv_start(*dn[4])
            conv_silu(*dn[3][:2])
            head_squares(lk_sq, KC, 4)

            def head_std(units, dst, scale):
                for n, u in enumerate(units):
                    m_wait(u)
                    act.activation(dst[:, 2 * n:2 * n + 2, :], two(m_bank(u)), ACT.Sqrt, bias=eps, scale=scale
                                   ).then_inc(m_empty["act"], 1)
            head_std(("lq0", "lq1"), lq_std, 1.0)
            conv_start(*dn[5])
            conv_silu(*dn[4][:2])
            head_std(("lk0", "lk1"), lk_std, 1.0)
            conv_silu(*dn[5][:2])
            for n, dst, sq in (("fq", FQ, fq_sq), ("fk", FK, fk_sq)):
                for c in range(2):
                    g_wait(f"{n}{c}")
                    act.activation(sq[:, 2 * c:2 * c + 2, :], two(g_bank(f"{n}{c}")), ACT.Square)
                    act.activation(dst[:, 2 * c:2 * c + 2, :], two(g_bank(f"{n}{c}")), ACT.Copy
                                   ).then_inc(g_empty["act"], 1)
                    adv(f"{n}{c}")
            adv("fv0")
            head_std(("sfq0", "sfq1"), fq_std, 1.0 / 64)
            adv("fv1")
            head_std(("sfk0", "sfk1"), fk_std, 1.0 / 64)

            def copy_unit(u, dst, func=ACT.Copy):
                g_wait(u)
                act.activation(dst, two(g_bank(u)), func).then_inc(g_empty["act"], 1)
                adv(u)
            copy_unit("scc0", CS[:, 0:2, :])
            copy_unit("scc1", CS[:, 2:4, :])

            def soft(a, h, ss):
                act.activation(ss[:, h, :], ss[:, h, :], ACT.Exp, bias=fneg[:, a, h:h + 1],
                               accum_out=fsum[:, a, h:h + 1]).then_inc(ss_exp, 1)
            act.wait_ge(ss_ready, 1)
            for h in range(8):
                soft(0, h, SS0)
            adv("scv0")
            act.wait_ge(ss_ready, 2)
            for h in range(4):
                soft(1, h, SS1)
            adv("scv1")
            for h in range(4, 8):
                soft(1, h, SS1)

            def p_copy(n):
                dst = (PT0[:, 0:4, 0:P], None, PT0[:, 0:4, P:T], None, PT1[:, 0:4, :])[n]
                act.activation(dst, four(l_wait(f"pt{n}")), ACT.Copy).then_inc(l_empty["act"], 1)
            p_copy(0)
            copy_unit("scb0", SCB[:, 0:2, :])
            p_copy(2)
            p_copy(4)
            copy_unit("scb1", SCB[:, 2:4, :])

            def y_split(n):
                act.wait_ge(y_f32, n + 1)
                act.activation(yhi[n], (YSC, None, ODN)[n], ACT.Copy).then_inc(y_hi, 1)
            y_split(0)
            for n in range(2):
                act.activation(yhi[1][:, 2 * n:2 * n + 2, :], two(l_wait(f"yf{n}")), ACT.Copy).then_inc(y_hi, 1)
            copy_unit("dz0", ZS[:, 0:2, :], ACT.Silu)
            copy_unit("dz1", ZS[:, 2:4, :], ACT.Silu)
            for n in range(2):
                act.activation(GBS[:, 2 * n:2 * n + 2, :], two(l_wait(f"gb{n}")), ACT.Copy
                               ).then_inc(l_empty["act"], 1)
            act.wait_ge(*l_done("gb1"))
            act.activation(QD, GBS, ACT.Exp).then_inc(qd_exp, 1)
            for n, d in enumerate((DT, DL)):
                act.wait_ge(d_raw, n + 1)
                act.activation(d, d, ACT.Exp, scale=(1.0, -1.0)[n]).then_inc(d_exp, 1)
            act.activation(bgcol, COLS[:, 1, 64:68], ACT.Exp).then_inc(bg_ready, 1)

            def gate(name):
                c = int(name[2])
                copy_unit(name, GATES[:, 2 * c:2 * c + 2, :], ACT.Sigmoid)
            gates_s = [f"gs{c}" for c in range(4)]
            for u in gates_s:
                gate(u)
            fill = ["brs0", "brs1", "gf0", "gf1", "gf2", "gf3"]

            def filler(name):
                if name[0] == "g":
                    gate(name)
                else:
                    adv(name)
            for lv in range(1, 7):
                for n in range(2):
                    act.activation(Y[:, 4 * n:4 * n + 4, :], four(l_wait(f"y{lv}{n}")), ACT.Copy
                                   ).then_inc(l_empty["act"], 1)
                filler(fill[lv - 1])
            for n in range(2):
                act.activation(U1[:, 4 * n:4 * n + 4, :], four(l_wait(f"us{n}")), ACT.Copy
                               ).then_inc(l_empty["act"], 1)
            act.activation(KCT, four(l_wait("kc")), ACT.Copy).then_inc(l_empty["act"], 1)
            act.activation(S1, four(l_wait("s1")), ACT.Copy).then_inc(l_empty["act"], 1)
            adv("brf0")
            adv("brf1")
            for n in range(2):
                src = two(l_wait(f"do{n}"))
                act.activation(DSQ[:, 2 * n:2 * n + 2, :], src, ACT.Square).then_inc(osq2, 1)
                act.activation(ODN[:, 2 * n:2 * n + 2, :], src, ACT.Copy).then_inc(l_empty["act"], 1)
            gate("gd0")
            head_std(("on2", "on3"), dstd, 1.0 / P)
            act.wait_ge(*m_done("pT"))
            act.activation(phi, PF.rearrange("p (k t) -> p k t", t=T), ACT.Copy).then_inc(p_hi, 1)
            gate("gd1")
            gate("gd2")
            y_split(2)
            gate("gd3")
            adv("brd0")
            for g in range(4):
                act.wait_ge(merged_f32, 5 + g)
                act.activation(hhi[:, 512 * g:512 * (g + 1)].rearrange("p (k t) -> p k t", k=2),
                               XC[:, 2 * g:2 * g + 2, :], ACT.Copy).then_inc(h_hi, 1)
            adv("brd1")
            squares(lambda c: g_done(f"wp{c}"), G["wp0"], dst=SQ2)
            norm_std("sum4", T, D)
            norm_hi(HT2, 14)
            adv("wp3")
            for j in range(FFT // 2):
                b = j % 2
                if j >= 2:
                    act.wait_ge(u2_f32, j - 1)
                for n, w in enumerate("ga"):
                    g_wait(f"s{w}{j}")
                    for t in range(2):
                        col = par("ffn_conv", k=2 * 2 * FFT + FFT * n + 2 * j + t)
                        ins = act.activation(acc2[:, b, n, t, :], g_bank(f"s{w}{j}")[:, T * t:T * (t + 1)], ACT.Copy,
                                             scale=col)
                    ins.then_inc(acc2_start, 1)
                    adv(f"s{w}{j}")
                act.wait_ge(*g_done(f"sg{j}"))
                act.activation(acc2[:, b, 0, :, :], acc2[:, b, 0, :, :], ACT.Silu).then_inc(silu2, 1)
                if j > 1:
                    adv(f"sd{j - 2}")
                act.wait_ge(u2_f32, j + 1)
                if j >= 3:
                    act.wait_ge(down_used, FFT // 2 + j - 2)
                act.activation(uhi[:, j % 3, :, :], uf[:, b, :, :], ACT.Copy).then_inc(u_hi, 1)
            adv(f"sd{FFT // 2 - 2}")

            def ple(n):
                u = f"ple{'abcd'[n]}"
                g_wait(u)
                act.activation(PLE[:, 2 * n:2 * n + 2, :], two(g_bank(u)), ACT.Copy).then_inc(g_empty["act"], 1)
            squares(lambda c: (x_new, 8 + c + 1), dst=SQ2)
            ple(0)
            ple(1)
            norm_std("sum5", T, D)
            ple(2)
            ple(3)
            norm_hi(HT2, 18)
            adv("sd10")
            adv("ple")
            for c in range(4):
                copy_unit(f"pg{c}", PG[:, 2 * c:2 * c + 2, :], ACT.Sigmoid)
            for n in range(2):
                act.wait_ge(l_full, len(l_units) + 2 * n + 1)
                act.activation(OUTN[:, n, 0:512], bank[4 + 2 * n][:, :], ACT.Copy).then_inc(out_act, 1)

        @block.tensor
        def _(pe):
            def g_open(u):
                n = g_no(u)
                if n >= 2:
                    e, k = g_emptied(n - 2)
                    pe.wait_ge(g_empty[e], k)
                return g_bank(u)

            def m_open(u):
                n = m_no(u)
                if n >= 2:
                    e, k = m_emptied(n - 2)
                    pe.wait_ge(m_empty[e], k)
                return m_bank(u)

            def w_parts(name, k):
                g = G[name]
                pe.wait_ge(w_hi, g + 1)
                pe.wait_ge(w_lo, g + 1)
                return [w[:, g % RING, :].rearrange("p (k n) -> p k n", k=k) for w in (whi, wlo)]

            def h_wait(g0, k, first):
                if first and k % 2 == 0:
                    pe.wait_ge(h_hi, g0 + k // 2 + 1)
                    pe.wait_ge(h_lo, g0 + k // 2 + 1)

            def product(o, w, a, start, stop, **kw):
                (wh, wl), (ah, al) = w, a
                pe.matmul(o, wh, ah, start=start, stop=False, **kw)
                pe.matmul(o, wh, al, start=False, stop=False, **kw)
                return pe.matmul(o, wl, ah, start=False, stop=stop, **kw)

            def acts(w, k, lo=0, n=None):
                n = n or w
                return [h[:, w * k + lo:w * k + lo + n] for h in (hhi, hlo)]

            pe.wait_ge(const_loaded, 16)
            pe.wait_ge(c_loaded, 16)
            pe.transpose(bank[6][:, 0:16], c_rows[0:16, :], ident[0:16, 0:16]).then_inc(c_T, 1)
            pe.wait_ge(x_loaded, 16)
            for k in range(4):
                o = g_open(f"xr{k}")
                for n in range(2):
                    for a in range(2):
                        ins = pe.transpose(o[:, T * n + P * a:T * n + P * (a + 1)],
                                           xn[:, a, P * (2 * k + n):P * (2 * k + n + 1)], ident)
                ins.then_inc(g_full, 1)
            pe.wait_ge(par_loaded, 16)
            pe.wait_ge(c_ready, 1)
            for a in range(5):
                r = min(P, N_ROWS - P * a)
                ins = pe.transpose(bank[6 + a // 4][:, P * (a % 4):P * (a % 4) + r], par_rows[0:r, a, :],
                                   ident[0:r, 0:r])
            ins.then_inc(par_T, 1)

            def sum_squares(u, s0, w, src=SQ):
                o = m_open(u)
                for k in range(KT):
                    if k % 2 == 0:
                        pe.wait_ge(sq_ready, s0 + k // 2 + 1)
                    ins = pe.matmul(o[:, 0:w], ones, src[:, w * k:w * (k + 1)], start=k == 0, stop=k == KT - 1)
                ins.then_inc(m_full, 1)
            def ada_sum(src, o, at, done):
                for nb in range(2):
                    ins = pe.matmul(o[:, at + 2 * nb:at + 2 * nb + 1], src[:, P * nb:P * (nb + 1)], ones[:, 0:1],
                                    start=True, stop=True)
                ins.then_inc(done, 1)

            pe.wait_ge(pool_step, 2)

            def row_sums(n):
                c = ADA_PE[n]
                m = ada_place[c]
                pe.wait_ge(raw_loaded[m % RING], 16 * (m // RING + 1))
                if n >= 2:
                    pe.wait_ge(rows_copied, n - 1)
                w = raw[:, m % RING, :].rearrange("p (k n) -> p k n", k=KT)
                for k in range(KT):
                    ins = pe.matmul(bank[2 + n % 2][0:2, 0:256], silu_c[:, k, :], w[:, k, :],
                                    start=k == 0, stop=k == KT - 1)
                ins.then_inc(rows_full, 1)

            def row_turn(n):
                c = ADA_PE[n]
                pe.wait_ge(rows_copied, n + 1)
                for nb in range(2):
                    at = 4 * (c % 4) + 2 * nb
                    ins = pe.transpose(bank[4 + c // 4][:, at:at + 2], row_buf[0:2, n % 2, P * nb:P * (nb + 1)],
                                       ident[0:2, 0:2])
                ins.then_inc(rows_turned, 1)

            def column_sums(c):
                for v in range(2):
                    m = 2 * ADA_DVE.index(c) + v
                    pe.wait_ge(ada_dve, m + 1)
                    ada_sum(acc_dve[:, m % 4, :], bank[4 + c // 4], 4 * (c % 4) + v, sum_dve)
            row_sums(0)
            column_sums(0)
            row_sums(1)
            row_turn(0)
            pe.wait_ge(xh_ready, 4)
            for k in range(KT):
                o = g_open(f"xt{k}")
                for n, src in enumerate((xh, ch)):
                    for a in range(2):
                        ins = pe.transpose(o[:, T * n + P * a:T * n + P * (a + 1)], src[:, a, P * k:P * (k + 1)], ident)
                ins.then_inc(g_full, 1)
            row_turn(1)
            column_sums(2)
            row_sums(2)
            row_sums(3)
            row_turn(2)
            row_turn(3)
            column_sums(5)
            row_sums(4)
            row_turn(4)

            def ada_unit(a):
                o = g_open(f"A{a}")
                pe.wait_ge(ada_pool, 4 * (a - 1))
                for c in range(4 * a, 4 * a + 4):
                    for nb in range(2):
                        at = 2 * (c % 4) + nb
                        src = XC[:, c % 8, :] if a < 5 else acc_late[:, c % 4, :]
                        ins = pe.matmul(o[:, at:at + 1], src[:, P * nb:P * (nb + 1)], ones[:, 0:1],
                                        start=True, stop=True)
                ins.then_inc(g_full, 1)

            def gemm(name, w, g0=None, n_tok=T, units="unit", part=(0, 1)):
                wh, wl = w_parts(name, KT)
                for nb in part:
                    u = name + ("ab"[nb] if units == "bank" else "")
                    if units == "bank" or nb == 0:
                        g_open(u)
                    bk = g_bank(u)
                    o = bk[:, 0:n_tok] if units == "bank" else bk[:, T * nb:T * (nb + 1)]
                    for k in range(KT):
                        if g0 is not None:
                            h_wait(g0, k, nb == 0)
                        ws = [x[:, k, P * nb:P * (nb + 1)] for x in (wh, wl)]
                        ins = product(o, ws, acts(w, k, 0, n_tok), k == 0, k == KT - 1)
                    if nb == 1 or units == "bank":
                        ins.then_inc(g_full, 1)

            def gemm_tok(name, w, unit=None, t0=0):
                wh, wl = w_parts(name, KT)
                bk = g_open(unit or name)
                for n in range(2):
                    for k in range(KT):
                        ah, al = acts(w, k, P * (t0 + n), P)
                        ins = product(bk[:, T * n:T * (n + 1)], (ah, al), (wh[:, k, :], wl[:, k, :]), k == 0,
                                      k == KT - 1)
                ins.then_inc(g_full, 1)

            for n, name in enumerate(("ff0", "ff1", "fb0", "fb1")):
                gemm(name, 512, 0 if n == 0 else None, 512, "bank")

            def tok_keys(d):
                src = (KFc, KBc)[d]
                pe.wait_ge(ctx_k, d + 1)
                for t in range(2):
                    o = m_open(f"k{'fb'[d]}T{t}")
                    for h in range(HEADS):
                        ins = pe.transpose(o[:, P * h:P * (h + 1)], src[:, h, P * t:P * (t + 1)], ident)
                    ins.then_inc(m_full, 1)

            def ctx_state(d):
                u = ("hf", "hb")[d]
                o = m_open(u)
                pe.wait_ge(*m_done(f"k{'fb'[d]}T1"))
                pe.wait_ge(g_empty["dve"], g_emptied(g_no("v1b"))[1])
                for h in range(HEADS):
                    for t in range(2):
                        ins = pe.matmul(o[:, P * h:P * (h + 1)], KTOK[d][:, t, P * h:P * (h + 1)],
                                        VTOK[:, 2 + t, P * h:P * (h + 1)], start=t == 0, stop=t == 1)
                ins.then_inc(m_full, 1)

            gemm("q0", 512)
            tok_keys(0)
            gemm("q1", 512)
            ada_unit(2)
            tok_keys(1)
            o = m_open("wsT")
            pe.wait_ge(sgu_loaded, 64)
            for h in range(HEADS):
                ins = pe.transpose(o[:, P * h:P * (h + 1)], ws_nat[:, h, :], ident)
            ins.then_inc(m_full, 1)

            def level(s):
                pe.wait_ge(lv_upd, max(s, 1))
                if s == 1 or s == 8:
                    pe.wait_ge(lv_copied, 1)
                if s >= 2:
                    pe.wait_ge(lv_empty, s - 1)
                for h in range(HEADS):
                    hs = slice(P * h, P * (h + 1))
                    t0, t1 = slice(0, P), slice(P, T)
                    if s == 0:
                        pairs = [(4, KSUM, Q, t0, t0), (5, KSUM, Q, t1, t1)]
                    elif s == 8:
                        pairs = [(4, KFx, QPf, t0, t1), (5, KBx, QSb, t1, t0)]
                    else:
                        pairs = [(4, KFx, QPf, t0, t0), (5, KBx, QSb, t0, t0),
                                 (6, KFx, QPf, t1, t1), (7, KBx, QSb, t1, t1)]
                    for bk, k, q, ts, tt in pairs:
                        ins = pe.matmul(bank[bk][:, hs], k[:, h, ts], q[:, h, tt], start=True, stop=True)
                ins.then_inc(lv_mm, 1)

            level(0)
            gemm_tok("v0", 512, "v0a", 0)
            level(1)
            gemm_tok("v0", 512, "v0b", 2)
            level(2)
            gemm_tok("v1", 512, "v1a", 0)
            level(3)
            gemm_tok("v1", 512, "v1b", 2)
            level(4)
            ctx_state(0)
            ctx_state(1)
            gemm_tok("mv0", 512)
            level(5)
            gemm_tok("mv1", 512)
            level(6)
            gemm("mu0", 512)
            ada_unit(3)
            level(7)
            gemm("mu1", 512)
            level(8)
            pe.wait_ge(vn_ready, 1)
            for n in range(2):
                o = m_open(f"z{n}")
                for hh in range(2):
                    h = 2 * n + hh
                    for t in range(2):
                        ins = pe.matmul(o[:, T * hh + P * t:T * hh + P * (t + 1)], MV[:, t, P * h:P * (h + 1)],
                                        wsT[:, h, :], start=True, stop=True)
                ins.then_inc(m_full, 1)
            gemm("gt0", 512)
            pe.wait_ge(lv_upd, 9)
            pe.wait_ge(lv_empty, 7)
            pe.wait_ge(lv_copied, 2)
            for n, u in enumerate(("oA", "oB")):
                o = m_open(u)
                for hh in range(2):
                    h = 2 * n + hh
                    hv = slice(P * h, P * (h + 1))
                    full, t0, t1 = (slice(T * hh + a, T * hh + b) for a, b in ((0, T), (0, P), (P, T)))
                    pe.matmul(o[:, full], HS[0][:, h, :], QPf[:, h, :], start=True, stop=False)
                    pe.matmul(o[:, full], HS[1][:, h, :], QSb[:, h, :], start=False, stop=False)
                    pe.matmul(o[:, t0], VTOK[:, 0, hv], S[0][:, h, :], start=False, stop=False)
                    pe.matmul(o[:, t0], VTOK[:, 1, hv], SX[1][:, h, :], start=False, stop=False)
                    pe.matmul(o[:, t1], VTOK[:, 1, hv], S[1][:, h, :], start=False, stop=False)
                    ins = pe.matmul(o[:, t1], VTOK[:, 0, hv], SX[0][:, h, :], start=False, stop=True)
                ins.then_inc(m_full, 1)
            gemm("gt1", 512)
            for n in range(2):
                o = m_open(f"on{n}")
                pe.wait_ge(osq_ready, n + 1)
                pe.matmul(o[:, :], ones, OSQ[:, 2 * n:2 * n + 2, :].rearrange("p h t -> p (h t)"),
                          start=True, stop=True).then_inc(m_full, 1)
            ada_unit(4)
            for ks in (range(4, 8), range(4)):
                for c in range(2):
                    wh, wl = w_parts(f"wo{c}", KT)
                    o = g_open(f"wo{c}")
                    for nb in range(2):
                        for k in ks:
                            if c == 0 and nb == 0 and k % 2 == 0:
                                pe.wait_ge(h_hi, 4 + (3, 4, 1, 2)[k // 2])
                                pe.wait_ge(h_lo, 4 + (3, 4, 1, 2)[k // 2])
                            ws = [x[:, k, P * nb:P * (nb + 1)] for x in (wh, wl)]
                            ins = product(o[:, T * nb:T * (nb + 1)], ws, acts(T, k), k == 4 and nb == 0, k == 3,
                                          skip_group_check=True)
                    if ks[0] == 0:
                        ins.then_inc(g_full, 1)
            for c in range(2, 4):
                gemm(f"wo{c}", T)
            sum_squares("sum1", 0, T)

            def down(j, tag="f"):
                b = j % 3
                wh, wl = w_parts(f"{tag}d{j}", 2)
                n = j + (FFT // 2 if tag == "s" else 0)
                pe.wait_ge(u_hi, n + 1)
                pe.wait_ge(u_lo, n + 1)
                for t in range(2):
                    for nb in range(KT):
                        o = bank[4 + nb // 2][:, T * (nb % 2):T * (nb % 2 + 1)]
                        ws = [x[:, t, P * nb:P * (nb + 1)] for x in (wh, wl)]
                        first = j == 0 and t == 0
                        ins = product(o, ws, (uhi[:, b, t, :], ulo[:, b, t, :]), first and nb % 2 == 0,
                                      j == FFT // 2 - 1 and t == 1, skip_group_check=True)
                ins.then_inc(down_used, 1)

            for j in range(FFT // 2):
                gemm(f"fg{j}", T, 8 if j == 0 else None)
                gemm(f"fa{j}", T)
                if j == 7:
                    ada_unit(5)
                if j > 1:
                    down(j - 2)
            down(FFT // 2 - 2)
            down(FFT // 2 - 1)
            o = [m_open("sum2"), m_open("sum3")]
            pe.wait_ge(weigh_ready, 1)
            for k in range(KT):
                pe.wait_ge(sq_ready, 4 + k // 2 + 1)
                for n in range(2):
                    ins = pe.matmul(o[n][:, 0:T], (ones, weigh[:, k, :])[n], SQ[:, T * k:T * (k + 1)], start=k == 0,
                                    stop=k == KT - 1)
                    if k == KT - 1:
                        ins.then_inc(m_full, 1)
            def l_open(u):
                n = l_no(u)
                if n >= 4:
                    e, k = l_emptied(n - 4)
                    pe.wait_ge(l_empty[e], k)
                return l_bank(u)
            gemm("dq0", T, 12)
            o = m_open("sm")
            pe.wait_ge(col_loaded, 16)
            pe.wait_ge(h_f32, 14)
            for k in range(KT):
                ins = pe.matmul(o[0:96, 0:T], wsm[:, k, :], HT2[:, T * k:T * (k + 1)], start=k == 0, stop=k == KT - 1)
            ins.then_inc(m_full, 1)
            gemm("dq1", T)
            gemm("dk0", T)
            gemm("dk1", T)
            o = m_open("colT")
            pe.wait_ge(rb_ready, 1)
            for t in range(2):
                ins = pe.transpose(o[:, 96 * t:96 * (t + 1)], RB[0:96, P * t:P * (t + 1)], ident[0:96, 0:96])
            ins.then_inc(m_full, 1)
            gemm("dv0", T)

            def head_sums(units, mat, src, n):
                pe.wait_ge(sq_done, n)
                for c, u in enumerate(units):
                    o = m_open(u)
                    pe.matmul(o[:, :], mat, src[:, 2 * c:2 * c + 2, :].rearrange("p h t -> p (h t)"),
                              start=True, stop=True).then_inc(m_full, 1)
            head_sums(("lq0", "lq1"), ones, lq_sq, 1)
            gemm("dv1", T)
            head_sums(("lk0", "lk1"), ones, lk_sq, 2)
            for u in ("fq0", "fq1", "fk0", "fk1"):
                gemm(u, T)
            gemm_tok("fv0", T)
            pe.wait_ge(b2_loaded, 80)
            for c in range(2):
                o = m_open(f"sfq{c}")
                pe.wait_ge(*g_done(f"fq{c}"))
                pe.matmul(o[:, :], half, fq_sq[:, 2 * c:2 * c + 2, :].rearrange("p h t -> p (h t)"),
                          start=True, stop=True).then_inc(m_full, 1)
            gemm_tok("fv1", T)
            for c in range(2):
                o = m_open(f"sfk{c}")
                pe.wait_ge(*g_done(f"fk{c}"))
                pe.matmul(o[:, :], half, fk_sq[:, 2 * c:2 * c + 2, :].rearrange("p h t -> p (h t)"),
                          start=True, stop=True).then_inc(m_full, 1)
            for u in ("scc0", "scc1", "scv0"):
                gemm(u, T)

            def fox_scores(u, a, heads):
                o = l_open(u)
                n = P * (a + 1)
                for m, h in enumerate(heads):
                    q, k = (FQ, FQO)[h % 2][:, h // 2, P * a:P * (a + 1)], FK[:, h // 2, 0:n]
                    pe.matmul(o[:, n * m:n * (m + 1)], q, k, start=True, stop=False)
                    ins = pe.matmul(o[:, n * m:n * (m + 1)], sel(0, h), NCF[0:8, 0:n], start=False, stop=True)
                ins.then_inc(l_full, 1)
            pe.wait_ge(f_ready, 2)
            fox_scores("sa0", 0, range(4))
            fox_scores("sa1", 0, range(4, 8))
            fox_scores("sb0", 1, range(0, 2))
            fox_scores("sb1", 1, range(2, 4))
            fox_scores("sb2", 1, range(4, 6))
            fox_scores("sb3", 1, range(6, 8))
            gemm("scv1", T)

            def fox_turn(n):
                src = (SS0[:, :, :], SS1[:, :, 0:P], SS1[:, :, P:T])[n // 2]
                o = l_open(f"pt{n}")
                for h in range(4):
                    ins = pe.transpose(o[:, P * h:P * (h + 1)], src[:, 4 * (n % 2) + h, :], ident)
                ins.then_inc(l_full, 1)
            pe.wait_ge(p_ready, 1)
            fox_turn(0)
            fox_turn(1)
            gemm("scb0", T)
            pe.wait_ge(p_ready, 2)
            for n in range(2, 6):
                fox_turn(n)
            gemm("scb1", T)
            for e in (4, 5):
                pe.wait_ge(*l_done(f"pt{e}"))
            for n in range(2):
                o = l_open(f"yf{n}")
                for pair in range(2):
                    for odd in range(2):
                        h = 4 * n + 2 * pair + odd
                        r = slice(64 * odd, 64 * odd + 64)
                        pe.matmul(o[r, T * pair:T * (pair + 1)], FV[:, 0, 64 * h:64 * h + 64], PT0[:, h, :],
                                  start=True, stop=False)
                        ins = pe.matmul(o[r, T * pair + P:T * (pair + 1)], FV[:, 1, 64 * h:64 * h + 64],
                                        PT1[:, h, :], start=False, stop=True)
                ins.then_inc(l_full, 1)
            gemm("dz0", T)
            gemm("dz1", T)
            for g, name in ((2, "gb"), (1, "bb")):
                for n in range(2):
                    o = l_open(f"{name}{n}")
                    for h in range(2):
                        ins = pe.matmul(o[:, T * h:T * (h + 1)], sel(g, 2 * n + h), RB[32 * g:32 * g + 4, :],
                                        start=True, stop=True)
                    ins.then_inc(l_full, 1)
            gemm("gs0", T)

            def per_chunk(name, lhsT, rhs):
                for c in range(2):
                    o = l_open(f"{name}{c}")
                    for h in range(HEADS):
                        ins = pe.matmul(o[:, P * h:P * (h + 1)], lhsT(c, h), rhs(c, h), start=True, stop=True)
                    ins.then_inc(l_full, 1)

            def tok(a):
                return lambda c, h: a[:, h, P * c:P * (c + 1)]

            def mat(a):
                return lambda c, h: a[:, 4 * c + h, :]
            pe.wait_ge(*l_done("bb1"))
            per_chunk("an", tok(KB), tok(KC))
            per_chunk("at", tok(KC), tok(KB))
            gemm("gs1", T)
            per_chunk("qk", tok(KC), tok(QC))

            def turn(name, src):
                for c in range(2):
                    o = l_open(f"{name}{c}")
                    for h in range(HEADS):
                        ins = pe.transpose(o[:, P * h:P * (h + 1)], src[:, h, P * c:P * (c + 1)], ident)
                    ins.then_inc(l_full, 1)
            turn("vt", VC)
            gemm("gs2", T)
            turn("kt", KC)
            gemm("gs3", T)

            def branch(name, n, part=(0, 1)):
                wh, wl = w_parts(name, 4)
                pe.wait_ge(y_hi, (1, 3, 4)[n])
                pe.wait_ge(*((y_lo, 1), l_done("yf1"), (y_lo, 2))[n])
                for nb in range(2 * part[0], 2 * part[-1] + 2):
                    if nb % 2 == 0:
                        o = g_open(name + "ab"[nb // 2])
                    for k in range(4):
                        ws = [x[:, k, P * nb:P * (nb + 1)] for x in (wh, wl)]
                        ins = product(o[:, T * (nb % 2):T * (nb % 2 + 1)], ws, (yhi[n][:, k, :], ylo[n][:, k, :]),
                                      k == 0, k == 3)
                    if nb % 2 == 1:
                        ins.then_inc(g_full, 1)

            fill = ["brs0", "brs1", "gf0", "gf1", "gf2", "gf3"]

            def filler(name, part=(0, 1)):
                if name[0] == "g":
                    gemm(name, T, part=part)
                else:
                    branch(name, "sf".index(name[2]), part)
            pe.wait_ge(x_init, 1)
            for lv in range(1, 7):
                if lv > 1:
                    pe.wait_ge(*l_done(f"xt{lv - 1}1"))
                per_chunk(f"y{lv}", mat(ANT), mat(XI))
                filler(fill[lv - 1], (0,))
                pe.wait_ge(*l_done(f"y{lv}1"))
                per_chunk(f"xx{lv}", mat(XIT), mat(Y))
                per_chunk(f"xt{lv}", mat(Y), mat(XIT))
                filler(fill[lv - 1], (1,))
            pe.wait_ge(*l_done("xt61"))
            per_chunk("us", mat(XIT), mat(VB))
            o = l_open("kc")
            for h in range(HEADS):
                ins = pe.matmul(o[:, P * h:P * (h + 1)], KBG[:, h, :], XIT[:, 4 + h, :], start=True, stop=True)
            ins.then_inc(l_full, 1)
            o = m_open("pT")
            pe.wait_ge(p_loaded, 16)
            for k in range(2):
                for t in range(2):
                    ins = pe.transpose(o[:, T * k + P * t:T * k + P * (t + 1)], PNAT[:, t, P * k:P * (k + 1)], ident)
            ins.then_inc(m_full, 1)
            filler("brf0", (0,))
            o = l_open("s1")
            pe.wait_ge(*l_done("us1"))
            for h in range(HEADS):
                ins = pe.matmul(o[:, P * h:P * (h + 1)], KD[:, h, :], U1[:, h, :], start=True, stop=True)
            ins.then_inc(l_full, 1)
            filler("brf0", (1,))
            o = l_open("w1")
            pe.wait_ge(*l_done("s1"))
            for h in range(HEADS):
                ins = pe.matmul(o[:, P * h:P * (h + 1)], KCT[:, h, :], S1[:, h, :], start=True, stop=True)
            ins.then_inc(l_full, 1)
            filler("brf1")
            pe.wait_ge(*l_done("w1"))
            for n in range(2):
                o = l_open(f"do{n}")
                for hh in range(2):
                    h = 2 * n + hh
                    t0, t1 = slice(T * hh, T * hh + P), slice(T * hh + P, T * hh + T)
                    pe.matmul(o[:, t0], U1[:, h, :], QKT[:, h, :], start=True, stop=True)
                    pe.matmul(o[:, t1], S1[:, h, :], QD[:, h, P:T], start=True, stop=False)
                    ins = pe.matmul(o[:, t1], U1[:, 4 + h, :], QKT[:, 4 + h, :], start=False, stop=True)
                ins.then_inc(l_full, 1)
            filler("gd0")
            for n in range(2):
                o = m_open(f"on{2 + n}")
                pe.wait_ge(osq2, n + 1)
                pe.matmul(o[:, :], ones, DSQ[:, 2 * n:2 * n + 2, :].rearrange("p h t -> p (h t)"),
                          start=True, stop=True).then_inc(m_full, 1)
            for c in range(1, 4):
                filler(f"gd{c}")
            branch("brd0", 2)
            branch("brd1", 2)
            for c in range(4):
                gemm(f"wp{c}", T, 16 if c == 0 else None)
            sum_squares("sum4", 8, T, SQ2)
            for j in range(FFT // 2):
                gemm(f"sg{j}", T, 20 if j == 0 else None)
                gemm(f"sa{j}", T)
                if j > 1:
                    down(j - 2, "s")
            down(FFT // 2 - 2, "s")
            down(FFT // 2 - 1, "s")

            def ple(units):
                wh, wl = w_parts("ple", 2)
                for u in units:
                    o = g_open("ple" + u)
                    for n in range(2):
                        nb = 2 * "abcd".index(u) + n
                        for k in range(2):
                            ws = [x[:, k, P * nb:P * (nb + 1)] for x in (wh, wl)]
                            ins = product(o[:, T * n:T * (n + 1)], ws, (phi[:, k, :], plo[:, k, :]), k == 0, k == 1)
                    ins.then_inc(g_full, 1)
            pe.wait_ge(p_hi, 1)
            pe.wait_ge(p_lo, 1)
            ple("ab")
            sum_squares("sum5", 12, T, SQ2)
            ple("cd")
            for c in range(4):
                gemm(f"pg{c}", T, 24 if c == 0 else None)
            for t in range(2):
                for c in range(2):
                    pe.wait_ge(x_new, 12 + 2 * (c + 1))
                    for k in range(4):
                        ins = pe.transpose(bank[4 + 2 * t + c][:, P * k:P * (k + 1)],
                                           XT[:, 4 * c + k, P * t:P * (t + 1)], ident)
                    ins.then_inc(l_full, 1)

        @block.vector
        def _(dve):
            steps = [0]

            def mark(ins):
                steps[0] += 1
                ins.then_inc(dve_step, 1)
                return steps[0]

            def link(ins):
                dve.wait_ge(dve_step, mark(ins))

            def g_wait(u):
                dve.wait_ge(g_full, g_no(u) + 1)
                return g_bank(u)


            def modulation(a, ps, done, v=1):
                b = par("b_ada", 8, 8 * a).unsqueeze(2).broadcast_to([P, 8, v])
                dve.tensor_tensor(mod[:, 8 * a:8 * a + 8, 0:v], ps[:, 0:8 * v].rearrange("p (n v) -> p n v", v=v), b,
                                  ALU.add).then_inc(done, 1)

            def normalise(ht, g0, w, xs, scale, shift, m_u):
                dve.wait_ge(m_empty["act"], m_emptied(m_no(m_u))[1])
                link(dve.reciprocal(rstd[:, 0:w], std[:, 0:w]))
                for g in range(4):
                    scaled(ht, w, xs, scale, g)
                    if g > 0:
                        low_parts(ht, w, shift, g0, g - 1)
                low_parts(ht, w, shift, g0, 3)

            def scaled(ht, w, xs, scale, g, by=rstd):
                for k in (2 * g, 2 * g + 1):
                    for n in range(w // T):
                        ins = dve.scalar_tensor_tensor(out=ht[:, w * k + T * n:w * k + T * (n + 1)],
                                                       in0=xs[:, k, T * n:T * (n + 1)], scalar=scale(k, n),
                                                       in1=by[:, T * n:T * (n + 1)], op0=ALU.mult, op1=ALU.mult)
                ins.then_inc(h_f32, 1)

            def low_parts(ht, w, shift, g0, g):
                dve.wait_ge(h_hi, g0 + g + 1)
                if shift is None:
                    s = slice(2 * w * g, 2 * w * (g + 1))
                    ins = dve.tensor_tensor(hlo[:, s], ht[:, s], hhi[:, s].bitcast(F32), ALU.subtract)
                else:
                    for k in (2 * g, 2 * g + 1):
                        for n in range(w // T):
                            s = slice(w * k + T * n, w * k + T * (n + 1))
                            ins = dve.scalar_tensor_tensor(out=hlo[:, s], in0=ht[:, s], scalar=shift(k, n),
                                                           in1=hhi[:, s].bitcast(F32), op0=ALU.add, op1=ALU.subtract)
                ins.then_inc(h_lo, 1)

            def weighted(c):
                n = ada_place[c]
                dve.wait_ge(raw_loaded[n % RING], 16 * (n // RING + 1))
                w = raw[:, n % RING, :].rearrange("p (k n) -> p k n", k=KT)
                marks = {}
                for k in range(KT):
                    for v in range(2):
                        m = 2 * ADA_DVE.index(c) + v
                        a, dst = silu_c[:, k, v:v + 1], (acc_dve[:, m % 4, :], acc_odd[:, v, :])[k % 2]
                        if k < 2:
                            if m >= 4 and k == 0:
                                dve.wait_ge(sum_dve, m - 3)
                            if m >= 2 and k == 1:
                                dve.wait_ge(ada_dve, m - 1)
                            ins = dve.tensor_scalar(dst, w[:, k, :], a, None, ALU.mult)
                        else:
                            dve.wait_ge(dve_step, marks[k - 2, v])
                            ins = dve.scalar_tensor_tensor(out=dst, in0=w[:, k, :], scalar=a, in1=dst,
                                                           op0=ALU.mult, op1=ALU.add)
                        marks[k, v] = mark(ins)
                for v in range(2):
                    dve.wait_ge(dve_step, marks[KT - 1, v])
                    dst = acc_dve[:, (2 * ADA_DVE.index(c) + v) % 4, :]
                    dve.tensor_tensor(dst, dst, acc_odd[:, v, :], ALU.add).then_inc(ada_dve, 1)

            dve.wait_ge(c_ready, 1)
            weighted(0)
            dve.wait_ge(ss_std, 1)
            dve.reciprocal(ss, ss).then_inc(ss_rstd, 1)
            weighted(2)
            weighted(5)
            dve.wait_ge(par_T, 1)
            dve.tensor_copy(params[:, 0:512], bank[6][:, :]).then_inc(par_ready, 1)
            dve.tensor_copy(params[:, 512:N_ROWS], bank[7][:, 0:N_ROWS - 512]).then_inc(par_ready, 1)
            dve.wait_ge(par_ready, 2)
            dve.wait_ge(rows_turned, 2)
            dve.wait_ge(sum_dve, 4)
            modulation(1, bank[4], mod_ready, 2)
            dve.wait_ge(mod_ready, 1)
            link(dve.scalar_tensor_tensor(out=scale1, in0=mod[:, 8:16, :], scalar=1.0,
                                          in1=par("norm_mix", 8).unsqueeze(2).broadcast_to([P, 8, 2]),
                                          op0=ALU.add, op1=ALU.mult))
            for g in range(4):
                dve.wait_ge(*g_done(f"xt{2 * g + 1}"))
                for k in (2 * g, 2 * g + 1):
                    for n in range(2):
                        h = HT[:, 512 * k + T * n:512 * k + T * (n + 1)]
                        ins = dve.tensor_scalar(h, h, scale1[:, k, n:n + 1], None, ALU.mult)
                ins.then_inc(h_f32, 1)
            dve.wait_ge(rows_turned, len(ADA_PE))
            dve.wait_ge(sum_dve, 2 * len(ADA_DVE))
            modulation(0, bank[5], mod_ready, 2)
            dve.wait_ge(mod_ready, 2)
            for g in range(4):
                low_parts(HT, 512, lambda k, n: mod[:, k, n:n + 1], 0, g)
                if g == 0:
                    split_lo(dve, 0)
            for g in range(1, RING):
                split_lo(dve, g)
            def ctx_decay(d):
                f, k = ((FFc, KFc), (FBc, KBc))[d]
                dve.wait_ge(g_empty["act"], g_emptied(g_no(("ff1b", "fb1b")[d]))[1])
                link(dve.memset(E[:, :, T - 1:T] if d == 0 else E[:, :, 0:1], 1.0))
                for h in range(HEADS):
                    if d == 0:
                        ins = dve.tensor_tensor_scan(E[:, h, 0:T - 1][:, ::-1], f[:, h, 1:T][:, ::-1],
                                                     ones_t[:, 0:T - 1], 1.0, ALU.mult, ALU.mult)
                    else:
                        ins = dve.tensor_tensor_scan(E[:, h, 1:T], f[:, h, 0:T - 1], ones_t[:, 0:T - 1], 1.0,
                                                     ALU.mult, ALU.mult)
                link(ins)
                dve.tensor_tensor(k[:, :, :], k[:, :, :], E[:, :, :], ALU.mult).then_inc(ctx_k, 1)
                dve.wait_ge(ctx_k, d + 1)

            def values(c, n):
                u = f"v{c}{'ab'[n]}"
                dve.tensor_copy(VTOK[:, 2 * n:2 * n + 2, T * c:T * (c + 1)],
                                g_wait(u)[:, :].rearrange("p (a v) -> p a v", a=2)).then_inc(g_empty["dve"], 1)
            for d, n in enumerate(("ff", "fb")):
                split_lo(dve, G[f"{n}0"] + RING)
                split_lo(dve, G[f"{n}1"] + RING)
                ctx_decay(d)
            dve.tensor_tensor(KSUM, KFx, KBx, ALU.add)
            dve.wait_ge(g_empty["act"], g_emptied(g_no("q0"))[1])
            link(dve.tensor_scalar(Q[:, 0:2, :], Q[:, 0:2, :], P ** -0.5, None, ALU.mult))
            dve.tensor_tensor(QPf[:, 0:2, :], Q[:, 0:2, :], FFx[:, 0:2, :], ALU.mult)
            dve.tensor_tensor(QSb[:, 0:2, :], Q[:, 0:2, :], FBx[:, 0:2, :], ALU.mult)
            split_lo(dve, G["q0"] + RING)
            dve.wait_ge(g_empty["act"], g_emptied(g_no("q1"))[1])
            link(dve.tensor_scalar(Q[:, 2:4, :], Q[:, 2:4, :], P ** -0.5, None, ALU.mult))
            dve.tensor_tensor(QPf[:, 2:4, :], Q[:, 2:4, :], FFx[:, 2:4, :], ALU.mult)
            dve.tensor_tensor(QSb[:, 2:4, :], Q[:, 2:4, :], FBx[:, 2:4, :], ALU.mult).then_inc(lv_upd, 1)
            split_lo(dve, G["q1"] + RING)

            def level(s):
                b = 1 << (s - 1)
                tf, tb = (t.rearrange("p h (n two) -> p (h n) two", two=2) for t in tot[b])

                def half(a, side):
                    return a.rearrange("p h (n two b) -> p (h n) two b", two=2, b=b)[:, :, side, :]

                def wide(t, side):
                    return t[:, :, side:side + 1].broadcast_to([P, HEADS * T // (2 * b), b])
                dve.wait_ge(lv_mm, s + 1)
                dve.wait_ge(lv_upd, s)
                dve.tensor_tensor(half(QPf, 1), half(QPf, 1), wide(tf, 0), ALU.mult)
                ins = dve.tensor_tensor(half(QSb, 0), half(QSb, 0), wide(tb, 1), ALU.mult)
                if s < 8:
                    dve.tensor_tensor(half(KFx, 0), half(KFx, 0), wide(tf, 1), ALU.mult)
                    dve.tensor_tensor(half(KBx, 1), half(KBx, 1), wide(tb, 0), ALU.mult)
                    for t, nxt in ((tf, tot[2 * b][0]), (tb, tot[2 * b][1])):
                        ins = dve.tensor_tensor(nxt.rearrange("p h n -> p (h n)").unsqueeze(2), t[:, :, 0:1],
                                                t[:, :, 1:2], ALU.mult)
                ins.then_inc(lv_upd, 1)
                if s == 8:
                    return
                if s == 1:
                    dve.wait_ge(lv_copied, 1)
                for d in range(2):
                    if d > 0:
                        dve.wait_ge(dve_step, kept[-1])
                    for t in range(2):
                        src = bank[4 + 2 * t + d][:, :].rearrange("p (h t) -> p h t", h=HEADS)
                        m = masks[:, s - 1, d, :].unsqueeze(1).broadcast_to([P, HEADS, P])
                        ins = dve.copy_predicated(S[t], m, src)
                        if d == 0 and t == 1:
                            kept.append(mark(ins))
                ins.then_inc(lv_empty, 1)
                dve.wait_ge(lv_empty, s)

            kept = []
            modulation(2, g_wait("A2"), g_empty["dve"])
            dve.wait_ge(masks_ready, 1)
            values(0, 0)
            level(1)
            values(0, 1)
            split_lo(dve, G["v0"] + RING)
            level(2)
            values(1, 0)
            level(3)
            values(1, 1)
            split_lo(dve, G["v1"] + RING)
            level(4)
            split_lo(dve, G["mv0"] + RING)
            level(5)
            split_lo(dve, G["mv1"] + RING)
            dve.wait_ge(*g_done("mv1"))
            for t in range(2):
                for h in range(HEADS):
                    ins = dve.bn_stats(ln_stats[:, 4 * t + h, :], MV[:, t, P * h:P * (h + 1)])
            link(ins)
            for n in range(8):
                ins = dve.bn_aggr(ln_mv[:, n, :], ln_stats[:, n, :])
            ins.then_inc(sg_stats, 1)
            level(6)
            modulation(3, g_wait("A3"), g_empty["dve"])
            split_lo(dve, G["mu0"] + RING)
            dve.wait_ge(sg_std, 1)
            link(dve.reciprocal(ln_rstd, ln_rstd))
            for t in range(2):
                for h in range(HEADS):
                    n = 4 * t + h
                    ins = dve.tensor_scalar(MV[:, t, P * h:P * (h + 1)], MV[:, t, P * h:P * (h + 1)],
                                            ln_mv[:, n, 0:1], ln_rstd[:, n:n + 1], ALU.subtract, ALU.mult)
            link(ins)
            level(7)
            dve.wait_ge(sgu_loaded, 64)
            link(dve.tensor_tensor(MV, MV, sgu_g.unsqueeze(1).broadcast_to([P, 2, 512]), ALU.mult))
            dve.tensor_tensor(MV, MV, sgu_b.unsqueeze(1).broadcast_to([P, 2, 512]), ALU.add).then_inc(vn_ready, 1)
            split_lo(dve, G["mu1"] + RING)
            level(8)
            for n in range(2):
                dve.wait_ge(m_full, m_no(f"z{n}") + 1)
                z = m_bank(f"z{n}")[:, :].rearrange("p (h t) -> p h t", h=2)
                o = OM[:, 4 + 2 * n:6 + 2 * n, :]
                for h in range(2):
                    bs = bs_row[:, P * (2 * n + h):P * (2 * n + h + 1)].unsqueeze(1).broadcast_to([P, 2, P])
                    ins = dve.tensor_tensor(o[:, h, :].rearrange("p (a t) -> p a t", a=2),
                                            z[:, h, :].rearrange("p (a t) -> p a t", a=2), bs, ALU.add)
                ins.then_inc(m_empty["dve"], 1)
                dve.wait_ge(m_empty["dve"], n + 1)
                dve.wait_ge(*g_done("mu1"))
                dve.tensor_tensor(o, o, U[:, 2 * n:2 * n + 2, :], ALU.mult).then_inc(sgu_out, 1)
            split_lo(dve, G["gt0"] + RING)
            modulation(4, g_wait("A4"), g_empty["dve"])
            split_lo(dve, G["gt1"] + RING)

            def mixed_low(g):
                dve.wait_ge(h_hi, 4 + (3, 4, 1, 2)[g])
                s = slice(2 * T * g, 2 * T * (g + 1))
                dve.tensor_tensor(hlo[:, s], OM.rearrange("p k t -> p (k t)")[:, s], hhi[:, s].bitcast(F32),
                                  ALU.subtract).then_inc(h_lo, 1)
            mixed_low(2)
            mixed_low(3)
            dve.wait_ge(*g_done("gt1"))
            for n in range(2):
                s = slice(2 * n, 2 * n + 2)
                dve.wait_ge(*m_done(f"on{n}"))
                link(dve.reciprocal(hrstd[:, s, :], hstd[:, s, :]))
                link(dve.tensor_tensor(OM[:, s, :], OM[:, s, :], hrstd[:, s, :], ALU.mult))
                for h in (2 * n, 2 * n + 1):
                    ins = dve.scalar_tensor_tensor(out=OM[:, h, :], in0=OM[:, h, :], scalar=par("hg_norm", k=h),
                                                   in1=GT[:, h, :], op0=ALU.mult, op1=ALU.mult)
                ins.then_inc(h_f32, 1)
                if n == 1:
                    mixed_low(0)
            dve.wait_ge(*g_done("A4"))
            link(dve.scalar_tensor_tensor(out=scale2, in0=mod[:, 32:40, 0], scalar=1.0, in1=par("norm_ffn", 8),
                                          op0=ALU.add, op1=ALU.mult))
            mixed_low(1)

            def residual(nb, ps, gate):
                return dve.scalar_tensor_tensor(out=XT[:, nb, 0:T], in0=ps, scalar=mod[:, gate + nb, 0:1],
                                                in1=XT[:, nb, 0:T], op0=ALU.mult, op1=ALU.add)
            for c in range(4):
                ps = g_wait(f"wo{c}")
                for h in range(2):
                    ins = residual(2 * c + h, ps[:, T * h:T * (h + 1)], 16)
                ins.then_inc(g_empty["dve"], 1)
                if c < 3:
                    split_lo(dve, G[f"wo{c}"] + RING)
            normalise(HT[:, 0:KT * T], 8, T, XT[:, :, 0:T], lambda k, n: scale2[:, k:k + 1],
                      lambda k, n: mod[:, 24 + k, 0:1], "sum1")
            split_lo(dve, G["wo3"] + RING)
            dve.tensor_tensor(gain2, par("norm_final", 8), par("g_mix", 8), ALU.mult)
            link(dve.tensor_tensor(nf2, par("norm_final", 8), par("norm_final", 8), ALU.mult))
            dve.tensor_copy(weigh, nf2.unsqueeze(2).broadcast_to([P, KT, P])).then_inc(weigh_ready, 1)
            for j in range(FFT // 2):
                b = j % 2
                dve.wait_ge(g_empty["act"], g_emptied(g_no(f"fg{j}"))[1])
                last = [None, None]
                for tap in range(9):
                    if tap == 4:
                        continue
                    for t in range(2):
                        if last[t]:
                            dve.wait_ge(dve_step, last[t])
                        dy, dx = tap // 3, tap % 3
                        a = acc[:, b, t, :].rearrange("p (r c) -> p r c", r=4)
                        ins = dve.scalar_tensor_tensor(out=a, in0=pad[:, b, t, dy:dy + 4, dx:dx + 64],
                                                       scalar=par("conv_w", k=FFT * tap + 2 * j + t), in1=a,
                                                       op0=ALU.mult, op1=ALU.add)
                        if tap < 8:
                            last[t] = mark(ins)
                    if tap == 3 and G[f"fg{j}"] + RING < N_SPLIT:
                        split_lo(dve, G[f"fg{j}"] + RING)
                ins.then_inc(conv_out, 1)
                if G[f"fa{j}"] + RING < N_SPLIT:
                    split_lo(dve, G[f"fa{j}"] + RING)
                dve.wait_ge(gelu_out, j + 1)
                if j >= 2:
                    dve.wait_ge(u_hi, j - 1)
                ps = g_wait(f"fa{j}")
                dve.tensor_tensor(uf[:, b, :, :], ps[:, :].rearrange("p (j t) -> p j t", j=2), gel[:, b, :, :],
                                  ALU.mult).then_inc(g_empty["dve"], 1)
                if j > 1:
                    split_lo(dve, G[f"fd{j - 2}"] + RING)
                dve.wait_ge(u_hi, j + 1)
                if j >= 3:
                    dve.wait_ge(down_used, j - 2)
                dve.tensor_tensor(ulo[:, j % 3, :, :], uf[:, b, :, :], uhi[:, j % 3, :, :].bitcast(F32), ALU.subtract
                                  ).then_inc(u_lo, 1)
                if j == 7:
                    modulation(5, g_wait("A5"), g_empty["dve"])
            split_lo(dve, G["fd9"] + RING)
            dve.wait_ge(down_used, FFT // 2)
            for c in range(4):
                for h in range(2):
                    ins = residual(2 * c + h, bank[4 + c][:, T * h:T * (h + 1)], 40)
                ins.then_inc(x_new, 1)
            def adv(name):
                if G[name] + RING < N_SPLIT:
                    split_lo(dve, G[name] + RING)

            def l_wait(u):
                dve.wait_ge(l_full, l_no(u) + 1)
                return l_bank(u)

            def two(ps):
                return ps[:, :].rearrange("p (j t) -> p j t", j=2)

            def four(ps):
                return ps[:, :].rearrange("p (j t) -> p j t", j=4)
            dve.wait_ge(m_full, m_no("sum3") + 1)
            dve.tensor_scalar(std[:, 0:T], m_bank("sum2")[:, 0:T], 1.0 / D, EPS, ALU.mult, ALU.add
                              ).then_inc(m_empty["dve"], 1)
            dve.wait_ge(*m_done("sum2"))
            link(dve.reciprocal(rstd[:, 0:T], std[:, 0:T]))
            dve.tensor_tensor(std2, m_bank("sum3")[:, 0:T], rstd[:, 0:T], ALU.mult).then_inc(m_empty["dve"], 1)
            dve.wait_ge(*m_done("sum3"))
            link(dve.tensor_scalar(std2, std2, 1.0 / D, EPS, ALU.mult, ALU.add))
            link(dve.reciprocal(rstd2, std2))
            dve.tensor_tensor(std2, rstd2, rstd[:, 0:T], ALU.mult).then_inc(var_ready, 1)
            dve.wait_ge(rstd_ready, 1)
            for g in range(4):
                scaled(HT2, T, XT[:, :, 0:T], lambda k, n: gain2[:, k:k + 1], g, rstd2)
                if g > 0:
                    low_parts(HT2, T, None, 12, g - 1)
            low_parts(HT2, T, None, 12, 3)
            adv("fd10")
            dve.wait_ge(rstd_ready, 2)
            for g in range(4):
                for k in (2 * g, 2 * g + 1):
                    ins = dve.scalar_tensor_tensor(out=XT[:, k, 0:T], in0=XT[:, k, 0:T], scalar=par("norm_final", k=k),
                                                   in1=std[:, 0:T], op0=ALU.mult, op1=ALU.mult)
                ins.then_inc(x_new, 1)

            def conv_dn(u, dst, tap):
                dve.wait_ge(acc_start, dn_no[u] + 1)
                ps = g_wait(u)
                last = [None, None]
                for d in (1, 2, 3):
                    for t in range(2):
                        if last[t]:
                            dve.wait_ge(dve_step, last[t])
                        ins = dve.scalar_tensor_tensor(
                            out=dst[:, t, d:T], in0=ps[:, T * t:T * (t + 1) - d],
                            scalar=par("dn_conv", k=12 * (3 - d) + tap + t), in1=dst[:, t, d:T], op0=ALU.mult,
                            op1=ALU.add)
                        if d < 3:
                            last[t] = mark(ins)
                ins.then_inc(g_empty["dve"], 1)
                adv(u)
            dn = [(f"d{n}{c}", (QC, KC, VC)["qkv".index(n)][:, 2 * c:2 * c + 2, :], 4 * "qkv".index(n) + 2 * c)
                  for n in "qkv" for c in range(2)]
            dn_no = {d[0]: n for n, d in enumerate(dn)}
            conv_dn(*dn[0])
            dve.wait_ge(m_full, m_no("sm") + 1)
            dve.wait_ge(wsm_zero, 3)
            dve.tensor_scalar(SMY[0:96, :], m_bank("sm")[0:96, 0:T], sm_bias[0:96, :], sm_sign[0:96, :], ALU.add,
                              ALU.mult).then_inc(m_empty["dve"], 1)
            conv_dn(*dn[1])
            dve.wait_ge(sm_ln, 1)
            dve.wait_ge(coef_ready, 1)
            link(dve.scalar_tensor_tensor(out=SMA[0:96, :], in0=SMY[0:96, :], scalar=0.0, in1=SMA[0:96, :],
                                          op0=ALU.max, op1=ALU.add))
            link(dve.tensor_scalar(SMA[0:96, :], SMA[0:96, :], sm_coef[0:96, :], None, ALU.mult))
            link(dve.tensor_tensor_scan(RB[0:8, :], ones_t[0:8, :], SMA[0:8, :], 0.0, ALU.mult, ALU.add))
            dve.tensor_scalar(NCF[0:8, :], RB[0:8, :], -1.0, None, ALU.mult)
            for c in range(2):
                s_ = slice(P * c, P * (c + 1))
                ins = dve.tensor_tensor_scan(RB[64:68, s_], ones_t[64:68, s_], SMA[64:68, s_], 0.0, ALU.mult, ALU.add)
            ins.then_inc(rb_ready, 1)
            conv_dn(*dn[2])
            conv_dn(*dn[3])
            dve.wait_ge(m_full, m_no("colT") + 1)
            dve.tensor_copy(COLS[:, :, :], m_bank("colT")[:, 0:192].rearrange("p (a r) -> p a r", a=2)
                            ).then_inc(m_empty["dve"], 1)
            conv_dn(*dn[4])

            def unit_norm(dst, std_, u, gain, sem_, odd=None):
                dve.wait_ge(*m_done(u))
                link(dve.reciprocal(std_, std_))
                if odd is not None:
                    link(dve.scalar_tensor_tensor(out=odd, in0=dst, scalar=fgain[:, 1:2], in1=std_, op0=ALU.mult,
                                                  op1=ALU.mult))
                dve.scalar_tensor_tensor(out=dst, in0=dst, scalar=gain, in1=std_, op0=ALU.mult, op1=ALU.mult
                                         ).then_inc(sem_, 1)
            dve.wait_ge(silu_done, 2)
            unit_norm(QC, lq_std, "lq1", P ** -0.5, qk_ready)
            conv_dn(*dn[5])
            dve.wait_ge(silu_done, 4)
            unit_norm(KC, lk_std, "lk1", 1.0, qk_ready)
            for u in ("fq0", "fq1", "fk0", "fk1"):
                adv(u)

            def fox_values(c):
                u = f"fv{c}"
                dve.tensor_copy(FV[:, :, T * c:T * (c + 1)], two(g_wait(u))).then_inc(g_empty["dve"], 1)
                adv(u)
            fox_values(0)
            dve.wait_ge(b2_loaded, 80)
            for n in range(2):
                ins = dve.tensor_scalar(fgain[:, n:n + 1], half[:, 127 * n:127 * n + 1], par("fox_gain", k=0),
                                        64 ** -0.5, ALU.mult, ALU.mult)
            link(ins)
            dve.wait_ge(*g_done("fq1"))
            unit_norm(FQ, fq_std, "sfq1", fgain[:, 0:1], f_ready, FQO)
            fox_values(1)
            dve.wait_ge(*g_done("fk1"))
            unit_norm(FK, fk_std, "sfk1", par("fox_gain", k=1), f_ready)
            adv("scc0")
            adv("scc1")

            def fox_max(u, a, heads):
                ps = l_wait(u)
                n = P * (a + 1)
                for m, h in enumerate(heads):
                    ins = dve.tensor_tensor_reduce((SS0, SS1)[a][:, h, :], ps[:, n * m:n * (m + 1)],
                                                   zlate[:, T - n:T], 1.0, -3e38, ALU.add, ALU.max,
                                                   fmax[:, a, h:h + 1])
                ins.then_inc(l_empty["dve"], 1)

            def fox_bias(a):
                cum = COLS[:, a, 0:8]
                link(dve.tensor_tensor(fmax[:, a, :], fmax[:, a, :], cum, ALU.add))
                dve.tensor_tensor(fneg[:, a, :], cum, fmax[:, a, :], ALU.subtract).then_inc(ss_ready, 1)
            dve.wait_ge(b2_loaded, 80)
            fox_max("sa0", 0, range(4))
            fox_max("sa1", 0, range(4, 8))
            dve.wait_ge(*l_done("sa1"))
            fox_bias(0)
            fox_max("sb0", 1, range(0, 2))
            fox_max("sb1", 1, range(2, 4))
            fox_max("sb2", 1, range(4, 6))
            fox_max("sb3", 1, range(6, 8))
            dve.wait_ge(*l_done("sb3"))
            fox_bias(1)

            def fox_prob(a, ss):
                dve.wait_ge(ss_exp, 8 * (a + 1))
                link(dve.reciprocal(frec[:, a, :], fsum[:, a, :]))
                dve.tensor_tensor(ss, ss, frec[:, a, :].unsqueeze(2).broadcast_to([P, 8, P * (a + 1)]), ALU.mult
                                  ).then_inc(p_ready, 1)
            fox_prob(0, SS0)

            def sc_product(c):
                s_ = slice(2 * c, 2 * c + 2)
                dve.wait_ge(*g_done(f"scc{c}"))
                dve.tensor_tensor(CS[:, s_, :], two(g_wait(f"scv{c}")), CS[:, s_, :], ALU.mult
                                  ).then_inc(g_empty["dve"], 1)
                adv(f"scv{c}")
            sc_product(0)
            sc_product(1)
            fox_prob(1, SS1)

            def p_copy(n):
                dst = (None, PT0[:, 4:8, 0:P], None, PT0[:, 4:8, P:T], None, PT1[:, 4:8, :])[n]
                dve.tensor_copy(dst, four(l_wait(f"pt{n}"))).then_inc(l_empty["dve"], 1)
            p_copy(1)
            adv("scb0")
            dve.wait_ge(*g_done("scv1"))
            last = [None] * HEADS
            for d in range(3):
                for t in range(HEADS):
                    w = par("sc_conv", k=4 * (2 - d) + t)
                    if d == 0:
                        last[t] = mark(dve.tensor_scalar(YSC[:, t, :], CS[:, t, :], w, None, ALU.mult))
                    else:
                        dve.wait_ge(dve_step, last[t])
                        last[t] = mark(dve.scalar_tensor_tensor(out=YSC[:, t, d:T], in0=CS[:, t, 0:T - d], scalar=w,
                                                                in1=YSC[:, t, d:T], op0=ALU.mult, op1=ALU.add))
            p_copy(3)
            p_copy(5)
            adv("scb1")
            dve.wait_ge(*g_done("scb1"))
            dve.wait_ge(dve_step, last[3])
            dve.tensor_tensor(YSC, YSC, SCB, ALU.mult).then_inc(y_f32, 1)

            def y_split(n):
                dve.wait_ge(y_hi, (1, 3, 4)[n])
                dve.tensor_tensor(ylo[n], (YSC, None, ODN)[n], yhi[n].bitcast(F32), ALU.subtract).then_inc(y_lo, 1)
            y_split(0)
            for n in range(2):
                s_ = slice(2 * n, 2 * n + 2)
                ps = two(l_wait(f"yf{n}"))
                dve.wait_ge(y_hi, 2 + n)
                dve.tensor_tensor(ylo[1][:, s_, :], ps, yhi[1][:, s_, :].bitcast(F32), ALU.subtract
                                  ).then_inc(l_empty["dve"], 1)
            adv("dz0")
            adv("dz1")
            dve.wait_ge(*l_done("gb1"))
            for n, (d, keep) in enumerate(((DT, keep_up), (DL, keep_low))):
                for c in range(2):
                    for h in range(HEADS):
                        ins = dve.scalar_tensor_tensor(out=d[:, 4 * c + h, :], in0=GBS[:, h, P * c:P * (c + 1)],
                                                       scalar=COLS[:, c, 64 + h:65 + h], in1=keep,
                                                       op0=ALU.subtract, op1=ALU.add)
                ins.then_inc(d_raw, 1)
            for n in range(2):
                s_ = slice(2 * n, 2 * n + 2)
                dve.tensor_tensor(KB[:, s_, :], KC[:, s_, :], two(l_wait(f"bb{n}")), ALU.mult
                                  ).then_inc(l_empty["dve"], 1)
            dve.wait_ge(qd_exp, 1)
            dve.tensor_tensor(QD, QC, QD, ALU.mult)
            eye8 = ident.unsqueeze(1).broadcast_to([P, 8, P])
            dve.tensor_copy(XI, eye8)
            link(dve.tensor_copy(XIT, eye8))
            adv("gs0")
            dve.wait_ge(d_exp, 2)
            for name, dst, d in (("an", AN, DL), ("at", ANT, DT)):
                for c in range(2):
                    s_ = slice(4 * c, 4 * c + 4)
                    dve.scalar_tensor_tensor(out=dst[:, s_, :], in0=four(l_wait(f"{name}{c}")), scalar=-1.0,
                                             in1=d[:, s_, :], op0=ALU.mult, op1=ALU.mult).then_inc(l_empty["dve"], 1)
            adv("gs1")
            dve.wait_ge(*l_done("at1"))
            low, up = (masks[:, 0, n, :].unsqueeze(1).broadcast_to([P, 8, P]) for n in (1, 0))
            dve.copy_predicated(XI, low, AN)
            dve.copy_predicated(XIT, up, ANT).then_inc(x_init, 1)
            for c in range(2):
                s_ = slice(4 * c, 4 * c + 4)
                dve.tensor_tensor(QKT[:, s_, :], four(l_wait(f"qk{c}")), DT[:, s_, :], ALU.mult
                                  ).then_inc(l_empty["dve"], 1)
            for c in range(2):
                dve.tensor_tensor(VB[:, 4 * c:4 * c + 4, :], four(l_wait(f"vt{c}")),
                                  COLS[:, c, 32:36].unsqueeze(2).broadcast_to([P, HEADS, P]), ALU.mult
                                  ).then_inc(l_empty["dve"], 1)
            adv("gs2")
            dve.wait_ge(bg_ready, 1)
            link(dve.tensor_tensor(bgcol, bgcol, COLS[:, 1, 32:36], ALU.mult))
            dve.tensor_tensor(KD, four(l_wait("kt0")), DT[:, 0:4, P - 1:P].broadcast_to([P, HEADS, P]), ALU.mult
                              ).then_inc(l_empty["dve"], 1)
            dve.tensor_tensor(KBG, four(l_wait("kt1")), bgcol.unsqueeze(2).broadcast_to([P, HEADS, P]), ALU.mult
                              ).then_inc(l_empty["dve"], 1)
            adv("gs3")
            gated = slot(17).rearrange("p (b j t) -> p b j t", b=2, j=2)
            n_gated = [0]

            def gated_sum(name, n):
                for u in "ab":
                    k = 4 * int(name[3]) + 2 * "ab".index(u)
                    ps = two(g_wait(name + u))
                    if n == 0:
                        dve.tensor_tensor(XC[:, k:k + 2, :], ps, GATES[:, k:k + 2, :], ALU.mult
                                          ).then_inc(g_empty["dve"], 1)
                        continue
                    b = n_gated[0] % 2
                    n_gated[0] += 1
                    dve.tensor_tensor(gated[:, b], ps, GATES[:, k:k + 2, :], ALU.mult).then_inc(g_empty["dve"], 1)
                    dve.wait_ge(*g_done(name + u))
                    dve.tensor_tensor(XC[:, k:k + 2, :], XC[:, k:k + 2, :], gated[:, b], ALU.add
                                      ).then_inc(merged_f32, 1)
                if name != "brd1":
                    adv(name)
            fill = ["brs0", "brs1", "gf0", "gf1", "gf2", "gf3"]

            def filler(name):
                if name[0] == "g":
                    adv(name)
                    return
                n = "sfd".index(name[2])
                dve.wait_ge(*g_done(f"g{name[2]}3"))
                gated_sum(name, n)
            for lv in range(1, 7):
                for name, dst, side in (("xx", XI, 1), ("xt", XIT, 0)):
                    for c in range(2):
                        m = masks[:, lv, side, :].unsqueeze(1).broadcast_to([P, HEADS, P])
                        dve.copy_predicated(dst[:, 4 * c:4 * c + 4, :], m, four(l_wait(f"{name}{lv}{c}"))
                                            ).then_inc(l_empty["dve"], 1)
                filler(fill[lv - 1])
            dve.wait_ge(m_full, m_no("pT") + 1)
            dve.tensor_copy(PF, m_bank("pT")[:, :]).then_inc(m_empty["dve"], 1)
            filler("brf0")
            dve.wait_ge(*l_done("us1"))
            dve.tensor_tensor(U1[:, 4:8, :], U1[:, 4:8, :], four(l_wait("w1")), ALU.subtract
                              ).then_inc(l_empty["dve"], 1)
            filler("brf1")
            adv("gd0")
            dve.wait_ge(*m_done("on3"))
            link(dve.reciprocal(dstd, dstd))
            link(dve.tensor_tensor(ODN, ODN, dstd, ALU.mult))
            dve.scalar_tensor_tensor(out=ODN, in0=ODN, scalar=par("dn_norm"), in1=ZS, op0=ALU.mult, op1=ALU.mult
                                     ).then_inc(y_f32, 2)
            adv("gd1")
            y_split(2)
            adv("gd2")
            adv("gd3")
            dve.wait_ge(p_hi, 1)
            dve.tensor_tensor(plo, PF.rearrange("p (k t) -> p k t", t=T), phi.bitcast(F32), ALU.subtract
                              ).then_inc(p_lo, 1)
            for name in ("brd0", "brd1"):
                gated_sum(name, 2)
            for g in range(4):
                dve.wait_ge(h_hi, 16 + g + 1)
                dve.wait_ge(merged_f32, 5 + g)
                s_ = slice(512 * g, 512 * (g + 1))
                dve.tensor_tensor(hlo[:, s_].rearrange("p (k t) -> p k t", k=2), XC[:, 2 * g:2 * g + 2, :],
                                  hhi[:, s_].rearrange("p (k t) -> p k t", k=2).bitcast(F32), ALU.subtract
                                  ).then_inc(h_lo, 1)

            adv("brd1")

            def add_x(nb, ps):
                return dve.tensor_tensor(XT[:, nb:nb + 2, 0:T], two(ps), XT[:, nb:nb + 2, 0:T], ALU.add)
            for c in range(4):
                add_x(2 * c, g_wait(f"wp{c}")).then_inc(g_empty["dve"], 1)
                if c < 3:
                    adv(f"wp{c}")
            dve.wait_ge(*g_done("wp3"))
            normalise(HT2, 20, T, XT[:, :, 0:T], lambda k, n: par("g_ffn", k=k), None, "sum4")
            adv("wp3")
            for j in range(FFT // 2):
                b = j % 2
                for n, w in enumerate("ga"):
                    ps = g_wait(f"s{w}{j}")
                    dve.wait_ge(acc2_start, 2 * j + n + 1)
                    last = [None, None]
                    for d in (1, 2):
                        for t in range(2):
                            if last[t]:
                                dve.wait_ge(dve_step, last[t])
                            ins = dve.scalar_tensor_tensor(
                                out=acc2[:, b, n, t, d:T], in0=ps[:, T * t:T * (t + 1) - d],
                                scalar=par("ffn_conv", k=2 * FFT * (2 - d) + FFT * n + 2 * j + t),
                                in1=acc2[:, b, n, t, d:T], op0=ALU.mult, op1=ALU.add)
                            if d == 1:
                                last[t] = mark(ins)
                    ins.then_inc(g_empty["dve"], 1)
                    adv(f"s{w}{j}")
                dve.wait_ge(silu2, j + 1)
                dve.wait_ge(*g_done(f"sa{j}"))
                if j >= 2:
                    dve.wait_ge(u_hi, FFT // 2 + j - 1)
                dve.tensor_tensor(uf[:, b, :, :], acc2[:, b, 0, :, :], acc2[:, b, 1, :, :], ALU.mult
                                  ).then_inc(u2_f32, 1)
                if j > 1:
                    adv(f"sd{j - 2}")
                dve.wait_ge(u_hi, FFT // 2 + j + 1)
                if j >= 3:
                    dve.wait_ge(down_used, FFT // 2 + j - 2)
                dve.tensor_tensor(ulo[:, j % 3, :, :], uf[:, b, :, :], uhi[:, j % 3, :, :].bitcast(F32), ALU.subtract
                                  ).then_inc(u_lo, 1)
            adv(f"sd{FFT // 2 - 2}")
            for c in range(4):
                dve.wait_ge(down_used, FFT)
                add_x(2 * c, bank[4 + c]).then_inc(x_new, 1)
            dve.wait_ge(x_new, 12)
            normalise(HT2, 24, T, XT[:, :, 0:T], lambda k, n: par("g_ple", k=k), None, "sum5")
            adv("sd10")
            adv("ple")
            for c in range(4):
                s_ = slice(2 * c, 2 * c + 2)
                adv(f"pg{c}")
                dve.wait_ge(*g_done(f"pg{c}"))
                link(dve.tensor_tensor(PG[:, s_, :], PG[:, s_, :], PLE[:, s_, :], ALU.mult))
                dve.tensor_tensor(XT[:, s_, 0:T], XT[:, s_, 0:T], PG[:, s_, :], ALU.add).then_inc(x_new, 1)
            for n in range(2):
                dve.wait_ge(l_full, len(l_units) + 2 * n + 2)
                dve.tensor_copy(OUTN[:, n, 512:1024], bank[5 + 2 * n][:, :]).then_inc(out_dve, 1)


_INS = ["x", "ctx", "w_ada", "w_in", "sgu_norm_g", "sgu_norm_b", "w_spatial", "b_spatial", "w_out", "w_up",
        "w_down", "p_2", "w_in_2", "w_branch_2", "w_o_2", "w_up_2", "w_down_2", "w_ple_gate_2", "w_ple_2"]


def kernel(**inputs):
    import numpy as _np
    import concourse.bacc as _bacc
    from concourse import mybir as _mybir
    from concourse.bass_utils import run_bass_kernel_spmd as _run

    nc = _bacc.Bacc("TRN2", target_bir_lowering=False, num_devices=1)
    arrays, args = {}, {}
    laid = dict(zip(("const_f", "const_m", "const_s"), host_constants()), **host_layout({n: _np.asarray(a) for n, a in inputs.items()}))
    for name in _INS + list(laid):
        a = _np.ascontiguousarray(laid[name] if name in laid else inputs[name])
        arrays[f"in_{name}_dram"] = a
        args[name] = nc.dram_tensor(f"in_{name}_dram", a.shape, _mybir.dt.from_np(a.dtype),
                                    kind="ExternalInput").ap()
    out = nc.dram_tensor("out_0_dram", (1, T, D), _mybir.dt.float32, kind="ExternalOutput").ap()
    build(nc, args, out.rearrange("b t d -> (b t) d"))
    r = _run(nc, [arrays], core_ids=[0])
    return r.results[0]["out_0_dram"]
```
